# Optimizing a Trainium2 kernel written in Bass

```python
import jax, jax.numpy as jnp
from jax import lax
import numpy as np

D_MODEL = 1024
BATCH = 1
SEQ = 1024
DEPTH = 1
DEC_BATCH = 1
DEC_SEQ = 64
PAST_LEN = 512

CHUNK = 64
RWKV_HEADS = 8
RWKV_HD = 64
RWKV_W = RWKV_HEADS * RWKV_HD
DECAY_LORA = 64
AAA_LORA = 64
GATE_LORA = 128
RWKV_SIZES = (RWKV_W, RWKV_W, RWKV_W, DECAY_LORA, AAA_LORA, GATE_LORA)
RWKV_COLS = 3 * RWKV_W + DECAY_LORA + AAA_LORA + GATE_LORA
GN_EPS = 64e-5
SWA_HEADS = 8
SWA_KV_HEADS = 2
SWA_GROUP = SWA_HEADS // SWA_KV_HEADS
SWA_HD = 64
WINDOW = 128
BAND_CHUNKS = WINDOW // CHUNK
MEM_TOKENS = 256
MEM_HEADS = 4
MEM_HD = 128
MEM_W = MEM_HEADS * MEM_HD
N_BRANCH = 3
BR_W = 512
IN_SIZES = (RWKV_COLS, SWA_HEADS * SWA_HD, SWA_KV_HEADS * SWA_HD, SWA_KV_HEADS * SWA_HD, MEM_W, N_BRANCH * D_MODEL)
IN_COLS = RWKV_COLS + SWA_HEADS * SWA_HD + 2 * SWA_KV_HEADS * SWA_HD + MEM_W + N_BRANCH * D_MODEL
D_FF = 2816
CONV_W = 3
RMS_EPS = 1e-6

kernel_name = 'hybrid_rwkv7_swa_sink_mem_convffn_step'

def _split_points(sizes):
    pts, acc = [], 0
    for s in sizes[:-1]:
        acc += s
        pts.append(acc)
    return pts

def _rms(x, g):
    xf = x.astype(jnp.float32)
    y = xf * lax.rsqrt(jnp.mean(xf * xf, axis=-1, keepdims=True) + RMS_EPS)
    return (y * g.astype(jnp.float32)).astype(x.dtype)

def _rwkv(p, shift_in, s0, mu, w0, w2, a0, a2, g2, k_k, k_a, r_k, ln_g, ln_b):
    B, T = p.shape[0], p.shape[1]
    p_pad = jnp.concatenate([shift_in.astype(p.dtype), p], axis=1)
    pm = p + (p_pad[:, :-1] - p) * mu
    r, k, v, xw, xa, xg = jnp.split(pm, _split_points(RWKV_SIZES), axis=-1)
    w = -jax.nn.softplus(-(w0 + jnp.tanh(xw) @ w2)) - 0.5
    decay = jnp.exp(-jnp.exp(w.astype(jnp.float32)))
    a = jax.nn.sigmoid(a0 + xa @ a2)
    g = jax.nn.sigmoid(xg) @ g2
    hs = lambda z: z.reshape(B, T, RWKV_HEADS, RWKV_HD).astype(jnp.float32)
    kk = hs(k * k_k)
    kk = kk / jnp.maximum(jnp.sqrt(jnp.sum(kk * kk, axis=-1, keepdims=True)), 1e-12)
    k = k * (1.0 + (a - 1.0) * k_a)
    rh, kh, vh, ah, wh = hs(r), hs(k), hs(v), hs(a), hs(decay)
    tm = lambda z: jnp.moveaxis(z, 1, 0)

    def step(S, inp):
        r_t, w_t, k_t, v_t, kk_t, a_t = inp
        sa = jnp.einsum('bhvk,bhk->bhv', S, -kk_t)
        S = S * w_t[:, :, None, :] + sa[..., None] * (kk_t * a_t)[:, :, None, :] + v_t[..., None] * k_t[:, :, None, :]
        return S, jnp.einsum('bhvk,bhk->bhv', S, r_t)

    s_fin, o = lax.scan(step, s0.astype(jnp.float32), (tm(rh), tm(wh), tm(kh), tm(vh), tm(kk), tm(ah)))
    o = jnp.moveaxis(o, 0, 1)
    mean = jnp.mean(o, axis=-1, keepdims=True)
    var = jnp.mean(jnp.square(o - mean), axis=-1, keepdims=True)
    o = ((o - mean) * lax.rsqrt(var + GN_EPS)).reshape(B, T, RWKV_W) * ln_g.astype(jnp.float32) + ln_b.astype(jnp.float32)
    bonus = jnp.sum(rh * kh * r_k.astype(jnp.float32), axis=-1, keepdims=True) * vh
    o = (o + bonus.reshape(B, T, RWKV_W)) * g.astype(jnp.float32)
    return o.astype(p.dtype), s_fin.astype(s0.dtype), p_pad[:, -1:]

def _attend_sink(q, k, v, dist, valid, sink):
    s = jnp.einsum('bcqhgd,bckhd->bchgqk', q, k).astype(jnp.float32) * (SWA_HD ** -0.5)
    slopes = jnp.exp2(-8.0 * jnp.arange(1, SWA_HEADS + 1, dtype=jnp.float32) / SWA_HEADS)
    s = s - slopes.reshape(SWA_KV_HEADS, SWA_GROUP, 1, 1) * dist
    if valid is not None:
        s = jnp.where(valid[None, :, None, None, None, :], s, -jnp.inf)
    sink_l = jnp.broadcast_to(sink.astype(jnp.float32).reshape(1, 1, SWA_KV_HEADS, SWA_GROUP, 1, 1), s.shape[:-1] + (1,))
    pr = jax.nn.softmax(jnp.concatenate([s, sink_l], axis=-1), axis=-1)[..., :-1]
    return jnp.einsum('bchgqk,bckhd->bcqhgd', pr.astype(v.dtype), v)

def _swa_prompt(q, k, v, sink):
    B, T = q.shape[0], q.shape[1]
    NC = T // CHUNK
    qc = q.reshape(B, NC, CHUNK, SWA_KV_HEADS, SWA_GROUP, SWA_HD)

    def band(z):
        zc = z.reshape(B, NC, CHUNK, SWA_KV_HEADS, SWA_HD)
        zp = jnp.pad(zc, ((0, 0), (BAND_CHUNKS, 0), (0, 0), (0, 0), (0, 0)))
        return jnp.concatenate([zp[:, i:i + NC] for i in range(BAND_CHUNKS + 1)], axis=2)

    KB = (BAND_CHUNKS + 1) * CHUNK
    qi = jnp.arange(CHUNK)
    kj = jnp.arange(KB)
    dist = jnp.abs(BAND_CHUNKS * CHUNK + qi[:, None] - kj[None, :]).astype(jnp.float32)
    valid = (jnp.arange(NC)[:, None] - BAND_CHUNKS + kj[None, :] // CHUNK) >= 0
    o = _attend_sink(qc, band(k), band(v), dist, valid, sink)
    return o.reshape(B, T, SWA_HEADS * SWA_HD)

def _swa_sample(q, k, v, k_cache, v_cache, sink):
    B, T = q.shape[0], q.shape[1]
    L = k_cache.shape[1]
    kf = jnp.concatenate([k_cache.astype(k.dtype), k], axis=1)
    vf = jnp.concatenate([v_cache.astype(v.dtype), v], axis=1)
    dist = jnp.abs(L + jnp.arange(T)[:, None] - jnp.arange(L + T)[None, :]).astype(jnp.float32)
    o = _attend_sink(q.reshape(B, 1, T, SWA_KV_HEADS, SWA_GROUP, SWA_HD), kf[:, None], vf[:, None], dist, None, sink)
    return o.reshape(B, T, SWA_HEADS * SWA_HD), kf[:, -L:], vf[:, -L:]

def _mem_kv(mem, g, w_kv, kn_g):
    B, M = mem.shape[0], mem.shape[1]
    mk, mv = jnp.split(_rms(mem, g) @ w_kv, 2, axis=-1)
    mk = _rms(mk.reshape(B, M, MEM_HEADS, MEM_HD), kn_g)
    return mk, mv.reshape(B, M, MEM_HEADS, MEM_HD)

def _mem_attend(q, mk, mv):
    s = jnp.einsum('bthd,bmhd->bhtm', q, mk.astype(q.dtype)).astype(jnp.float32) * (MEM_HD ** -0.5)
    pr = jax.nn.softmax(s, axis=-1)
    return jnp.einsum('bhtm,bmhd->bthd', pr.astype(q.dtype), mv.astype(q.dtype))

def _layer(x, lw, mem_k, mem_v, shift_in, s0, conv_in, swa_k_cache, swa_v_cache):
    B, T = x.shape[0], x.shape[1]
    h = _rms(x, lw['norm1_g'])
    proj = h @ lw['w_in']
    p_rwkv, q, k, v, qm, gates = jnp.split(proj, _split_points(IN_SIZES), axis=-1)
    o_a, s_new, shift_new = _rwkv(p_rwkv, shift_in, s0, lw['rwkv_mu'], lw['rwkv_w0'], lw['rwkv_w2'], lw['rwkv_a0'],
                                  lw['rwkv_a2'], lw['rwkv_g2'], lw['rwkv_kk'], lw['rwkv_ka'], lw['rwkv_rk'],
                                  lw['rwkv_ln_g'], lw['rwkv_ln_b'])
    q = _rms(q.reshape(B, T, SWA_HEADS, SWA_HD), lw['swa_qn_g'])
    k = _rms(k.reshape(B, T, SWA_KV_HEADS, SWA_HD), lw['swa_kn_g'])
    v = v.reshape(B, T, SWA_KV_HEADS, SWA_HD)
    if swa_k_cache is None:
        o_b = _swa_prompt(q, k, v, lw['swa_sink'])
        kw, vw = k[:, -WINDOW:], v[:, -WINDOW:]
    else:
        o_b, kw, vw = _swa_sample(q, k, v, swa_k_cache, swa_v_cache, lw['swa_sink'])
    qm = _rms(qm.reshape(B, T, MEM_HEADS, MEM_HD), lw['mem_qn_g'])
    o_m = _mem_attend(qm, mem_k, mem_v).reshape(B, T, MEM_W)
    br = jnp.einsum('btnc,ncd->btnd', jnp.stack([o_a, o_b, o_m], axis=2), lw['w_branch'])
    gt = jax.nn.sigmoid(gates.reshape(B, T, N_BRANCH, D_MODEL))
    x = x + jnp.sum(gt * br, axis=2) @ lw['w_out']
    h = _rms(x, lw['norm2_g'])
    a_in, u = jnp.split(h @ lw['w_up'], 2, axis=-1)
    a_pad = jnp.concatenate([conv_in.astype(a_in.dtype), a_in], axis=1)
    c = lw['conv_b'] + sum([a_pad[:, j:j + T] * lw['conv_w'][j] for j in range(CONV_W)])
    x = x + (jax.nn.gelu(c) * u) @ lw['w_down']
    return x, (kw, vw, s_new, shift_new, a_pad[:, -(CONV_W - 1):])

def setup_inputs(seed: int = 0) -> dict:
    key = jax.random.key(seed)
    ks = iter(jax.random.split(key, 48))
    nrm = lambda shape, scale: jax.random.normal(next(ks), shape, jnp.float32) * scale
    L = DEPTH
    swa_len = min(WINDOW, PAST_LEN)
    return {
        'x_prompt': nrm((BATCH, SEQ, D_MODEL), 1.0),
        'x_sample': nrm((DEC_BATCH, DEC_SEQ, D_MODEL), 1.0),
        'cache_swa_k': nrm((L, DEC_BATCH, swa_len, SWA_KV_HEADS, SWA_HD), 1.0),
        'cache_swa_v': nrm((L, DEC_BATCH, swa_len, SWA_KV_HEADS, SWA_HD), 1.0),
        'cache_mem_k': nrm((L, DEC_BATCH, MEM_TOKENS, MEM_HEADS, MEM_HD), 1.0),
        'cache_mem_v': nrm((L, DEC_BATCH, MEM_TOKENS, MEM_HEADS, MEM_HD), 1.0),
        'state_rwkv': nrm((L, DEC_BATCH, RWKV_HEADS, RWKV_HD, RWKV_HD), 0.1),
        'state_shift': nrm((L, DEC_BATCH, 1, RWKV_COLS), 1.0),
        'state_conv': nrm((L, DEC_BATCH, CONV_W - 1, D_FF), 1.0),
        'mem_prompt': nrm((BATCH, MEM_TOKENS, D_MODEL), 1.0),
        'norm1_g': 1.0 + nrm((L, D_MODEL), 0.02),
        'w_in': nrm((L, D_MODEL, IN_COLS), D_MODEL ** -0.5),
        'rwkv_mu': jax.random.uniform(next(ks), (L, RWKV_COLS), jnp.float32),
        'rwkv_w0': jax.random.uniform(next(ks), (L, RWKV_W), jnp.float32, -6.0, -1.0),
        'rwkv_w2': nrm((L, DECAY_LORA, RWKV_W), 0.1 * DECAY_LORA ** -0.5),
        'rwkv_a0': nrm((L, RWKV_W), 0.5),
        'rwkv_a2': nrm((L, AAA_LORA, RWKV_W), 0.5 * AAA_LORA ** -0.5),
        'rwkv_g2': nrm((L, GATE_LORA, RWKV_W), GATE_LORA ** -0.5),
        'rwkv_kk': 0.85 + nrm((L, RWKV_W), 0.02),
        'rwkv_ka': 1.0 + nrm((L, RWKV_W), 0.02),
        'rwkv_rk': nrm((L, RWKV_HEADS, RWKV_HD), 0.1),
        'rwkv_ln_g': 1.0 + nrm((L, RWKV_W), 0.02),
        'rwkv_ln_b': nrm((L, RWKV_W), 0.02),
        'swa_qn_g': 1.0 + nrm((L, SWA_HD), 0.02),
        'swa_kn_g': 1.0 + nrm((L, SWA_HD), 0.02),
        'swa_sink': nrm((L, SWA_HEADS), 0.5),
        'mem_norm_g': 1.0 + nrm((L, D_MODEL), 0.02),
        'w_mem_kv': nrm((L, D_MODEL, 2 * MEM_W), D_MODEL ** -0.5),
        'mem_qn_g': 1.0 + nrm((L, MEM_HD), 0.02),
        'mem_kn_g': 1.0 + nrm((L, MEM_HD), 0.02),
        'w_branch': nrm((L, N_BRANCH, BR_W, D_MODEL), BR_W ** -0.5),
        'w_out': nrm((L, D_MODEL, D_MODEL), D_MODEL ** -0.5),
        'norm2_g': 1.0 + nrm((L, D_MODEL), 0.02),
        'w_up': nrm((L, D_MODEL, 2 * D_FF), D_MODEL ** -0.5),
        'conv_w': nrm((L, CONV_W, D_FF), CONV_W ** -0.5),
        'conv_b': nrm((L, D_FF), 0.02),
        'w_down': nrm((L, D_FF, D_MODEL), D_FF ** -0.5),
    }

def reference(x_prompt, x_sample, cache_swa_k, cache_swa_v, cache_mem_k, cache_mem_v, state_rwkv, state_shift,
              state_conv, mem_prompt, norm1_g, w_in, rwkv_mu, rwkv_w0, rwkv_w2, rwkv_a0, rwkv_a2, rwkv_g2, rwkv_kk,
              rwkv_ka, rwkv_rk, rwkv_ln_g, rwkv_ln_b, swa_qn_g, swa_kn_g, swa_sink, mem_norm_g, w_mem_kv, mem_qn_g,
              mem_kn_g, w_branch, w_out, norm2_g, w_up, conv_w, conv_b, w_down):
    Bp = x_prompt.shape[0]
    dt = x_prompt.dtype
    yp, ys = x_prompt, x_sample
    swk_p, swv_p, mk_p, mv_p, rw_p, sh_p, cv_p = [], [], [], [], [], [], []
    swk_s, swv_s, rw_s, sh_s, cv_s = [], [], [], [], []
    for l in range(DEPTH):
        lw = {'norm1_g': norm1_g[l], 'w_in': w_in[l], 'rwkv_mu': rwkv_mu[l], 'rwkv_w0': rwkv_w0[l],
              'rwkv_w2': rwkv_w2[l], 'rwkv_a0': rwkv_a0[l], 'rwkv_a2': rwkv_a2[l], 'rwkv_g2': rwkv_g2[l],
              'rwkv_kk': rwkv_kk[l], 'rwkv_ka': rwkv_ka[l], 'rwkv_rk': rwkv_rk[l], 'rwkv_ln_g': rwkv_ln_g[l],
              'rwkv_ln_b': rwkv_ln_b[l], 'swa_qn_g': swa_qn_g[l], 'swa_kn_g': swa_kn_g[l], 'swa_sink': swa_sink[l],
              'mem_qn_g': mem_qn_g[l], 'w_branch': w_branch[l], 'w_out': w_out[l], 'norm2_g': norm2_g[l],
              'w_up': w_up[l], 'conv_w': conv_w[l], 'conv_b': conv_b[l], 'w_down': w_down[l]}
        mk, mv = _mem_kv(mem_prompt, mem_norm_g[l], w_mem_kv[l], mem_kn_g[l])
        yp, (kw, vw, s_new, sh_new, cv_new) = _layer(
            yp, lw, mk, mv,
            jnp.zeros((Bp, 1, RWKV_COLS), dt),
            jnp.zeros((Bp, RWKV_HEADS, RWKV_HD, RWKV_HD), dt),
            jnp.zeros((Bp, CONV_W - 1, D_FF), dt), None, None)
        swk_p.append(kw); swv_p.append(vw); mk_p.append(mk); mv_p.append(mv)
        rw_p.append(s_new); sh_p.append(sh_new); cv_p.append(cv_new)
        ys, (kw, vw, s_new, sh_new, cv_new) = _layer(
            ys, lw, cache_mem_k[l], cache_mem_v[l], state_shift[l], state_rwkv[l], state_conv[l],
            cache_swa_k[l], cache_swa_v[l])
        swk_s.append(kw); swv_s.append(vw); rw_s.append(s_new); sh_s.append(sh_new); cv_s.append(cv_new)
    return (yp, ys,
            jnp.stack(swk_p), jnp.stack(swv_p), jnp.stack(mk_p), jnp.stack(mv_p),
            jnp.stack(rw_p), jnp.stack(sh_p), jnp.stack(cv_p),
            jnp.stack(swk_s), jnp.stack(swv_s), jnp.stack(rw_s), jnp.stack(sh_s), jnp.stack(cv_s))


_drawn_inputs = setup_inputs


def setup_inputs(seed=0):
    import zlib

    import numpy as np

    out = dict(_drawn_inputs(seed))
    spreads = {}
    factors = {'rwkv_w2': 8.0,
     'rwkv_ln_g': 8.0,
     'rwkv_ln_b': 8.0,
     'swa_qn_g': 44.571,
     'swa_sink': 56.56,
     'mem_norm_g': 2.783,
     'mem_qn_g': 8.0,
     'mem_kn_g': 2.893,
     'norm2_g': 2.689,
     'conv_b': 5.649}
    for name, (base, spread) in spreads.items():
        noise = np.random.default_rng([zlib.crc32(name.encode()), seed]).standard_normal(out[name].shape)
        drawn = base * np.exp(spread * noise) if base else spread * noise
        out[name] = __import__('jax').numpy.asarray(drawn.astype(out[name].dtype))
    for name, factor in factors.items():
        out[name] = (out[name] * factor).astype(out[name].dtype)
    return out
```

```python
from contextlib import ExitStack

import numpy as np

import concourse.bass as bass
from concourse import mybir

F32 = mybir.dt.float32
F32R = mybir.dt.float32r
ACT = mybir.ActivationFunctionType
ALU = mybir.AluOpType
AX = mybir.AxisListType

P = 128
D = 1024
DT = D // P
SEQ, DEC = 1024, 64
CHUNK = 64
WINDOW = 128
KEYS = WINDOW + CHUNK
FF = 2816
FT = FF // P
MEM = 256
R_TILES = 14
A_TILES = 10
GROUPS = ((0, 576), (576, 512))
PROMPT_END = SEQ - GROUPS[1][0]
RMS_EPS = 1e-6
GN_EPS = 64e-5
DECAY = float(np.exp(-0.5))
LN_SCALE = 2.0 ** 20

VEC = {}
_at = 0
for _name, _n in (("norm1_g", 8), ("norm2_g", 8), ("mem_g", 8), ("mu", 14), ("w0", 4), ("a0", 4), ("kk", 4),
                  ("ka", 4), ("rk", 4), ("ln_g", 4), ("ln_b", 4), ("qn", 1), ("kn", 1), ("mqn", 1), ("mkn", 1),
                  ("sink", 4), ("conv_w", 3 * FT), ("conv_b", FT), ("shift", 14), ("conv_s", 2 * FT),
                  ("log_half_scale", 1)):
    VEC[_name] = (_at, _at + _n)
    _at += _n
N_VEC = _at


def loop(eng, start, end, body):
    body(start, True)
    if end - start > 1:
        with eng.Fori(start + 1, end) as i:
            body(i, False)


def at(tensor, i):
    if isinstance(i, int):
        return tensor[:, i]
    return tensor[:, bass.ds(i, 1)].rearrange("p a t -> p (a t)")


def cols(tensor, tiles, start, n):
    if isinstance(start, int):
        return tensor[:, tiles, start:start + n]
    return tensor[:, tiles, bass.ds(start, n)]


def copy(eng, dst, src):
    return eng.tensor_scalar(dst, src, 1.0, None, ALU.mult)


class Phase:

    def __init__(self, nc, tag):
        self.nc, self.tag, self.stack, self.sems = nc, tag, ExitStack(), []

    def __enter__(self):
        self.stack.__enter__()
        return self

    def __exit__(self, *exc):
        out = self.stack.__exit__(*exc)
        for sem in self.sems:
            self.nc.gpsimd.sem_clear(sem)
        return out

    def sb(self, name, shape, dtype=F32):
        return self.stack.enter_context(self.nc.sbuf_tensor(f"{self.tag}_{name}", shape, dtype))

    def ps(self, name, shape):
        return self.stack.enter_context(self.nc.psum_tensor(f"{self.tag}_{name}", shape, F32))

    def sem(self, name):
        self.sems.append(self.stack.enter_context(self.nc.semaphore(f"{self.tag}_{name}")))
        return self.sems[-1]

    def block(self):
        return self.stack.enter_context(self.nc.Block())


def pieces(T):
    n = -(-T // 512)
    return n, T // n


def two(ap, T):
    return ap.rearrange("p (n t) -> p n t", n=pieces(T)[0])


def vec(c, name, i=0, n=1):
    a = VEC[name][0] + i
    return c.vecs[:, a:a + n]




def norm_phase(nc, c, tag, T, x, gain, hi, lo):
    nb, nt = pieces(T)
    with Phase(nc, tag) as f:
        sq = f.sb("sq", [P, 2, T])
        xs, y, t = f.sb("xs", [P, T]), f.sb("y", [P, T]), f.sb("t", [P, T])
        xn = f.sb("xn", [P, 2, T])
        ps = f.ps("ps", [P, nb, 512])
        squared, sq_used = f.sem("squared"), f.sem("sq_used")
        root, newton = f.sem("root"), f.sem("newton")
        normed, hi_done, lo_done = f.sem("normed"), f.sem("hi_done"), f.sem("lo_done")
        block = f.block()

        @block.scalar
        def _(act):
            for k in range(DT):
                if k >= 2:
                    act.wait_ge(sq_used, k - 1)
                act.activation(sq[:, k % 2], x[:, k], ACT.Square).then_inc(squared, 1)
            act.wait_ge(newton, 1)
            act.activation(t[:, :], xs[:, :], ACT.Ln).then_inc(root, 1)
            act.wait_ge(root, 1)
            act.activation(y[:, :], t[:, :], ACT.Exp, scale=-0.5).then_inc(root, 1)
            for k in range(DT):
                act.wait_ge(normed, k + 1)
                act.activation(hi[:, k], xn[:, k % 2], ACT.Copy).then_inc(hi_done, 1)

        @block.tensor
        def _(pe):
            for k in range(DT):
                pe.wait_ge(squared, k + 1)
                for n in range(nb):
                    mm = pe.matmul(ps[:, n, 0:nt], c.ones[:, :], sq[:, k % 2, n * nt:(n + 1) * nt],
                                   start=(k == 0), stop=(k == DT - 1))
                mm.then_inc(sq_used, 1)

        @block.vector
        def _(dve):
            dve.wait_ge(sq_used, DT)
            dve.tensor_scalar(two(xs[:, :], T), ps[:, :, 0:nt], 1.0 / D, RMS_EPS, ALU.mult, ALU.add).then_inc(newton, 1)
            dve.wait_ge(root, 2)
            dve.wait_ge(newton, 1)
            dve.tensor_tensor(t[:, :], xs[:, :], y[:, :], ALU.mult).then_inc(newton, 1)
            dve.wait_ge(newton, 2)
            dve.scalar_tensor_tensor(t[:, :], t[:, :], -0.5, y[:, :], ALU.mult, ALU.mult).then_inc(newton, 1)
            dve.wait_ge(newton, 3)
            dve.scalar_tensor_tensor(y[:, :], t[:, :], 1.5, y[:, :], ALU.add, ALU.mult).then_inc(newton, 1)
            dve.wait_ge(newton, 4)
            for k in range(DT):
                if k >= 2:
                    dve.wait_ge(lo_done, k - 1)
                dve.scalar_tensor_tensor(xn[:, k % 2], x[:, k], vec(c, gain, k), y[:, :],
                                         ALU.mult, ALU.mult).then_inc(normed, 1)

        @block.gpsimd
        def _(pool):
            for k in range(DT):
                pool.wait_ge(hi_done, k + 1)
                pool.tensor_tensor(lo[:, k], xn[:, k % 2], hi[:, k].bitcast(F32), ALU.subtract).then_inc(lo_done, 1)




def dense_phase(nc, c, tag, T, steps, body, epilogue, before=None, extra=None, after=None):
    nb, nt = pieces(T)
    n_w = len(body)
    n_sum = sum(b[5] for b in body)
    assert n_w % 2 == 0 and n_sum % 2 == 0
    with Phase(nc, tag) as f:
        slot_k = [max(b[1] for b in body[s::2]) for s in range(2)]
        raw = [f.sb(f"raw{s}", [P, slot_k[s] * P]) for s in range(2)]
        w_hi = [f.sb(f"w_hi{s}", [P, slot_k[s] * P], F32R) for s in range(2)]
        w_lo = [f.sb(f"w_lo{s}", [P, slot_k[s] * P], F32R) for s in range(2)]
        sums = f.ps("sums", [P, 2, 2, 512])
        loaded = [f.sem(f"loaded{s}") for s in range(2)]
        hi_done, lo_done, w_used = f.sem("hi_done"), f.sem("lo_done"), f.sem("w_used")
        sum_free = [f.sem(f"sum_free{s}") for s in range(2)]
        work = epilogue(f, sum_free, lambda a: sums[:, a % 2, 0:nb, 0:nt])
        sum_of, last_tile, a = [], [], 0
        for n, b in enumerate(body):
            sum_of.append(a)
            if b[5]:
                last_tile.append(n)
            a += b[5]
        block = f.block()

        def wait_sum(eng, i, a):
            eng.wait_ge(w_used, n_w * i + last_tile[a] + 1)

        @block.sync
        def _(sp):
            if before:
                before(f, sp)

            def step(i, first):
                for b, (w, kt, *_) in enumerate(body):
                    if not (first and b < 2):
                        sp.wait_ge(lo_done, n_w * i + b - 1)
                    index, src = w
                    src = src[index] if first else (
                        src[bass.ds(index + i * w_stride[b], 1)].rearrange("a p m -> p (a m)"))
                    sp.dma_start(raw[b % 2][:, 0:kt * P], src).then_inc(loaded[b % 2], 16)

            w_stride = [sum(1 for o in body if o[0][1] is b[0][1]) for b in body]
            loop(sp, 0, steps, step)
            if after:
                after(f, sp)

        @block.scalar
        def _(act):
            def step(i, first):
                for b, (_, kt, *_) in enumerate(body):
                    act.wait_ge(loaded[b % 2], 16 * ((n_w // 2) * i + b // 2 + 1))
                    if not (first and b < 2):
                        act.wait_ge(w_used, n_w * i + b - 1)
                    act.activation(w_hi[b % 2][:, 0:kt * P], raw[b % 2][:, 0:kt * P], ACT.Copy).then_inc(hi_done, 1)
                    if "act" in work:
                        if b > 0 and body[b - 1][5]:
                            wait_sum(act, i, sum_of[b - 1])
                            work["act"](act, i, sum_of[b - 1])
                        elif b == 0 and not first:
                            wait_sum(act, i - 1, n_sum - 1)
                            work["act"](act, i - 1, n_sum - 1)

            loop(act, 0, steps, step)
            if "act" in work:
                wait_sum(act, steps - 1, n_sum - 1)
                work["act"](act, steps - 1, n_sum - 1)

        @block.gpsimd
        def _(pool):
            def step(i, first):
                for b, (_, kt, *_) in enumerate(body):
                    pool.wait_ge(hi_done, n_w * i + b + 1)
                    pool.tensor_tensor(w_lo[b % 2][:, 0:kt * P], raw[b % 2][:, 0:kt * P],
                                       w_hi[b % 2][:, 0:kt * P].bitcast(F32), ALU.subtract).then_inc(lo_done, 1)

            loop(pool, 0, steps, step)

        @block.tensor
        def _(pe):
            def step(i, first):
                for b, (_, kt, x_hi, x_lo, begins, ends) in enumerate(body):
                    a = sum_of[b]
                    pe.wait_ge(lo_done, n_w * i + b + 1)
                    if begins and not (first and a < 2):
                        pe.wait_ge(sum_free[a % 2], (n_sum // 2) * i + a // 2)
                    for n in range(nb):
                        out = sums[:, a % 2, n, 0:nt]
                        for k in range(kt):
                            wh = w_hi[b % 2][:, k * P:(k + 1) * P]
                            wl = w_lo[b % 2][:, k * P:(k + 1) * P]
                            xh, xl = x_hi[:, k, n * nt:(n + 1) * nt], x_lo[:, k, n * nt:(n + 1) * nt]
                            pe.matmul(out, wh, xh, start=(begins and k == 0), stop=False)
                            pe.matmul(out, wh, xl, start=False, stop=False)
                            mm = pe.matmul(out, wl, xh, start=False, stop=(ends and k == kt - 1))
                    mm.then_inc(w_used, 1)

            loop(pe, 0, steps, step)

        @block.vector
        def _(dve):
            def step(i, first):
                for a in range(n_sum):
                    wait_sum(dve, i, a)
                    work["dve"](dve, i, a, first)

            loop(dve, 0, steps, step)
            if "dve_end" in work:
                work["dve_end"](dve)


def project_phase(nc, c, tag, T, tiles, w, w_at, dst, dst_at):
    def epilogue(f, sum_free, acc):
        def dve(eng, i, a, first):
            copy(eng, two(at(dst, dst_at + 2 * i + a), T), acc(a)).then_inc(sum_free[a], 1)
        return {"dve": dve}

    body = [((w_at + s, w), DT, c.x_hi, c.x_lo, True, True) for s in range(2)]
    dense_phase(nc, c, tag, T, tiles // 2, body, epilogue)


def rsqrt_act(act, c, xs, t, y, root, r0, xs_ready, n0, scaled=False):
    act.wait_ge(xs_ready, n0)
    act.activation(t, xs, ACT.Ln, scale=LN_SCALE if scaled else 1.0).then_inc(root, 1)
    act.wait_ge(root, r0 + 1)
    act.activation(y, t, ACT.Exp, scale=-0.5,
                   **({"bias": vec(c, "log_half_scale")} if scaled else {})).then_inc(root, 1)


def rsqrt_dve(dve, xs, t, y, root, r0, newton, n0):
    dve.wait_ge(root, r0 + 2)
    dve.tensor_tensor(t, xs, y, ALU.mult).then_inc(newton, 1)
    dve.wait_ge(newton, n0 + 1)
    dve.scalar_tensor_tensor(t, t, -0.5, y, ALU.mult, ALU.mult).then_inc(newton, 1)
    dve.wait_ge(newton, n0 + 2)
    dve.scalar_tensor_tensor(y, t, 1.5, y, ALU.add, ALU.mult).then_inc(newton, 1)
    dve.wait_ge(newton, n0 + 3)




def memory_phase(nc, c):
    with Phase(nc, "mem") as g:
        mem = g.sb("mem", [P, DT, MEM])
        m_hi, m_lo = g.sb("m_hi", [P, DT, MEM], F32R), g.sb("m_lo", [P, DT, MEM], F32R)
        mk = g.sb("mk", [P, 4, MEM])
        with Phase(nc, "mem0") as f:
            in_sem = f.sem("in")
            block = f.block()

            @block.sync
            def _(sp):
                sp.dma_start(mem[:, :, :], c.a["memT"]).then_inc(in_sem, 16)
                sp.wait_ge(in_sem, 16)

        norm_phase(nc, c, "mem1", MEM, mem, "mem_g", m_hi, m_lo)

        def epilogue(f, sum_free, acc):
            def dve(eng, i, a, first):
                copy(eng, two(at(mk, 2 * i + a), MEM), acc(a)).then_inc(sum_free[a], 1)
            return {"dve": dve}

        body = [((s, c.a["w_mk"]), DT, m_hi, m_lo, True, True) for s in range(2)]
        dense_phase(nc, c, "mem2", MEM, 2, body, epilogue)

        with Phase(nc, "mem3") as f:
            sq, xs, t, y = (f.sb(n, [P, 4, MEM]) for n in ("sq", "xs", "t", "y"))
            raw = f.sb("raw", [P, DT, 512])
            w_hi, w_lo = f.sb("w_hi", [P, DT, 512], F32R), f.sb("w_lo", [P, DT, 512], F32R)
            mv = f.sb("mv", [P, 2, 512])
            ps, pv = f.ps("ps", [P, 2, 512]), f.ps("pv", [P, 2, 512])
            squared, mean, root, newton = f.sem("squared"), f.sem("mean"), f.sem("root"), f.sem("newton")
            loaded, hi_done, lo_done, mv_sum, mv_out, out = (
                f.sem(n) for n in ("loaded", "hi_done", "lo_done", "mv_sum", "mv_out", "out"))
            block = f.block()

            @block.sync
            def _(sp):
                sp.dma_start(raw[:, :, :], c.a["w_mv"]).then_inc(loaded, 16)
                sp.wait_ge(newton, 5)
                sp.dma_start(c.a["o_mk"], mk[:, :, :]).then_inc(out, 16)
                sp.wait_ge(mv_out, 1)
                sp.dma_start(c.a["o_mv"], mv[:, :, :]).then_inc(out, 16)
                sp.wait_ge(out, 32)

            @block.scalar
            def _(act):
                act.activation(sq[:, :, :], mk[:, :, :], ACT.Square).then_inc(squared, 1)
                act.wait_ge(loaded, 16)
                act.activation(w_hi[:, :, :], raw[:, :, :], ACT.Copy).then_inc(hi_done, 1)
                rsqrt_act(act, c, xs[:, :, :], t[:, :, :], y[:, :, :], root, 0, newton, 1)

            @block.gpsimd
            def _(pool):
                pool.wait_ge(hi_done, 1)
                pool.tensor_tensor(w_lo[:, :, :], raw[:, :, :], w_hi[:, :, :].bitcast(F32),
                                   ALU.subtract).then_inc(lo_done, 1)

            @block.tensor
            def _(pe):
                pe.wait_ge(squared, 1)
                for n in range(2):
                    mm = pe.matmul(ps[:, n, :], c.ones[:, :], sq[:, 2 * n:2 * n + 2, :].rearrange("p a t -> p (a t)"),
                                   start=True, stop=True)
                mm.then_inc(mean, 1)
                pe.wait_ge(lo_done, 1)
                for n in range(2):
                    tok = slice(n * P, (n + 1) * P)
                    for k in range(DT):
                        pe.matmul(pv[:, n, :], m_hi[:, k, tok], w_hi[:, k, :], start=(k == 0), stop=False)
                        pe.matmul(pv[:, n, :], m_hi[:, k, tok], w_lo[:, k, :], start=False, stop=False)
                        mm = pe.matmul(pv[:, n, :], m_lo[:, k, tok], w_hi[:, k, :], start=False, stop=(k == DT - 1))
                mm.then_inc(mv_sum, 1)

            @block.vector
            def _(dve):
                dve.wait_ge(mean, 1)
                dve.tensor_scalar(xs[:, :, :].rearrange("p (n a) t -> p n (a t)", n=2), ps[:, :, :], 1.0 / P, RMS_EPS,
                                  ALU.mult, ALU.add).then_inc(newton, 1)
                rsqrt_dve(dve, xs[:, :, :], t[:, :, :], y[:, :, :], root, 0, newton, 1)
                dve.scalar_tensor_tensor(mk[:, :, :], mk[:, :, :], vec(c, "mkn"), y[:, :, :], ALU.mult,
                                         ALU.mult).then_inc(newton, 1)
                dve.wait_ge(mv_sum, 1)
                dve.tensor_copy(mv[:, :, :], pv[:, :, :]).then_inc(mv_out, 1)




def attention_prep(nc, c, tag, g, T, pa, kw, vw):
    nb, nt = pieces(T)
    normed_tiles = [0, 1, 2, 3, 4, 6, 7, 8, 9]
    n_n = len(normed_tiles)
    prompt = T if g == 0 else PROMPT_END
    with Phase(nc, tag) as f:
        sq = f.sb("sq", [P, 2, T])
        xs, t, y = (f.sb(n, [P, n_n, T]) for n in ("xs", "t", "y"))
        ps = f.ps("ps", [P, 2, 2, 512])
        squared, ss, ss_read = f.sem("squared"), f.sem("ss"), f.sem("ss_read")
        root, newton, done, out, v_done, cache = (
            f.sem(n) for n in ("root", "newton", "done", "out", "v_done", "cache"))
        block = f.block()

        @block.sync
        def _(sp):
            if g == 1:
                w0 = WINDOW + PROMPT_END
                sp.dma_start(kw[:, w0:w0 + WINDOW], c.a["cache_k"]).then_inc(cache, 16)
                sp.dma_start(vw[:, w0:w0 + WINDOW], c.a["cache_v"]).then_inc(cache, 16)
                sp.wait_ge(cache, 32)
                sp.wait_ge(done, n_n)
                sp.wait_ge(v_done, 1)
                for dst, src in (("o_kp", kw[:, PROMPT_END:PROMPT_END + WINDOW]),
                                 ("o_vp", vw[:, PROMPT_END:PROMPT_END + WINDOW]),
                                 ("o_ks", kw[:, w0 + CHUNK:w0 + KEYS]), ("o_vs", vw[:, w0 + CHUNK:w0 + KEYS])):
                    sp.dma_start(c.a[dst], src).then_inc(out, 16)
                sp.wait_ge(out, 64)

        @block.gpsimd
        def _(pool):
            pool.tensor_copy(vw[:, WINDOW:WINDOW + prompt], pa[:, 5, 0:prompt])
            if g == 0:
                pool.memset(kw[:, 0:WINDOW], 0.0)
                pool.memset(vw[:, 0:WINDOW], 0.0).then_inc(v_done, 1)
            else:
                pool.tensor_copy(vw[:, 2 * WINDOW + prompt:2 * WINDOW + T], pa[:, 5, prompt:T])
                pool.tensor_copy(kw[:, 0:WINDOW], c.kv_carry[:, 0])
                pool.tensor_copy(vw[:, 0:WINDOW], c.kv_carry[:, 1]).then_inc(v_done, 1)

        @block.scalar
        def _(act):
            for n, m in enumerate(normed_tiles):
                if n >= 2:
                    act.wait_ge(ss, n - 1)
                act.activation(sq[:, n % 2], pa[:, m], ACT.Square).then_inc(squared, 1)
            rsqrt_act(act, c, xs[:, :, :], t[:, :, :], y[:, :, :], root, 0, ss_read, n_n)

        @block.tensor
        def _(pe):
            for n, m in enumerate(normed_tiles):
                pe.wait_ge(squared, n + 1)
                if n >= 2:
                    pe.wait_ge(ss_read, n - 1)
                for b in range(nb):
                    mm = pe.matmul(ps[:, n % 2, b, 0:nt], (c.ones_head if m < 5 else c.ones)[:, :],
                                   sq[:, n % 2, b * nt:(b + 1) * nt], start=True, stop=True)
                mm.then_inc(ss, 1)

        @block.vector
        def _(dve):
            for n, m in enumerate(normed_tiles):
                dve.wait_ge(ss, n + 1)
                dve.tensor_scalar(two(xs[:, n], T), ps[:, n % 2, 0:nb, 0:nt], 1.0 / (64 if m < 5 else P), RMS_EPS,
                                  ALU.mult, ALU.add).then_inc(ss_read, 1)
            rsqrt_dve(dve, xs[:, :, :], t[:, :, :], y[:, :, :], root, 0, newton, 0)
            for n, m in enumerate(normed_tiles):
                gain = vec(c, "qn" if m < 4 else "kn" if m == 4 else "mqn")
                if m != 4:
                    dve.scalar_tensor_tensor(pa[:, m], pa[:, m], gain, y[:, n], ALU.mult, ALU.mult).then_inc(done, 1)
                    continue
                ins = dve.scalar_tensor_tensor(kw[:, WINDOW:WINDOW + prompt], pa[:, m, 0:prompt], gain,
                                               y[:, n, 0:prompt], ALU.mult, ALU.mult)
                if g == 1:
                    ins = dve.scalar_tensor_tensor(kw[:, 2 * WINDOW + prompt:2 * WINDOW + T], pa[:, m, prompt:T], gain,
                                                   y[:, n, prompt:T], ALU.mult, ALU.mult)
                ins.then_inc(done, 1)
            if g == 0:
                dve.wait_ge(done, n_n)
                dve.wait_ge(v_done, 1)
                dve.tensor_copy(c.kv_carry[:, 0], kw[:, T:T + WINDOW])
                dve.tensor_copy(c.kv_carry[:, 1], vw[:, T:T + WINDOW])


def attention_phase(nc, c, tag, g, T, pa, kw, vw, o):
    n_chunks = T // CHUNK
    with Phase(nc, tag) as f:
        alibi = f.sb("alibi", [P, 3, 4, KEYS])
        mk, mv = f.sb("mk", [P, 2, 4, MEM]), f.sb("mv", [P, 2, 2, 512])
        q, qm = f.sb("q", [P, 4, CHUNK]), f.sb("qm", [P, 4, CHUNK])
        kwin, vwin = f.sb("kwin", [P, KEYS]), f.sb("vwin", [P, KEYS])
        s, p = f.sb("s", [P, 4, KEYS]), f.sb("p", [P, 4, KEYS])
        pm = f.sb("pm", [P, 2, MEM])
        top, neg, srow, total, inv = (f.sb(n, [P, 4]) for n in ("top", "neg", "srow", "total", "inv"))
        esink = f.sb("esink", [P, 4])
        mtop, mneg, mtotal, minv = (f.sb(n, [P, 2]) for n in ("mtop", "mneg", "mtotal", "minv"))
        vt = f.sb("vt", [P, 2, P])
        pt, pt_tail, pmt = f.sb("pt", [P, 4, P]), f.sb("pt_tail", [CHUNK, 4, P]), f.sb("pmt", [P, 4, P])
        ps_s, ps_m = f.ps("ps_s", [P, 2, 512]), f.ps("ps_m", [P, 2, MEM])
        ps_v = f.ps("ps_v", [P, 4, P])
        ps_t, ps_tail, ps_mt = f.ps("ps_t", [P, 4, P]), f.ps("ps_tail", [P, 4, P]), f.ps("ps_mt", [P, 4, P])
        ps_o = f.ps("ps_o", [P, 8, CHUNK])
        names = ("consts staged swa_scores mem_scores v_turned v_read biased topped shifted sink_exp exps summed "
                 "inverse scaled turned pt_read tail_read mem_top mem_neg mem_exps mem_inv mem_scaled mem_turned "
                 "pmt_read pv mem_pv swa_out mem_out").split()
        S = {n: f.sem(n) for n in names}
        block = f.block()

        def plan(c_):
            if g == 1 and c_ == n_chunks - 1:
                return WINDOW + PROMPT_END, 2, 1
            return CHUNK * c_, (c_ if g == 0 and c_ < 2 else 2), 0

        def chunks(eng, body):
            peeled = 2 if g == 0 else 1
            last = n_chunks if g == 0 else n_chunks - 1
            for i in range(peeled):
                body(i, i == 0, *plan(i))
            with eng.Fori(peeled, last) as i:
                body(i, False, i * CHUNK, 2, 0)
            if g == 1:
                body(last, False, *plan(last))

        @block.sync
        def _(sp):
            sp.dma_start(alibi[:, :, :, :], c.a["alibi"]).then_inc(S["consts"], 16)
            sp.dma_start(mk[:, 0], c.a["o_mk"]).then_inc(S["consts"], 16)
            sp.dma_start(mv[:, 0], c.a["o_mv"]).then_inc(S["consts"], 16)
            sp.dma_start(mk[:, 1], c.a["cache_mk"]).then_inc(S["consts"], 16)
            sp.dma_start(mv[:, 1], c.a["cache_mv"]).then_inc(S["consts"], 16)
            sp.wait_ge(S["consts"], 80)

        @block.gpsimd
        def _(pool):
            def chunk(i, first, win, bias, mem):
                if not first:
                    pool.wait_ge(S["swa_scores"], i)
                    pool.wait_ge(S["mem_scores"], i)
                    pool.wait_ge(S["v_turned"], i)
                pool.tensor_copy(q[:, :, :], cols(pa, slice(0, 4), i * CHUNK, CHUNK))
                pool.tensor_copy(kwin[:, :], kw[:, win:win + KEYS] if isinstance(win, int) else kw[:, bass.ds(win, KEYS)])
                pool.tensor_copy(vwin[:, :], vw[:, win:win + KEYS] if isinstance(win, int) else vw[:, bass.ds(win, KEYS)])
                pool.tensor_copy(qm[:, :, :], cols(pa, slice(6, 10), i * CHUNK, CHUNK)).then_inc(S["staged"], 1)

            chunks(pool, chunk)

        @block.tensor
        def _(pe):
            pe.wait_ge(S["consts"], 80)

            def chunk(i, first, win, bias, mem):
                pe.wait_ge(S["staged"], i + 1)
                if not first:
                    pe.wait_ge(S["biased"], i)
                    pe.wait_ge(S["v_read"], i)
                pe.transpose(ps_v[:, 0, :], vwin[:, 0:P], c.ident[:, :])
                pe.matmul(ps_v[0:CHUNK, 1, :], vwin[:, P:KEYS], c.ident[:, :],
                          start=True, stop=True).then_inc(S["v_turned"], 1)
                for j in range(4):
                    for e in range(2):
                        h = slice(64 * e, 64 * e + 64)
                        mm = pe.matmul(ps_s[h, j // 2, (j % 2) * KEYS:(j % 2 + 1) * KEYS], q[h, j, :], kwin[h, :],
                                       start=True, stop=True)
                mm.then_inc(S["swa_scores"], 1)
                if not first:
                    pe.wait_ge(S["mem_exps"], i)
                for h in range(4):
                    mm = pe.matmul(ps_m[64 * (h % 2):64 * (h % 2) + 64, h // 2, :], qm[:, h, :], mk[:, mem, h, :],
                                   start=True, stop=True)
                mm.then_inc(S["mem_scores"], 1)
                pe.wait_ge(S["scaled"], i + 1)
                if not first:
                    pe.wait_ge(S["pt_read"], i)
                    pe.wait_ge(S["tail_read"], i)
                for j in range(4):
                    pe.transpose(ps_t[:, j, :], p[:, j, 0:P], c.ident[:, :])
                for j in range(4):
                    mm = pe.matmul(ps_tail[0:CHUNK, j, :], p[:, j, P:KEYS], c.ident[:, :], start=True, stop=True)
                mm.then_inc(S["turned"], 1)
                pe.wait_ge(S["mem_scaled"], i + 1)
                if not first:
                    pe.wait_ge(S["pmt_read"], i)
                for a in range(4):
                    mm = pe.transpose(ps_mt[:, a, :], pm[:, a // 2, (a % 2) * P:(a % 2 + 1) * P], c.ident[:, :])
                mm.then_inc(S["mem_turned"], 1)
                pe.wait_ge(S["v_read"], i + 1)
                pe.wait_ge(S["pt_read"], i + 1)
                pe.wait_ge(S["tail_read"], i + 1)
                if not first:
                    pe.wait_ge(S["swa_out"], i)
                    pe.wait_ge(S["mem_out"], i)
                for e in range(2):
                    h = slice(64 * e, 64 * e + 64)
                    pe.matmul(ps_o[h, 0:4, :], vt[:, 0, h], pt[:, :, h], start=True, stop=False)
                    mm = pe.matmul(ps_o[h, 0:4, :], vt[0:CHUNK, 1, h], pt_tail[:, :, h], start=False, stop=True)
                mm.then_inc(S["pv"], 1)
                pe.wait_ge(S["pmt_read"], i + 1)
                for h in range(4):
                    q_ = slice(64 * (h % 2), 64 * (h % 2) + 64)
                    for half in range(2):
                        mm = pe.matmul(ps_o[:, 4 + h, :], mv[:, mem, half, h * P:(h + 1) * P],
                                       pmt[:, 2 * (h // 2) + half, q_], start=(half == 0), stop=(half == 1))
                mm.then_inc(S["mem_pv"], 1)

            chunks(pe, chunk)

        @block.vector
        def _(dve):
            dve.wait_ge(S["consts"], 80)

            def chunk(i, first, win, bias, mem):
                dve.wait_ge(S["swa_scores"], i + 1)
                for a in range(2):
                    ins = dve.scalar_tensor_tensor(
                        s[:, 2 * a:2 * a + 2, :], ps_s[:, a, 0:2 * KEYS].rearrange("p (j k) -> p j k", j=2), 0.125,
                        alibi[:, bias, 2 * a:2 * a + 2, :], ALU.mult, ALU.add)
                ins.then_inc(S["biased"], 1)
                dve.wait_ge(S["biased"], i + 1)
                dve.tensor_reduce(top[:, :], s[:, :, :], AX.X, ALU.max).then_inc(S["topped"], 1)
                dve.wait_ge(S["mem_scores"], i + 1)
                dve.tensor_reduce(mtop[:, :], ps_m[:, :, :], AX.X, ALU.max).then_inc(S["mem_top"], 1)
                dve.wait_ge(S["topped"], 3 * i + 1)
                dve.tensor_tensor(top[:, :], top[:, :], vec(c, "sink", 0, 4), ALU.max).then_inc(S["topped"], 1)
                dve.wait_ge(S["mem_top"], i + 1)
                dve.tensor_scalar(mneg[:, :], mtop[:, :], -float(P) ** -0.5, None, ALU.mult).then_inc(S["mem_neg"], 1)
                dve.wait_ge(S["topped"], 3 * i + 2)
                dve.tensor_scalar(neg[:, :], top[:, :], -1.0, None, ALU.mult)
                dve.tensor_tensor(srow[:, :], vec(c, "sink", 0, 4), top[:, :], ALU.subtract).then_inc(S["topped"], 1)
                dve.wait_ge(S["v_turned"], i + 1)
                if not first:
                    dve.wait_ge(S["pv"], i)
                dve.tensor_copy(vt[:, 0, :], ps_v[:, 0, :])
                dve.tensor_copy(vt[0:CHUNK, 1, :], ps_v[0:CHUNK, 1, :]).then_inc(S["v_read"], 1)
                dve.wait_ge(S["exps"], i + 1)
                dve.tensor_tensor(total[:, :], total[:, :], esink[:, :], ALU.add).then_inc(S["summed"], 1)
                dve.wait_ge(S["summed"], i + 1)
                dve.reciprocal(inv[:, :], total[:, :]).then_inc(S["inverse"], 1)
                dve.wait_ge(S["inverse"], i + 1)
                dve.tensor_tensor(p[:, :, :], p[:, :, :], inv[:, :].unsqueeze(2).to_broadcast([P, 4, KEYS]),
                                  ALU.mult).then_inc(S["scaled"], 1)
                dve.wait_ge(S["mem_exps"], i + 1)
                dve.reciprocal(minv[:, :], mtotal[:, :]).then_inc(S["mem_inv"], 1)
                dve.wait_ge(S["mem_inv"], i + 1)
                dve.tensor_tensor(pm[:, :, :], pm[:, :, :], minv[:, :].unsqueeze(2).to_broadcast([P, 2, MEM]),
                                  ALU.mult).then_inc(S["mem_scaled"], 1)
                dve.wait_ge(S["turned"], i + 1)
                if not first:
                    dve.wait_ge(S["pv"], i)
                dve.tensor_copy(pt_tail[:, :, :], ps_tail[0:CHUNK, :, :]).then_inc(S["tail_read"], 1)
                dve.wait_ge(S["mem_pv"], i + 1)
                copy(dve, cols(o, slice(4, 8), i * CHUNK, CHUNK), ps_o[:, 0:4, :]).then_inc(S["swa_out"], 1)
                copy(dve, cols(o, slice(8, 12), i * CHUNK, CHUNK), ps_o[:, 4:8, :]).then_inc(S["mem_out"], 1)

            chunks(dve, chunk)

        @block.scalar
        def _(act):
            def chunk(i, first, win, bias, mem):
                act.wait_ge(S["topped"], 3 * i + 3)
                if not first:
                    act.wait_ge(S["turned"], i)
                for j in range(4):
                    act.activation(p[:, j, :], s[:, j, :], ACT.Exp, bias=neg[:, j:j + 1], accum_out=total[:, j:j + 1])
                act.activation(esink[:, :], srow[:, :], ACT.Exp).then_inc(S["exps"], 1)
                act.wait_ge(S["mem_neg"], i + 1)
                if not first:
                    act.wait_ge(S["mem_turned"], i)
                for a in range(2):
                    ins = act.activation(pm[:, a, :], ps_m[:, a, :], ACT.Exp, bias=mneg[:, a:a + 1],
                                         scale=float(P) ** -0.5, accum_out=mtotal[:, a:a + 1])
                ins.then_inc(S["mem_exps"], 1)
                act.wait_ge(S["turned"], i + 1)
                if not first:
                    act.wait_ge(S["pv"], i)
                act.activation(pt[:, :, :], ps_t[:, :, :], ACT.Copy).then_inc(S["pt_read"], 1)
                act.wait_ge(S["mem_turned"], i + 1)
                if not first:
                    act.wait_ge(S["mem_pv"], i)
                act.activation(pmt[:, :, :], ps_mt[:, :, :], ACT.Copy).then_inc(S["pmt_read"], 1)

            chunks(act, chunk)



RAW, MIX, EXTRA = 0, 14, 28
X_BON, X_CUM, X_KK, X_G = slice(0, 4), slice(4, 8), slice(8, 12), slice(12, 16)
X_WA, X_XG = 14, 15
X_R, X_K, X_V, X_B = slice(16, 20), slice(20, 24), slice(24, 28), slice(28, 32)


def rwkv_prep(nc, c, tag, g, T, ar):
    nb, nt = pieces(T)
    with Phase(nc, tag) as f:
        mask = f.sb("mask", [P, T])
        half = f.sb("half", [P, 8])
        one_ka = f.sb("one_ka", [P, 4])
        t1, t2, t3, sq = (f.sb(n, [P, 4, T]) for n in ("t1", "t2", "t3", "sq"))
        ps = f.ps("ps", [P, 2, 2, 512])
        setup, d_done, mixed, lora_in = f.sem("setup"), f.sem("d_done"), f.sem("mixed"), f.sem("lora_in")
        prod, tan, dstep, root, newton, a_free = (
            f.sem(n) for n in ("prod", "tan", "dstep", "root", "newton", "a_free"))
        out, g_done, sq_done = f.sem("out"), f.sem("g_done"), f.sem("sq_done")
        read = f.sem("read")
        block = f.block()
        pp = lambda n: ps[:, n % 2, 0:nb, 0:nt]
        raw = ar[:, RAW:RAW + 14, :]
        mix = ar[:, MIX:MIX + 14, :]

        @block.sync
        def _(sp):
            if g == 1:
                sp.wait_ge(d_done, 4)
                sp.dma_start(c.a["o_shp"], c.shift_out[:, 0]).then_inc(out, 16)
                sp.dma_start(c.a["o_shs"], c.shift_out[:, 1]).then_inc(out, 16)
                sp.wait_ge(out, 32)

        @block.gpsimd
        def _(pool):
            pool.memset(mask[:, :], 1.0).then_inc(setup, 1)
            pool.wait_ge(setup, 1)
            pool.memset(mask[:, :].rearrange("p (c t) -> p c t", t=CHUNK)[:, :, 0:1], 0.0).then_inc(setup, 1)
            pool.tensor_scalar(half[:, :], vec(c, "w0", 0, 8), 0.5, None, ALU.mult).then_inc(setup, 1)
            pool.tensor_scalar(one_ka[:, :], vec(c, "ka", 0, 4), -1.0, 1.0, ALU.mult, ALU.add).then_inc(setup, 1)

        @block.vector
        def _(dve):
            dve.tensor_tensor(mix[:, :, 1:T], raw[:, :, 0:T - 1], raw[:, :, 1:T], ALU.subtract).then_inc(d_done, 1)
            if g == 0:
                dve.tensor_scalar(mix[:, :, 0:1], raw[:, :, 0:1], -1.0, None, ALU.mult).then_inc(d_done, 1)
                dve.tensor_copy(c.shift_carry[:, :], raw[:, :, T - 1]).then_inc(d_done, 1)
            else:
                dve.wait_ge(d_done, 1)
                dve.tensor_tensor(mix[:, :, 0], c.shift_carry[:, :], raw[:, :, 0], ALU.subtract).then_inc(d_done, 1)
                dve.tensor_tensor(mix[:, :, PROMPT_END], vec(c, "shift", 0, 14), raw[:, :, PROMPT_END],
                                  ALU.subtract).then_inc(d_done, 1)
                dve.tensor_copy(c.shift_out[:, 0], raw[:, :, PROMPT_END - 1])
                dve.tensor_copy(c.shift_out[:, 1], raw[:, :, T - 1]).then_inc(d_done, 1)
            dve.wait_ge(d_done, 3 if g == 0 else 4)
            for m in range(14):
                dve.scalar_tensor_tensor(mix[:, m], mix[:, m], vec(c, "mu", m), raw[:, m], ALU.mult,
                                         ALU.add).then_inc(mixed, 1)
            dve.wait_ge(mixed, 14)
            dve.wait_ge(tan, 2)
            dve.tensor_scalar(ar[:, X_XG], ar[:, X_XG], 0.5, 0.5, ALU.mult, ALU.add).then_inc(lora_in, 1)
            dve.wait_ge(tan, 2 + 4)
            dve.tensor_scalar(t1[:, :, :], t1[:, :, :], -0.5 * DECAY, -0.5 * DECAY, ALU.mult, ALU.add).then_inc(dstep, 1)
            dve.wait_ge(dstep, 1)
            dve.wait_ge(setup, 4)
            for m in range(4):
                dve.tensor_tensor_scan(ar[:, 4 + m], mask[:, :], t1[:, m], 0.0, ALU.mult, ALU.add)
            dve.wait_ge(tan, 2 + 8)
            dve.tensor_scalar(t2[:, :, :], t2[:, :, :], 0.5, 0.5, ALU.mult, ALU.add).then_inc(dstep, 1)
            for m in range(4):
                ins = dve.tensor_scalar(ar[:, 8 + m], ar[:, 20 + m], vec(c, "kk", m), None, ALU.mult)
            ins.then_inc(dstep, 1)
            dve.wait_ge(dstep, 3)
            for m in range(4):
                ins = dve.tensor_scalar(t3[:, m], t2[:, m], vec(c, "ka", m), one_ka[:, m:m + 1], ALU.mult, ALU.add)
            ins.then_inc(dstep, 1)
            dve.wait_ge(dstep, 4)
            dve.tensor_tensor(ar[:, X_K, :], ar[:, X_K, :], t3[:, :, :], ALU.mult).then_inc(dstep, 1)
            dve.wait_ge(dstep, 5)
            for m in range(4):
                ins = dve.scalar_tensor_tensor(t3[:, m], ar[:, 16 + m], vec(c, "rk", m), ar[:, 20 + m],
                                               ALU.mult, ALU.mult)
            ins.then_inc(dstep, 1)
            for m in range(4):
                dve.wait_ge(prod, 12 + m + 1)
                ins = dve.tensor_scalar(two(t1[:, m], T), pp(12 + m), 1e-24, None, ALU.max)
                ins.then_inc(read, 1)
            dve.wait_ge(read, 4)
            rsqrt_dve(dve, t1[:, :, :], sq[:, :, :], ar[:, X_B, :], root, 0, newton, 0)
            dve.tensor_tensor(ar[:, X_KK, :], ar[:, X_KK, :], ar[:, X_B, :], ALU.mult).then_inc(dstep, 1)
            dve.wait_ge(dstep, 7)
            dve.tensor_tensor(ar[:, X_B, :], ar[:, X_KK, :], t2[:, :, :], ALU.mult)
            for m in range(4):
                dve.wait_ge(prod, 16 + m + 1)
                dve.tensor_tensor(two(ar[:, m], T), pp(16 + m), two(ar[:, 24 + m], T), ALU.mult).then_inc(read, 1)

        @block.scalar
        def _(act):
            act.wait_ge(mixed, 1)
            act.activation(ar[0:64, X_WA], ar[0:64, X_WA], ACT.Tanh).then_inc(tan, 1)
            act.wait_ge(mixed, 2)
            act.activation(ar[:, X_XG], ar[:, X_XG], ACT.Tanh, scale=0.5).then_inc(tan, 1)
            act.wait_ge(setup, 4)
            for m in range(8):
                act.wait_ge(prod, m + 1)
                dst = t1 if m < 4 else t2
                act.activation(two(dst[:, m % 4], T), pp(m), ACT.Tanh, bias=half[:, m:m + 1], scale=0.5).then_inc(tan, 1)
            for m in range(4):
                act.wait_ge(prod, 8 + m + 1)
                if m == 3:
                    act.wait_ge(prod, 12)
                act.activation(two(ar[:, 12 + m], T), pp(8 + m), ACT.Copy).then_inc(g_done, 1)
            act.wait_ge(dstep, 3)
            act.activation(sq[:, :, :], ar[:, X_KK, :], ACT.Square).then_inc(sq_done, 1)
            rsqrt_act(act, c, t1[:, :, :], sq[:, :, :], ar[:, X_B, :], root, 0, read, 4, scaled=True)

        @block.tensor
        def _(pe):
            def product(n, lhs, rhs, lo, hi):
                for b in range(nb):
                    mm = pe.matmul(ps[:, n % 2, b, 0:nt], lhs, rhs[lo:hi, b * nt:(b + 1) * nt], start=True, stop=True)
                mm.then_inc(prod, 1)

            pe.wait_ge(tan, 1)
            for m in range(4):
                if m >= 2:
                    pe.wait_ge(tan, 2 + m - 1)
                product(m, c.lora[0:64, 0, m * P:(m + 1) * P], ar[:, X_WA], 0, 64)
            for m in range(4):
                pe.wait_ge(tan, 2 + 4 + m - 1)
                product(4 + m, c.lora[64:128, 0, m * P:(m + 1) * P], ar[:, X_WA], 64, 128)
            pe.wait_ge(lora_in, 1)
            for m in range(4):
                pe.wait_ge(tan, min(10, 2 + 8 + m - 1))
                if m >= 2:
                    pe.wait_ge(g_done, m - 1)
                product(8 + m, c.lora[:, 1, m * P:(m + 1) * P], ar[:, X_XG], 0, 128)
            pe.wait_ge(sq_done, 1)
            for m in range(4):
                if m < 2:
                    pe.wait_ge(g_done, 3 + m)
                else:
                    pe.wait_ge(read, m - 1)
                product(12 + m, c.ones_head[:, :], sq[:, m], 0, 128)
            pe.wait_ge(dstep, 6)
            for m in range(4):
                pe.wait_ge(read, 3 + m)
                product(16 + m, c.ones_head[:, :], t3[:, m], 0, 128)


def rwkv_scan(nc, c, tag, g, T, ar, o):
    n_chunks = T // CHUNK
    C = CHUNK
    with Phase(nc, tag) as f:
        ep, en = f.sb("ep", [P, 4, C + 1]), f.sb("en", [P, 4, C])
        arc, bkc, bkh = f.sb("arc", [P, 4, 2, C]), f.sb("bkc", [P, 4, 2, C]), f.sb("bkh", [P, 4, 2, C])
        vch = f.sb("vch", [P, 4, C])
        mt = f.sb("mt", [P, 2, 4, 2 * C])
        a1, a2, a4 = (f.sb(n, [P, 2, 4, C]) for n in ("a1", "a2", "a4"))
        a8t, off, y1, y2, y4, inv, invt = (f.sb(n, [P, 4, C]) for n in ("a8t", "off", "y1", "y2", "y4", "inv", "invt"))
        nn, n2, f1, gg, tin = f.sb("nn", [P, 2, 4, C]), *(f.sb(n, [P, 4, C]) for n in ("n2", "f1", "gg", "tin"))
        sav = f.sb("sav", [P, 2, 4, C])
        tok = f.sb("tok", [P, 2, 4, C])
        x, s0p = f.sb("x", [P, 4, C]), f.sb("s0p", [P, 4, C])
        ps_g = f.ps("ps_g", [P, 2, 4, 2 * C])
        ps_l = f.ps("ps_l", [P, 2, 4, C])
        ps_1, ps_2 = f.ps("ps_1", [P, 2, 4, C]), f.ps("ps_2", [P, 2, 4, C])
        ps_v, ps_x, ps_s = f.ps("ps_v", [P, 2, 4, C]), f.ps("ps_x", [P, 2, 4, C]), f.ps("ps_s", [P, 2, 4, C])
        names = ("ones decays loaded shifted operands vloaded gram gram_read low low_read y1 pow2 pow2_read pow4 "
                 "pow4_read y2 y2_read pow8 pow8_read y4_read y8 y8_read invt invt_read nblk nblk_read f1 nsq "
                 "nsq_read gsum gsum_read tinv tinv_read vtok vtok_read hat tok tok_read xs xs_read sa sa_read "
                 "osum o_read ssum state s0p swapped").split()
        S = {n: f.sem(n) for n in names}
        block = f.block()
        H = [slice(0, 64), slice(64, 128)]
        eye = c.masks[:, 2, 0:C]
        bc = lambda m: m.unsqueeze(1).to_broadcast([P, 4, m.shape[1]])
        pc = ep[:, :, C:C + 1].to_broadcast([P, 4, C])

        def chunks(eng, body):
            last = n_chunks if g == 0 else n_chunks - 1
            loop(eng, 0, last, body)
            if g == 1:
                if eng is nc.vector:
                    sample_state(eng)
                body(last, False)

        def sample_state(dve):
            dve.wait_ge(S["state"], n_chunks - 1)
            dve.tensor_copy(c.state_out[:, :, :], c.state[:, :, :]).then_inc(S["swapped"], 1)
            dve.wait_ge(S["osum"], n_chunks - 1)
            dve.wait_ge(S["swapped"], 1)
            dve.tensor_copy(c.state[:, :, :], c.state_in[:, :, :]).then_inc(S["swapped"], 1)
            dve.wait_ge(S["swapped"], 2)

        @block.scalar
        def _(act):
            def chunk(i, first):
                t0 = i * C
                if not first:
                    act.wait_ge(S["operands"], 2 * i)
                    act.wait_ge(S["hat"], i)
                    act.wait_ge(S["s0p"], i)
                act.activation(ep[:, :, 1:C + 1], cols(ar, X_CUM, t0, C), ACT.Exp)
                act.activation(en[:, :, :], cols(ar, X_CUM, t0, C), ACT.Exp, scale=-1.0).then_inc(S["decays"], 1)
                act.wait_ge(S["pow2"], i + 1)
                act.activation(a2[:, :, :, :], ps_1[:, :, :, :], ACT.Copy).then_inc(S["pow2_read"], 1)
                act.wait_ge(S["pow4"], i + 1)
                act.activation(a4[:, :, :, :], ps_2[:, :, :, :], ACT.Copy).then_inc(S["pow4_read"], 1)
                act.wait_ge(S["vtok"], i + 1)
                if not first:
                    act.wait_ge(S["ssum"], i)
                for e in range(2):
                    ins = act.activation(sav[H[e], e, :, :], ps_v[H[e], 0, :, :], ACT.Copy)
                ins.then_inc(S["vtok_read"], 1)
                act.wait_ge(S["pow8"], i + 1)
                act.activation(a8t[:, :, :], ps_2[:, 0, :, :], ACT.Copy).then_inc(S["pow8_read"], 1)
                act.wait_ge(S["tok"], i + 1)
                if not first:
                    act.wait_ge(S["ssum"], i)
                for e in range(2):
                    ins = act.activation(tok[:, e, :, :], ps_g[:, e, :, 0:C], ACT.Copy)
                ins.then_inc(S["tok_read"], 1)
                act.wait_ge(S["invt"], i + 1)
                act.activation(invt[:, :, :], ps_1[:, 0, :, :], ACT.Copy).then_inc(S["invt_read"], 1)
                act.wait_ge(S["nblk"], i + 1)
                act.activation(nn[:, :, :, :], ps_2[:, :, :, :], ACT.Copy).then_inc(S["nblk_read"], 1)
                act.wait_ge(S["nsq"], i + 1)
                act.activation(n2[:, :, :], ps_1[:, 0, :, :], ACT.Copy).then_inc(S["nsq_read"], 1)
                act.wait_ge(S["tinv"], i + 1)
                act.activation(tin[:, :, :], ps_1[:, 0, :, :], ACT.Copy).then_inc(S["tinv_read"], 1)
                act.wait_ge(S["osum"], i + 1)
                act.activation(cols(o, slice(0, 4), t0, C), ps_v[:, 1, :, :], ACT.Copy).then_inc(S["o_read"], 1)

            chunks(act, chunk)

        @block.gpsimd
        def _(pool):
            pool.memset(ep[:, :, 0:1], 1.0).then_inc(S["ones"], 1)

            def chunk(i, first):
                if not first:
                    pool.wait_ge(S["vtok"], i)
                pool.tensor_copy(vch[:, :, :], cols(ar, X_V, i * C, C)).then_inc(S["vloaded"], 1)
                pool.wait_ge(S["operands"], 2 * i + 2)
                if not first:
                    pool.wait_ge(S["tok"], i)
                for q in range(2):
                    ins = pool.tensor_tensor(bkh[:, :, q, :], bkc[:, :, q, :], pc, ALU.mult)
                ins.then_inc(S["hat"], 1)

            chunks(pool, chunk)

        @block.vector
        def _(dve):
            dve.wait_ge(S["ones"], 1)

            def chunk(i, first):
                t0 = i * C
                dve.wait_ge(S["decays"], i + 1)
                if not first:
                    dve.wait_ge(S["osum"], i)
                dve.scalar_tensor_tensor(arc[:, :, 0, :], cols(ar, X_KK, t0, C), -1.0, ep[:, :, 0:C], ALU.mult, ALU.mult)
                dve.tensor_tensor(arc[:, :, 1, :], cols(ar, X_R, t0, C), ep[:, :, 1:C + 1],
                                  ALU.mult).then_inc(S["operands"], 1)
                if not first:
                    dve.wait_ge(S["hat"], i)
                for e in range(2):
                    for src, q in ((X_K, e), (X_B, 1 - e)):
                        a_ = ar[H[e], src, t0:t0 + C] if isinstance(t0, int) else ar[H[e], src, bass.ds(t0, C)]
                        ins = dve.tensor_tensor(bkc[H[e], :, q, :], a_, en[H[e], :, :], ALU.mult)
                ins.then_inc(S["operands"], 1)
                dve.wait_ge(S["low"], i + 1)
                dve.tensor_tensor(a1[:, 0, :, :], ps_l[:, 0, :, :], bc(c.masks[:, 0, 0:C]), ALU.mult).then_inc(S["y1"], 1)
                dve.tensor_tensor(a1[:, 1, :, :], ps_l[:, 1, :, :], bc(c.masks[:, 1, 0:C]), ALU.mult)
                dve.tensor_tensor(off[:, :, :], ps_l[:, 0, :, :], bc(c.masks[:, 3, 0:C]), ALU.mult)
                dve.wait_ge(S["y1"], i + 1)
                dve.tensor_tensor(y1[:, :, :], a1[:, 0, :, :], bc(eye), ALU.add).then_inc(S["low_read"], 1)
                dve.wait_ge(S["gram"], i + 1)
                for e in range(2):
                    ins = dve.tensor_tensor(mt[:, e, :, :], ps_g[:, e, :, :], bc(c.masks[:, 4, :]), ALU.mult)
                ins.then_inc(S["gram_read"], 1)
                if not first:
                    dve.wait_ge(S["state"], i)
                dve.tensor_tensor(s0p[:, :, :], c.state[:, :, :], pc, ALU.mult).then_inc(S["s0p"], 1)
                dve.wait_ge(S["y2"], i + 1)
                dve.wait_ge(S["low_read"], i + 1)
                dve.tensor_tensor(y2[:, :, :], ps_l[:, 0, :, :], y1[:, :, :], ALU.add).then_inc(S["y2_read"], 1)
                dve.wait_ge(S["pow8"], i + 1)
                dve.wait_ge(S["y2_read"], i + 1)
                dve.tensor_tensor(y4[:, :, :], ps_l[:, 0, :, :], y2[:, :, :], ALU.add).then_inc(S["y4_read"], 1)
                dve.wait_ge(S["y8"], i + 1)
                dve.wait_ge(S["y4_read"], i + 1)
                dve.tensor_tensor(inv[:, :, :], ps_l[:, 0, :, :], y4[:, :, :], ALU.add).then_inc(S["y8_read"], 1)
                dve.wait_ge(S["nblk_read"], i + 1)
                dve.tensor_tensor(f1[:, :, :], nn[:, 1, :, :], bc(eye), ALU.add).then_inc(S["f1"], 1)
                dve.wait_ge(S["gsum"], i + 1)
                dve.wait_ge(S["f1"], i + 1)
                dve.tensor_tensor(gg[:, :, :], ps_2[:, 0, :, :], f1[:, :, :], ALU.add).then_inc(S["gsum_read"], 1)
                dve.wait_ge(S["xs"], i + 1)
                dve.tensor_copy(x[:, :, :], ps_x[:, 0, :, :]).then_inc(S["xs_read"], 1)
                dve.wait_ge(S["sa"], i + 1)
                for e in range(2):
                    ins = dve.tensor_copy(sav[H[1 - e], e, :, :], ps_x[H[1 - e], 0, :, :])
                ins.then_inc(S["sa_read"], 1)
                dve.wait_ge(S["ssum"], i + 1)
                dve.wait_ge(S["osum"], i + 1)
                dve.wait_ge(S["s0p"], i + 1)
                dve.tensor_tensor(c.state[:, :, :], ps_s[:, 0, :, :], s0p[:, :, :], ALU.add).then_inc(S["state"], 1)

            chunks(dve, chunk)

        @block.tensor
        def _(pe):
            mmul = lambda out, a, b: pe.matmul(out, a, b, start=True, stop=True)
            flat = lambda m: m.rearrange("p a t -> p (a t)")
            ident = lambda e: c.ident[H[e], H[e]].unsqueeze(1).to_broadcast([64, 4, C])

            def each(out, lhs, rhs, cross=False, lead=None):
                for e in (1, 0) if cross else (0, 1):
                    h = H[1 - e] if cross else H[e]
                    for j in range(4):
                        if j == 0 and h is H[0]:
                            wide = flat(lhs(e)[:, 0:2, :]) if lead is None else lead
                            mm = mmul(out[0:wide.shape[1], 0, :], wide, rhs(e)[:, 0, :])
                        else:
                            mm = mmul(out[h, j, :], lhs(e)[:, j, :], rhs(e)[:, j, :])
                return mm

            def each_pair(fn):
                for e in range(2):
                    for j in range(4):
                        mm = fn(j, e, H[e])
                return mm

            def chunk(i, first):
                pe.wait_ge(S["operands"], 2 * i + 2)
                if not first:
                    pe.wait_ge(S["y8_read"], i)
                    pe.wait_ge(S["tok_read"], i)
                each(ps_l[:, 0], lambda e: arc[H[e], :, 0, :], lambda e: bkc[H[e], :, 1 - e, :],
                     lead=flat(arc[H[0], 0]))
                each(ps_l[:, 1], lambda e: bkc[H[e], :, 1 - e, :], lambda e: arc[H[e], :, 0, :],
                     lead=bkc[H[0], 0, 1]).then_inc(S["low"], 1)
                each_pair(lambda j, e, h: mmul(ps_g[:, e, j, :], bkc[h, j, :, :].rearrange("p a t -> p (a t)"),
                                          arc[h, j, :, :].rearrange("p a t -> p (a t)"))).then_inc(S["gram"], 1)
                pe.wait_ge(S["vloaded"], i + 1)
                if not first:
                    pe.wait_ge(S["o_read"], i)
                each(ps_v[:, 0], lambda e: vch[H[e]], ident).then_inc(S["vtok"], 1)
                pe.wait_ge(S["low_read"], i + 1)
                if not first:
                    pe.wait_ge(S["tinv_read"], i)
                each(ps_1[:, 0], lambda e: a1[H[e], 1], lambda e: a1[H[e], 0])
                each(ps_1[:, 1], lambda e: a1[H[e], 0], lambda e: a1[H[e], 1]).then_inc(S["pow2"], 1)
                pe.wait_ge(S["hat"], i + 1)
                pe.wait_ge(S["gram_read"], i + 1)
                each_pair(lambda j, e, h: mmul(ps_g[:, e, j, 0:C], bkh[h, j, :, :].rearrange("p a t -> p (a t)"),
                                          c.ident[h, h])).then_inc(S["tok"], 1)
                pe.wait_ge(S["pow2_read"], i + 1)
                if not first:
                    pe.wait_ge(S["gsum_read"], i)
                each(ps_2[:, 0], lambda e: a2[H[e], 1], lambda e: a2[H[e], 0])
                each(ps_2[:, 1], lambda e: a2[H[e], 0], lambda e: a2[H[e], 1]).then_inc(S["pow4"], 1)
                each(ps_l[:, 0], lambda e: a2[H[e], 1], lambda e: y1[H[e]]).then_inc(S["y2"], 1)
                pe.wait_ge(S["pow4_read"], i + 1)
                pe.wait_ge(S["y2_read"], i + 1)
                each(ps_2[:, 0], lambda e: a4[H[e], 0], lambda e: a4[H[e], 1])
                each(ps_l[:, 0], lambda e: a4[H[e], 1], lambda e: y2[H[e]]).then_inc(S["pow8"], 1)
                pe.wait_ge(S["pow8_read"], i + 1)
                pe.wait_ge(S["y4_read"], i + 1)
                each(ps_l[:, 0], lambda e: a8t[H[e]], lambda e: y4[H[e]]).then_inc(S["y8"], 1)
                pe.wait_ge(S["y8_read"], i + 1)
                each(ps_1[:, 0], lambda e: inv[H[e]], ident).then_inc(S["invt"], 1)
                pe.wait_ge(S["invt_read"], i + 1)
                each(ps_2[:, 0], lambda e: invt[H[e]], lambda e: off[H[e]])
                each(ps_2[:, 1], lambda e: off[H[e]], lambda e: invt[H[e]]).then_inc(S["nblk"], 1)
                pe.wait_ge(S["nblk_read"], i + 1)
                each(ps_1[:, 0], lambda e: nn[H[e], 1], lambda e: nn[H[e], 0]).then_inc(S["nsq"], 1)
                pe.wait_ge(S["nsq_read"], i + 1)
                pe.wait_ge(S["f1"], i + 1)
                each(ps_2[:, 0], lambda e: n2[H[e]], lambda e: f1[H[e]]).then_inc(S["gsum"], 1)
                pe.wait_ge(S["gsum_read"], i + 1)
                each(ps_1[:, 0], lambda e: inv[H[e]], lambda e: gg[H[e]]).then_inc(S["tinv"], 1)
                pe.wait_ge(S["vtok_read"], i + 1)
                if not first:
                    pe.wait_ge(S["state"], i)
                if g == 1 and isinstance(i, int) and i > 0:
                    pe.wait_ge(S["swapped"], 2)
                mmul(ps_x[:, 0, 0, :], flat(arc[H[0], 0]), c.state[H[0], 0, :])
                for e in range(2):
                    h = H[e]
                    for j in range(4):
                        pe.matmul(ps_x[h, 0, j, :], arc[h, j, 0, :], c.state[h, j, :], start=True, stop=False)
                        mm = pe.matmul(ps_x[h, 0, j, :], mt[h, e, j, 0:C], sav[h, e, j, :], start=False, stop=True)
                mm.then_inc(S["xs"], 1)
                pe.wait_ge(S["tinv_read"], i + 1)
                pe.wait_ge(S["xs_read"], i + 1)
                each(ps_x[:, 0], lambda e: tin[H[e]], lambda e: x[H[e]], cross=True).then_inc(S["sa"], 1)
                pe.wait_ge(S["sa_read"], i + 1)
                pe.wait_ge(S["tok_read"], i + 1)
                each_pair(lambda j, e, h: mmul(ps_s[h, 0, j, :], tok[:, e, j, :], sav[:, e, j, :])).then_inc(S["ssum"], 1)
                for e in range(2):
                    for j in range(4):
                        pe.matmul(ps_v[H[e], 1, j, :], c.state[H[e], j, :], arc[H[e], j, 1, :], start=True, stop=False)
                        mm = pe.matmul(ps_v[H[e], 1, j, :], sav[:, e, j, :], mt[:, e, j, C:2 * C], start=False,
                                       stop=True)
                mm.then_inc(S["osum"], 1)

            chunks(pe, chunk)

        @block.sync
        def _(sp):
            if g == 1:
                sp.wait_ge(S["state"], n_chunks)
                sp.dma_start(c.a["o_rp"], c.state_out[:, :, :]).then_inc(S["loaded"], 16)
                sp.dma_start(c.a["o_rs"], c.state[:, :, :]).then_inc(S["loaded"], 16)
                sp.wait_ge(S["loaded"], 32)


def rwkv_post(nc, c, tag, T, ar, o):
    nb, nt = pieces(T)
    with Phase(nc, tag) as f:
        sq, xs, t, y = (f.sb(n, [P, 4, T]) for n in ("sq", "xs", "t", "y"))
        ps = f.ps("ps", [P, 2, 2, 512])
        mean, centred, squared, var, root, newton, done = (
            f.sem(n) for n in ("mean", "centred", "squared", "var", "root", "newton", "done"))
        read = f.sem("read")
        block = f.block()

        @block.tensor
        def _(pe):
            for m in range(4):
                if m >= 2:
                    pe.wait_ge(centred, m - 1)
                for b in range(nb):
                    mm = pe.matmul(ps[:, m % 2, b, 0:nt], c.ones_head[:, :], o[:, m, b * nt:(b + 1) * nt],
                                   start=True, stop=True)
                mm.then_inc(mean, 1)
            for m in range(4):
                pe.wait_ge(squared, m + 1)
                if m >= 2:
                    pe.wait_ge(read, m - 1)
                else:
                    pe.wait_ge(centred, 3 + m)
                for b in range(nb):
                    mm = pe.matmul(ps[:, m % 2, b, 0:nt], c.ones_head[:, :], sq[:, m, b * nt:(b + 1) * nt],
                                   start=True, stop=True)
                mm.then_inc(var, 1)

        @block.scalar
        def _(act):
            for m in range(4):
                act.wait_ge(centred, m + 1)
                act.activation(sq[:, m], o[:, m], ACT.Square).then_inc(squared, 1)
            rsqrt_act(act, c, xs[:, :, :], t[:, :, :], y[:, :, :], root, 0, read, 4)

        @block.vector
        def _(dve):
            for m in range(4):
                dve.wait_ge(mean, m + 1)
                dve.scalar_tensor_tensor(two(o[:, m], T), ps[:, m % 2, 0:nb, 0:nt], -1.0 / 64, two(o[:, m], T),
                                         ALU.mult, ALU.add).then_inc(centred, 1)
            for m in range(4):
                dve.wait_ge(var, m + 1)
                dve.tensor_scalar(two(xs[:, m], T), ps[:, m % 2, 0:nb, 0:nt], 1.0 / 64, GN_EPS, ALU.mult,
                                  ALU.add).then_inc(read, 1)
            dve.wait_ge(read, 4)
            rsqrt_dve(dve, xs[:, :, :], t[:, :, :], y[:, :, :], root, 0, newton, 0)
            for m in range(4):
                dve.scalar_tensor_tensor(o[:, m], o[:, m], vec(c, "ln_g", m), y[:, m], ALU.mult,
                                         ALU.mult).then_inc(done, 1)
            for m in range(4):
                dve.wait_ge(done, m + 1)
                dve.scalar_tensor_tensor(o[:, m], o[:, m], vec(c, "ln_b", m), ar[:, m], ALU.add,
                                         ALU.add).then_inc(done, 1)
            dve.wait_ge(done, 8)
            dve.tensor_tensor(o[:, 0:4, :], o[:, 0:4, :], ar[:, X_G, :], ALU.mult)




def split_phase(nc, c, tag, src, hi, lo, tiles):
    with Phase(nc, tag) as f:
        hi_done, lo_done = f.sem("hi_done"), f.sem("lo_done")
        block = f.block()

        @block.scalar
        def _(act):
            for k in range(tiles):
                act.activation(hi[:, k], src[:, k], ACT.Copy).then_inc(hi_done, 1)

        @block.vector
        def _(dve):
            for k in range(0, tiles, 2):
                dve.wait_ge(hi_done, k + 1)
                dve.tensor_tensor(lo[:, k], src[:, k], hi[:, k].bitcast(F32), ALU.subtract)

        @block.gpsimd
        def _(pool):
            for k in range(1, tiles, 2):
                pool.wait_ge(hi_done, k + 1)
                pool.tensor_tensor(lo[:, k], src[:, k], hi[:, k].bitcast(F32), ALU.subtract)


def merge_phase(nc, c, tag, T, o_hi, o_lo, merged):
    def epilogue(f, sum_free, acc):
        th, pr = f.sb("th", [P, 2, T]), f.sb("pr", [P, T])
        tan, added = f.sem("tan"), f.sem("added")

        def act(eng, i, a):
            if a % 2:
                return
            n = 3 * i + a // 2
            eng.activation(two(th[:, 0], T), acc(a), ACT.Tanh, scale=0.5).then_inc(tan, 1)
            eng.wait_ge(tan, n + 1)
            if not (isinstance(n, int) and n == 0):
                eng.wait_ge(sum_free[1], n)
            eng.activation(th[:, 1], th[:, 0], ACT.Copy, scale=0.5, bias=0.5).then_inc(sum_free[0], 1)

        def dve(eng, i, a, first):
            if a % 2 == 0:
                return
            n = 3 * i + a // 2
            eng.wait_ge(sum_free[0], n + 1)
            dst = at(merged, i)
            out = dst if a == 1 else pr[:, :]
            if a == 3 and not first:
                eng.wait_ge(added, 2 * i)
            if a == 5:
                eng.wait_ge(added, 2 * i + 1)
            eng.tensor_tensor(two(out, T), acc(a), two(th[:, 1], T), ALU.mult).then_inc(sum_free[1], 1)
            if a > 1:
                eng.wait_ge(sum_free[1], n + 1)
                eng.tensor_tensor(dst, dst, pr[:, :], ALU.add).then_inc(added, 1)
        return {"act": act, "dve": dve}

    body = []
    for n in range(3):
        body.append(((n, c.a["w_gate"]), DT, c.x_hi, c.x_lo, True, True))
        body.append(((n, c.a["w_branch"]), 4, o_hi[:, 4 * n:4 * n + 4, :], o_lo[:, 4 * n:4 * n + 4, :], True, True))
    dense_phase(nc, c, tag, T, DT, body, epilogue)


def add_phase(nc, c, tag, T, steps, body, base, dst, after=None):
    def epilogue(f, sum_free, acc):
        def dve(eng, i, a, first):
            m = 2 * i + a
            ins = eng.tensor_tensor(two(at(dst, m), T), acc(a), two(at(base, m), T), ALU.add)
            ins.then_inc(sum_free[a], 1)
        return {"dve": dve}

    dense_phase(nc, c, tag, T, steps, body, epilogue, after=after)


def up_phase(nc, c, tag, g, T, h_hi, h_lo):
    def epilogue(f, sum_free, acc):
        a_raw, cv, gl = f.sb("a_raw", [P, T + 2]), f.sb("cv", [P, T]), f.sb("gl", [P, T])
        h = f.sb("h", [P, T])
        a_in, conv, gelu, hi_done, lo_done = (f.sem(n) for n in ("a_in", "conv", "gelu", "h_hi_done", "h_lo_done"))
        h_done = sum_free[1]
        ws = f.sb("ws", [P, 4])
        if g == 1:
            fix = f.sb("fix", [P, 4])
        per = 4 if g == 0 else 7
        cw, cb, cs = VEC["conv_w"][0], VEC["conv_b"][0], VEC["conv_s"][0]

        def col(tensor, i, n=1):
            return tensor[:, i:i + n] if isinstance(i, int) else tensor[:, bass.ds(i, n)]

        def act(eng, i, a):
            if a == 0:
                eng.wait_ge(conv, per * i + per)
                if not (isinstance(i, int) and i == 0):
                    eng.wait_ge(h_done, i)
                eng.activation(gl[:, :], cv[:, :], ACT.Gelu_apprx_tanh).then_inc(gelu, 1)
            else:
                eng.wait_ge(h_done, i + 1)
                eng.activation(at(h_hi, i), h[:, :], ACT.Copy).then_inc(hi_done, 1)

        def dve(eng, i, a, first):
            if a == 0:
                copy(eng, a_raw[:, 0:2], col(c.conv_carry, 2 * i, 2)).then_inc(a_in, 1)
                eng.tensor_copy(two(a_raw[:, 2:T + 2], T), acc(0)).then_inc(sum_free[0], 1)
                eng.tensor_copy(ws[:, 0:3], col(c.vecs, cw + 3 * i, 3))
                eng.tensor_copy(ws[:, 3:4], col(c.vecs, cb + i)).then_inc(a_in, 1)
                eng.wait_ge(sum_free[0], i + 1)
                eng.wait_ge(a_in, 2 * i + 2)
                if not first:
                    eng.wait_ge(gelu, i)
                eng.tensor_scalar(cv[:, :], a_raw[:, 2:T + 2], ws[:, 2:3], ws[:, 3:4], ALU.mult,
                                  ALU.add).then_inc(conv, 1)
                eng.wait_ge(conv, per * i + 1)
                eng.scalar_tensor_tensor(cv[:, :], a_raw[:, 1:T + 1], ws[:, 1:2], cv[:, :], ALU.mult,
                                         ALU.add).then_inc(conv, 1)
                eng.wait_ge(conv, per * i + 2)
                eng.scalar_tensor_tensor(cv[:, :], a_raw[:, 0:T], ws[:, 0:1], cv[:, :], ALU.mult,
                                         ALU.add).then_inc(conv, 1)
                eng.wait_ge(conv, per * i + 3)
                if g == 0:
                    copy(eng, col(c.conv_carry, 2 * i, 2), a_raw[:, T:T + 2]).then_inc(conv, 1)
                    return
                e0 = PROMPT_END
                copy(eng, fix[:, 0:2], col(c.vecs, cs + 2 * i, 2))
                eng.tensor_copy(fix[:, 2:4], a_raw[:, 2 + e0:4 + e0])
                copy(eng, col(c.conv_carry, 2 * i, 2), a_raw[:, e0:e0 + 2])
                eng.tensor_copy(col(c.conv_last, 2 * i, 2), a_raw[:, T:T + 2]).then_inc(conv, 1)
                eng.wait_ge(conv, per * i + 4)
                eng.tensor_scalar(cv[:, e0:e0 + 2], fix[:, 2:4], ws[:, 2:3], ws[:, 3:4], ALU.mult,
                                  ALU.add).then_inc(conv, 1)
                eng.wait_ge(conv, per * i + 5)
                eng.scalar_tensor_tensor(cv[:, e0:e0 + 2], fix[:, 1:3], ws[:, 1:2], cv[:, e0:e0 + 2], ALU.mult,
                                         ALU.add).then_inc(conv, 1)
                eng.wait_ge(conv, per * i + 6)
                eng.scalar_tensor_tensor(cv[:, e0:e0 + 2], fix[:, 0:2], ws[:, 0:1], cv[:, e0:e0 + 2], ALU.mult,
                                         ALU.add).then_inc(conv, 1)
            else:
                eng.wait_ge(gelu, i + 1)
                if not first:
                    eng.wait_ge(lo_done, i)
                eng.tensor_tensor(two(h[:, :], T), acc(1), two(gl[:, :], T), ALU.mult).then_inc(h_done, 1)
                eng.wait_ge(hi_done, i + 1)
                eng.tensor_tensor(at(h_lo, i), h[:, :], at(h_hi, i).bitcast(F32), ALU.subtract).then_inc(lo_done, 1)
        return {"act": act, "dve": dve}

    body = [((s, c.a["w_up"]), DT, c.x_hi, c.x_lo, True, True) for s in range(2)]
    dense_phase(nc, c, tag, T, FT, body, epilogue)




class Consts:
    pass


def build(nc, a):
    c = Consts()
    c.a = a
    with Phase(nc, "k") as k:
        c.vecs = k.sb("vecs", [P, N_VEC])
        c.ident, c.ones, c.ones_head = k.sb("ident", [P, P]), k.sb("ones", [P, P]), k.sb("ones_head", [P, P])
        c.lora = k.sb("lora", [P, 2, 512])
        c.masks = k.sb("masks", [P, 5, P])
        c.state, c.state_in, c.state_out = (k.sb(n, [P, 4, CHUNK]) for n in ("state", "state_in", "state_out"))
        c.kv_carry = k.sb("kv_carry", [P, 2, WINDOW])
        c.shift_carry, c.shift_out = k.sb("shift_carry", [P, 14]), k.sb("shift_out", [P, 2, 14])
        c.conv_carry, c.conv_last = k.sb("conv_carry", [P, 2 * FT]), k.sb("conv_last", [P, 2 * FT])

        with Phase(nc, "start") as f:
            in_sem, zero = f.sem("in"), f.sem("zero")
            block = f.block()

            @block.sync
            def _(sp):
                for n, (dst, src) in enumerate((
                        (c.vecs[:, :], a["vecs"]), (c.ident[:, :], a["ident"]), (c.ones[:, :], a["ones"]),
                        (c.ones_head[:, :], a["ones_head"]), (c.lora[:, :, :], a["lora"]),
                        (c.masks[:, :, :], a["masks"]), (c.state_in[:, :, :], a["state"]))):
                    sp.dma_start(dst, src).then_inc(in_sem, 16)
                sp.wait_ge(in_sem, 16 * 7)

            @block.vector
            def _(dve):
                dve.memset(c.state[:, :, :], 0.0)
                dve.memset(c.conv_carry[:, :], 0.0)

        memory_phase(nc, c)
        for g, (start, T) in enumerate(GROUPS):
            group(nc, c, g, start, T)

        with Phase(nc, "end") as f:
            out = f.sem("out")
            block = f.block()

            @block.sync
            def _(sp):
                sp.dma_start(a["o_cp"], c.conv_carry[:, :]).then_inc(out, 16)
                sp.dma_start(a["o_cs"], c.conv_last[:, :]).then_inc(out, 16)
                sp.wait_ge(out, 32)


def load(nc, tag, dst, src):
    with Phase(nc, tag) as f:
        in_sem = f.sem("in")
        block = f.block()

        @block.sync
        def _(sp):
            sp.dma_start(dst, src).then_inc(in_sem, 16)
            sp.wait_ge(in_sem, 16)


def group(nc, c, g, start, T):
    a, t = c.a, f"g{g}"
    x_src = a["xT"][:, :, start:start + T]
    with Phase(nc, t) as k:
        c.x_hi, c.x_lo = k.sb("x_hi", [P, DT, T], F32R), k.sb("x_lo", [P, DT, T], F32R)
        with Phase(nc, t + "o") as ko:
            o = ko.sb("o", [P, 12, T])
            with Phase(nc, t + "x") as kx:
                x = kx.sb("x", [P, DT, T])
                load(nc, t + "ld", x[:, :, :], x_src)
                norm_phase(nc, c, t + "n1", T, x, "norm1_g", c.x_hi, c.x_lo)
            with Phase(nc, t + "a") as ka:
                pa = ka.sb("pa", [P, A_TILES, T])
                width = WINDOW + T if g == 0 else 2 * WINDOW + T
                kw, vw = ka.sb("kw", [P, width]), ka.sb("vw", [P, width])
                project_phase(nc, c, t + "pa", T, A_TILES, a["w_attn"], 0, pa, 0)
                attention_prep(nc, c, t + "ap", g, T, pa, kw, vw)
                attention_phase(nc, c, t + "at", g, T, pa, kw, vw, o)
            with Phase(nc, t + "r") as kr:
                ar = kr.sb("ar", [P, 32, T])
                project_phase(nc, c, t + "pr", T, R_TILES, a["w_rwkv"], 0, ar, 0)
                rwkv_prep(nc, c, t + "rp", g, T, ar)
                rwkv_scan(nc, c, t + "rs", g, T, ar, o)
                rwkv_post(nc, c, t + "rq", T, ar, o)
            with Phase(nc, t + "m") as km:
                merged = km.sb("merged", [P, DT, T])
                with Phase(nc, t + "s") as ks:
                    o_hi, o_lo = ks.sb("o_hi", [P, 12, T], F32R), ks.sb("o_lo", [P, 12, T], F32R)
                    split_phase(nc, c, t + "so", o, o_hi, o_lo, 12)
                    merge_phase(nc, c, t + "mg", T, o_hi, o_lo, merged)
                split_phase(nc, c, t + "sm", merged, c.x_hi, c.x_lo, DT)
        with Phase(nc, t + "y") as ky:
            x1 = ky.sb("x1", [P, DT, T])
            load(nc, t + "l2", x1[:, :, :], x_src)
            body = [((s, a["w_out"]), DT, c.x_hi, c.x_lo, True, True) for s in range(2)]
            add_phase(nc, c, t + "wo", T, DT // 2, body, x1, x1)
            norm_phase(nc, c, t + "n2", T, x1, "norm2_g", c.x_hi, c.x_lo)
            h_hi, h_lo = ky.sb("h_hi", [P, FT, T], F32R), ky.sb("h_lo", [P, FT, T], F32R)
            up_phase(nc, c, t + "up", g, T, h_hi, h_lo)
            half = FT // 2
            body = []
            for s in range(4):
                k0 = (s % 2) * half
                body.append(((s, a["w_down"]), half, h_hi[:, k0:k0 + half, :], h_lo[:, k0:k0 + half, :],
                             s % 2 == 0, s % 2 == 1))

            add_phase(nc, c, t + "wd", T, DT // 2, body, x1, x1)
            store(nc, t + "st", a["o_y"][:, :, start:start + T], x1[:, :, :])


def store(nc, tag, dst, src):
    with Phase(nc, tag) as f:
        out = f.sem("out")
        block = f.block()

        @block.sync
        def _(sp):
            sp.dma_start(dst, src).then_inc(out, 16)
            sp.wait_ge(out, 16)




def tiles(w):
    k, m = w.shape
    return np.ascontiguousarray(w.reshape(k // P, P, m // P, P).transpose(2, 1, 0, 3).reshape(m // P, P, k))


def columns(v):
    return v.reshape(-1, P).T


def constants():
    i = np.arange(P)
    ident = np.eye(P, dtype=np.float32)
    head = (i[:, None] // 64 == i[None, :] // 64).astype(np.float32)
    r, q = i % 64, np.arange(P)
    masks = np.zeros((P, 5, P), np.float32)
    same = r[:, None] // 16 == q[None, :] // 16
    masks[:, 0] = same & (r[:, None] > q[None, :])
    masks[:, 1] = same & (r[:, None] < q[None, :])
    masks[:, 2] = r[:, None] == q[None, :]
    masks[:, 3] = (r[:, None] // 16 > q[None, :] // 16)
    masks[:, 4, 0:64] = r[:, None] < q[None, 0:64]
    masks[:, 4, 64:128] = r[:, None] <= q[None, 0:64]
    slopes = np.exp2(-8.0 * np.arange(1, 9, dtype=np.float32) / 8).astype(np.float32)
    dist = np.abs(WINDOW + np.arange(64)[:, None] - np.arange(KEYS)[None, :]).astype(np.float32)
    alibi = np.zeros((P, 3, 4, KEYS), np.float32)
    for v in range(3):
        for j in range(4):
            for e in range(2):
                t = -slopes[j + 4 * e] * dist
                t = np.where(np.arange(KEYS)[None, :] < WINDOW - CHUNK * v, np.float32(-1e30), t)
                alibi[64 * e:64 * e + 64, v, j] = t
    return {"ident": ident, "ones": np.ones((P, P), np.float32), "ones_head": head, "masks": masks, "alibi": alibi}


def lay_out(x):
    f32 = np.float32
    w_in = np.asarray(x["w_in"][0])
    rw = w_in[:, 0:1792]
    order = [slice(1536, 1664), slice(1664, 1792), slice(0, 512), slice(512, 1024), slice(1024, 1536)]
    reorder = lambda v: np.concatenate([v[..., s] for s in order], -1)
    heads = [h for j in range(4) for h in (j, j + 4)]
    q = w_in[:, 1792:2304].reshape(D, 8, 64)[:, heads].reshape(D, 512)
    attn = np.concatenate([q, w_in[:, 2304:3072]], 1)
    gates = w_in[:, 3072:].reshape(D, 3, DT, P).transpose(0, 2, 1, 3).reshape(D, 3 * D)
    branch = np.asarray(x["w_branch"][0]).copy()
    branch[1] = branch[1].reshape(8, 64, D)[heads].reshape(512, D)
    branch = np.stack([tiles(b) for b in branch], 1).reshape(3 * DT, P, 512)
    up = np.asarray(x["w_up"][0]).reshape(D, 2, FT, P).transpose(0, 2, 1, 3).reshape(D, 2 * FF)
    down = tiles(np.asarray(x["w_down"][0])).reshape(DT, P, 2, FF // 2).transpose(0, 2, 1, 3).reshape(2 * DT, P, FF // 2)
    mem_kv = np.asarray(x["w_mem_kv"][0])
    both = lambda v: np.tile(v, 2)[:, None]
    sink = np.asarray(x["swa_sink"][0])
    sinks = np.concatenate([np.tile(sink[4 * e:4 * e + 4][None], (64, 1)) for e in range(2)], 0)
    conv_w = np.asarray(x["conv_w"][0]).reshape(3, FT, P).transpose(2, 1, 0).reshape(P, 3 * FT)
    conv_s = np.asarray(x["state_conv"][0, 0]).reshape(2, FT, P).transpose(2, 1, 0).reshape(P, 2 * FT)
    one = lambda n: columns(np.asarray(x[n][0]).reshape(-1))
    vecs = np.concatenate([
        one("norm1_g"), one("norm2_g"), one("mem_norm_g"), columns(reorder(np.asarray(x["rwkv_mu"][0]))),
        one("rwkv_w0"), one("rwkv_a0"), one("rwkv_kk"), one("rwkv_ka"), one("rwkv_rk"), one("rwkv_ln_g"),
        one("rwkv_ln_b"), both(np.asarray(x["swa_qn_g"][0])), both(np.asarray(x["swa_kn_g"][0])),
        one("mem_qn_g"), one("mem_kn_g"), sinks, conv_w, one("conv_b"),
        columns(reorder(np.asarray(x["state_shift"][0, 0, 0]))), conv_s,
        np.full((P, 1), 0.5 * np.log(LN_SCALE), f32)], 1)
    assert vecs.shape == (P, N_VEC)
    fm = lambda v: v.reshape(-1, DT, P).transpose(2, 1, 0)
    tokens = np.concatenate([np.asarray(x["x_prompt"][0]), np.asarray(x["x_sample"][0])], 0)
    lora = np.stack([np.concatenate([np.asarray(x["rwkv_w2"][0]), np.asarray(x["rwkv_a2"][0])], 0),
                     np.asarray(x["rwkv_g2"][0])], 1)
    out = {
        "xT": fm(tokens), "memT": fm(np.asarray(x["mem_prompt"][0])), "vecs": vecs, "lora": lora,
        "w_attn": tiles(attn), "w_rwkv": tiles(reorder(rw)), "w_gate": tiles(gates), "w_branch": branch,
        "w_out": tiles(np.asarray(x["w_out"][0])), "w_up": tiles(up), "w_down": down,
        "w_mk": tiles(mem_kv[:, 0:512]), "w_mv": mem_kv[:, 512:].reshape(DT, P, 512).transpose(1, 0, 2),
        "cache_k": np.asarray(x["cache_swa_k"][0, 0]).reshape(WINDOW, P).T,
        "cache_v": np.asarray(x["cache_swa_v"][0, 0]).reshape(WINDOW, P).T,
        "cache_mk": np.asarray(x["cache_mem_k"][0, 0]).transpose(2, 1, 0),
        "cache_mv": np.asarray(x["cache_mem_v"][0, 0]).reshape(2, P, 512).transpose(1, 0, 2),
        "state": np.asarray(x["state_rwkv"][0, 0]).reshape(4, 2, 64, 64).transpose(1, 3, 0, 2).reshape(P, 4, 64),
    }
    out.update(constants())
    return {n: np.ascontiguousarray(v) for n, v in out.items()}


OUTS = {
    "o_y": (P, DT, SEQ + DEC), "o_mk": (P, 4, MEM), "o_mv": (P, 2, 512), "o_kp": (P, WINDOW), "o_vp": (P, WINDOW),
    "o_ks": (P, WINDOW), "o_vs": (P, WINDOW), "o_rp": (P, 4, 64), "o_rs": (P, 4, 64), "o_shp": (P, 14),
    "o_shs": (P, 14), "o_cp": (P, 2 * FT), "o_cs": (P, 2 * FT),
}


def kernel(**inputs):
    import concourse.bacc as _bacc
    from concourse.bass_utils import run_bass_kernel_spmd as _run

    nc = _bacc.Bacc("TRN2", target_bir_lowering=False, num_devices=1)
    arrays = lay_out(inputs)
    a = {n: nc.dram_tensor(n, v.shape, mybir.dt.from_np(v.dtype), kind="ExternalInput").ap() for n, v in arrays.items()}
    for n, s in OUTS.items():
        a[n] = nc.dram_tensor(n, s, F32, kind="ExternalOutput").ap()
    build(nc, a)
    r = _run(nc, [arrays], core_ids=[0]).results[0]

    y = r["o_y"].transpose(2, 1, 0).reshape(SEQ + DEC, D)
    kv = lambda v: np.ascontiguousarray(v.T).reshape(1, 1, WINDOW, 2, 64)
    state = lambda v: v.reshape(2, 64, 4, 64).transpose(2, 0, 3, 1).reshape(1, 1, 8, 64, 64)

    def shift(v):
        flat = v.T.reshape(1792)
        return np.concatenate([flat[256:], flat[0:256]]).reshape(1, 1, 1, 1792)

    conv = lambda v: v.reshape(P, FT, 2).transpose(2, 1, 0).reshape(1, 1, 2, FF)
    return (y[None, 0:SEQ], y[None, SEQ:],
            kv(r["o_kp"]), kv(r["o_vp"]),
            r["o_mk"].transpose(2, 1, 0).reshape(1, 1, MEM, 4, P),
            r["o_mv"].transpose(1, 0, 2).reshape(1, 1, MEM, 4, P),
            state(r["o_rp"]), shift(r["o_shp"]), conv(r["o_cp"]),
            kv(r["o_ks"]), kv(r["o_vs"]), state(r["o_rs"]), shift(r["o_shs"]), conv(r["o_cs"]))
```

```python
from contextlib import ExitStack

import numpy as np

import concourse.bass as bass
from concourse import mybir

F32 = mybir.dt.float32
F32R = mybir.dt.float32r
ACT = mybir.ActivationFunctionType
ALU = mybir.AluOpType
AX = mybir.AxisListType

P = 128
D = 1024
DT = D // P
SEQ, DEC = 1024, 64
CHUNK = 64
WINDOW = 128
KEYS = WINDOW + CHUNK
FF = 2816
FT = FF // P
MEM = 256
R_TILES = 14
A_TILES = 10
GROUPS = ((0, 576), (576, 512))
PROMPT_END = SEQ - GROUPS[1][0]
RMS_EPS = 1e-6
GN_EPS = 64e-5
DECAY = float(np.exp(-0.5))
LN_SCALE = 2.0 ** 20

VEC = {}
_at = 0
for _name, _n in (("norm1_g", 8), ("norm2_g", 8), ("mem_g", 8), ("mu", 14), ("w0", 4), ("a0", 4), ("kk", 4),
                  ("ka", 4), ("rk", 4), ("ln_g", 4), ("ln_b", 4), ("qn", 1), ("kn", 1), ("mqn", 1), ("mkn", 1),
                  ("sink", 4), ("conv_w", 3 * FT), ("conv_b", FT), ("shift", 14), ("conv_s", 2 * FT),
                  ("log_half_scale", 1)):
    VEC[_name] = (_at, _at + _n)
    _at += _n
N_VEC = _at


def loop(eng, start, end, body):
    body(start, True)
    if end - start > 1:
        with eng.Fori(start + 1, end) as i:
            body(i, False)


def at(tensor, i):
    if isinstance(i, int):
        return tensor[:, i]
    return tensor[:, bass.ds(i, 1)].rearrange("p a t -> p (a t)")


def cols(tensor, tiles, start, n):
    if isinstance(start, int):
        return tensor[:, tiles, start:start + n]
    return tensor[:, tiles, bass.ds(start, n)]


def copy(eng, dst, src):
    return eng.tensor_scalar(dst, src, 1.0, None, ALU.mult)


class Phase:

    def __init__(self, nc, tag):
        self.nc, self.tag, self.stack, self.sems = nc, tag, ExitStack(), []

    def __enter__(self):
        self.stack.__enter__()
        return self

    def __exit__(self, *exc):
        out = self.stack.__exit__(*exc)
        for sem in self.sems:
            self.nc.gpsimd.sem_clear(sem)
        return out

    def sb(self, name, shape, dtype=F32):
        return self.stack.enter_context(self.nc.sbuf_tensor(f"{self.tag}_{name}", shape, dtype))

    def ps(self, name, shape):
        return self.stack.enter_context(self.nc.psum_tensor(f"{self.tag}_{name}", shape, F32))

    def sem(self, name):
        self.sems.append(self.stack.enter_context(self.nc.semaphore(f"{self.tag}_{name}")))
        return self.sems[-1]

    def block(self):
        return self.stack.enter_context(self.nc.Block())


def pieces(T):
    n = -(-T // 512)
    return n, T // n


def two(ap, T):
    return ap.rearrange("p (n t) -> p n t", n=pieces(T)[0])


def vec(c, name, i=0, n=1):
    a = VEC[name][0] + i
    return c.vecs[:, a:a + n]




def norm_phase(nc, c, tag, T, x, gain, hi, lo):
    nb, nt = pieces(T)
    with Phase(nc, tag) as f:
        sq, total = f.sb("sq", [P, DT, T]), f.sb("total", [P, T])
        xs, y, t = f.sb("xs", [P, T]), f.sb("y", [P, T]), f.sb("t", [P, T])
        xn = f.sb("xn", [P, 3, T])
        ps = f.ps("ps", [P, nb, 512])
        squared, added, mean = f.sem("squared"), f.sem("added"), f.sem("mean")
        root, newton = f.sem("root"), f.sem("newton")
        normed, hi_done, lo_done = f.sem("normed"), f.sem("hi_done"), f.sem("lo_done")
        block = f.block()

        @block.scalar
        def _(act):
            for k in range(DT):
                act.activation(sq[:, k], x[:, k], ACT.Square).then_inc(squared, 1)
            act.wait_ge(newton, 1)
            act.activation(t[:, :], xs[:, :], ACT.Ln).then_inc(root, 1)
            act.wait_ge(root, 1)
            act.activation(y[:, :], t[:, :], ACT.Exp, scale=-0.5).then_inc(root, 1)
            for k in range(DT):
                act.wait_ge(normed, k + 1)
                act.activation(hi[:, k], xn[:, k % 3], ACT.Copy).then_inc(hi_done, 1)

        @block.tensor
        def _(pe):
            pe.wait_ge(added, DT - 1)
            for n in range(nb):
                mm = pe.matmul(ps[:, n, 0:nt], c.ones[:, :], total[:, n * nt:(n + 1) * nt], start=True, stop=True)
            mm.then_inc(mean, 1)

        @block.vector
        def _(dve):
            dve.wait_ge(squared, 2)
            dve.tensor_tensor(total[:, :], sq[:, 0], sq[:, 1], ALU.add).then_inc(added, 1)
            for k in range(2, DT - 1):
                dve.wait_ge(squared, k + 1)
                dve.wait_ge(added, k - 1)
                dve.tensor_tensor(total[:, :], total[:, :], sq[:, k], ALU.add).then_inc(added, 1)
            dve.wait_ge(added, DT - 2)
            dve.wait_ge(squared, DT)
            dve.tensor_tensor(total[:, :], total[:, :], sq[:, DT - 1], ALU.add).then_inc(added, 1)
            dve.wait_ge(mean, 1)
            dve.tensor_scalar(two(xs[:, :], T), ps[:, :, 0:nt], 1.0 / D, RMS_EPS, ALU.mult, ALU.add).then_inc(newton, 1)
            dve.wait_ge(root, 2)
            dve.wait_ge(newton, 1)
            dve.tensor_tensor(t[:, :], xs[:, :], y[:, :], ALU.mult).then_inc(newton, 1)
            dve.wait_ge(newton, 2)
            dve.scalar_tensor_tensor(t[:, :], t[:, :], -0.5, y[:, :], ALU.mult, ALU.mult).then_inc(newton, 1)
            dve.wait_ge(newton, 3)
            dve.scalar_tensor_tensor(y[:, :], t[:, :], 1.5, y[:, :], ALU.add, ALU.mult).then_inc(newton, 1)
            dve.wait_ge(newton, 4)
            for k in range(DT):
                if k >= 3:
                    dve.wait_ge(lo_done, k - 2)
                dve.scalar_tensor_tensor(xn[:, k % 3], x[:, k], vec(c, gain, k), y[:, :],
                                         ALU.mult, ALU.mult).then_inc(normed, 1)

        @block.gpsimd
        def _(pool):
            for k in range(DT):
                pool.wait_ge(hi_done, k + 1)
                pool.tensor_tensor(lo[:, k], xn[:, k % 3], hi[:, k].bitcast(F32), ALU.subtract).then_inc(lo_done, 1)




def dense_phase(nc, c, tag, T, steps, body, epilogue, slots=2, act_lag=1, store=None):
    nb, nt = pieces(T)
    n_w = len(body)
    n_sum = sum(b[5] for b in body)
    assert n_w % slots == 0 and n_sum % 2 == 0 and act_lag <= n_w
    with Phase(nc, tag) as f:
        slot_k = [max(b[1] for b in body[s::slots]) for s in range(slots)]
        raw = [f.sb(f"raw{s}", [P, k * P]) for s, k in enumerate(slot_k)]
        w_hi = [f.sb(f"w_hi{s}", [P, k * P], F32R) for s, k in enumerate(slot_k)]
        w_lo = [f.sb(f"w_lo{s}", [P, k * P], F32R) for s, k in enumerate(slot_k)]
        sums = f.ps("sums", [P, 2, 2, 512])
        loaded = [f.sem(f"loaded{s}") for s in range(slots)]
        stored = f.sem("stored")
        hi_done, lo_done, w_used = f.sem("hi_done"), f.sem("lo_done"), f.sem("w_used")
        sum_free = [f.sem(f"sum_free{s}") for s in range(2)]
        work = epilogue(f, sum_free, lambda a: sums[:, a % 2, 0:nb, 0:nt])
        sum_of, last_tile, a = [], [], 0
        for n, b in enumerate(body):
            sum_of.append(a)
            if b[5]:
                last_tile.append(n)
            a += b[5]
        block = f.block()

        def wait_sum(eng, i, a):
            eng.wait_ge(w_used, n_w * i + last_tile[a] + 1)

        @block.sync
        def _(sp):
            stride = [sum(1 for o in body if o[0][1] is b[0][1]) for b in body]

            def results(i):
                for h in range(2):
                    sp.wait_ge(sum_free[h], (n_sum // 2) * (i + 1))
                store(sp, i).then_inc(stored, 16)

            def step(i, first):
                for b, ((index, w), kt, *_) in enumerate(body):
                    if not (first and b < slots):
                        sp.wait_ge(lo_done, n_w * i + b - slots + 1)
                    src = w[index] if first else w[bass.ds(index + i * stride[b], 1)].rearrange("a p m -> p (a m)")
                    sp.dma_start(raw[b % slots][:, 0:kt * P], src).then_inc(loaded[b % slots], 16)
                    if first and b == slots - 1 and "load" in work:
                        work["load"](sp)
                if store and not first:
                    results(i - 1)

            loop(sp, 0, steps, step)
            if store:
                results(steps - 1)
                sp.wait_ge(stored, 16 * steps)

        @block.scalar
        def _(act):
            ended = []
            for b in range(n_w):
                t = (b - act_lag) % n_w
                ended.append((sum_of[t], b < act_lag) if body[t][5] else None)

            def rest(i, b):
                a, last_step = ended[b]
                j = i - 1 if last_step else i
                wait_sum(act, j, a)
                work["act"](act, j, a)

            def step(i, first):
                for b, (_, kt, *_) in enumerate(body):
                    act.wait_ge(loaded[b % slots], 16 * ((n_w // slots) * i + b // slots + 1))
                    if not (first and b < slots):
                        act.wait_ge(w_used, n_w * i + b - slots + 1)
                    act.activation(w_hi[b % slots][:, 0:kt * P], raw[b % slots][:, 0:kt * P],
                                   ACT.Copy).then_inc(hi_done, 1)
                    if "act" in work and ended[b] and not (first and ended[b][1]):
                        rest(i, b)

            loop(act, 0, steps, step)
            if "act" in work:
                for b in range(n_w):
                    if ended[b] and ended[b][1]:
                        rest(steps, b)

        @block.gpsimd
        def _(pool):
            def step(i, first):
                for b, (_, kt, *_) in enumerate(body):
                    pool.wait_ge(hi_done, n_w * i + b + 1)
                    pool.tensor_tensor(w_lo[b % slots][:, 0:kt * P], raw[b % slots][:, 0:kt * P],
                                       w_hi[b % slots][:, 0:kt * P].bitcast(F32), ALU.subtract).then_inc(lo_done, 1)

            loop(pool, 0, steps, step)

        @block.tensor
        def _(pe):
            def step(i, first):
                for b, (_, kt, x_hi, x_lo, begins, ends) in enumerate(body):
                    a = sum_of[b]
                    pe.wait_ge(lo_done, n_w * i + b + 1)
                    if begins and not (first and a < 2):
                        pe.wait_ge(sum_free[a % 2], (n_sum // 2) * i + a // 2)
                    for n in range(nb):
                        out = sums[:, a % 2, n, 0:nt]
                        for k in range(kt):
                            wh = w_hi[b % slots][:, k * P:(k + 1) * P]
                            wl = w_lo[b % slots][:, k * P:(k + 1) * P]
                            xh, xl = x_hi[:, k, n * nt:(n + 1) * nt], x_lo[:, k, n * nt:(n + 1) * nt]
                            pe.matmul(out, wh, xh, start=(begins and k == 0), stop=False)
                            pe.matmul(out, wh, xl, start=False, stop=False)
                            mm = pe.matmul(out, wl, xh, start=False, stop=(ends and k == kt - 1))
                    mm.then_inc(w_used, 1)

            loop(pe, 0, steps, step)

        @block.vector
        def _(dve):
            def step(i, first):
                for a in range(n_sum):
                    wait_sum(dve, i, a)
                    work["dve"](dve, i, a, first)

            loop(dve, 0, steps, step)
            if "dve_end" in work:
                work["dve_end"](dve)


def project_phase(nc, c, tag, T, tiles, w, w_at, dst, dst_at):
    def epilogue(f, sum_free, acc):
        def dve(eng, i, a, first):
            copy(eng, two(at(dst, dst_at + 2 * i + a), T), acc(a)).then_inc(sum_free[a], 1)
        return {"dve": dve}

    body = [((w_at + s, w), DT, c.x_hi, c.x_lo, True, True) for s in range(2)]
    dense_phase(nc, c, tag, T, tiles // 2, body, epilogue)


def rsqrt_act(act, c, xs, t, y, root, r0, xs_ready, n0, scaled=False):
    act.wait_ge(xs_ready, n0)
    act.activation(t, xs, ACT.Ln, scale=LN_SCALE if scaled else 1.0).then_inc(root, 1)
    act.wait_ge(root, r0 + 1)
    act.activation(y, t, ACT.Exp, scale=-0.5,
                   **({"bias": vec(c, "log_half_scale")} if scaled else {})).then_inc(root, 1)


def rsqrt_dve(dve, xs, t, y, root, r0, newton, n0):
    dve.wait_ge(root, r0 + 2)
    dve.tensor_tensor(t, xs, y, ALU.mult).then_inc(newton, 1)
    dve.wait_ge(newton, n0 + 1)
    dve.scalar_tensor_tensor(t, t, -0.5, y, ALU.mult, ALU.mult).then_inc(newton, 1)
    dve.wait_ge(newton, n0 + 2)
    dve.scalar_tensor_tensor(y, t, 1.5, y, ALU.add, ALU.mult).then_inc(newton, 1)
    dve.wait_ge(newton, n0 + 3)




def memory_phase(nc, c):
    with Phase(nc, "mem") as g:
        mem = g.sb("mem", [P, DT, MEM])
        m_hi, m_lo = g.sb("m_hi", [P, DT, MEM], F32R), g.sb("m_lo", [P, DT, MEM], F32R)
        mk = g.sb("mk", [P, 4, MEM])
        with Phase(nc, "mem0") as f:
            in_sem = f.sem("in")
            block = f.block()

            @block.sync
            def _(sp):
                sp.dma_start(mem[:, :, :], c.a["memT"]).then_inc(in_sem, 16)
                sp.wait_ge(in_sem, 16)

        norm_phase(nc, c, "mem1", MEM, mem, "mem_g", m_hi, m_lo)

        def epilogue(f, sum_free, acc):
            def dve(eng, i, a, first):
                copy(eng, two(at(mk, 2 * i + a), MEM), acc(a)).then_inc(sum_free[a], 1)
            return {"dve": dve}

        body = [((s, c.a["w_mk"]), DT, m_hi, m_lo, True, True) for s in range(2)]
        dense_phase(nc, c, "mem2", MEM, 2, body, epilogue)

        with Phase(nc, "mem3") as f:
            sq, xs, t, y = (f.sb(n, [P, 4, MEM]) for n in ("sq", "xs", "t", "y"))
            raw = f.sb("raw", [P, DT, 512])
            w_hi, w_lo = f.sb("w_hi", [P, DT, 512], F32R), f.sb("w_lo", [P, DT, 512], F32R)
            mv = f.sb("mv", [P, 2, 512])
            ps, pv = f.ps("ps", [P, 2, 512]), f.ps("pv", [P, 2, 512])
            squared, mean, root, newton = f.sem("squared"), f.sem("mean"), f.sem("root"), f.sem("newton")
            loaded, hi_done, lo_done, mv_sum, mv_out, out = (
                f.sem(n) for n in ("loaded", "hi_done", "lo_done", "mv_sum", "mv_out", "out"))
            block = f.block()

            @block.sync
            def _(sp):
                sp.dma_start(raw[:, :, :], c.a["w_mv"]).then_inc(loaded, 16)
                sp.wait_ge(newton, 5)
                sp.dma_start(c.a["o_mk"], mk[:, :, :]).then_inc(out, 16)
                sp.wait_ge(mv_out, 1)
                sp.dma_start(c.a["o_mv"], mv[:, :, :]).then_inc(out, 16)
                sp.wait_ge(out, 32)

            @block.scalar
            def _(act):
                act.activation(sq[:, :, :], mk[:, :, :], ACT.Square).then_inc(squared, 1)
                act.wait_ge(loaded, 16)
                act.activation(w_hi[:, :, :], raw[:, :, :], ACT.Copy).then_inc(hi_done, 1)
                rsqrt_act(act, c, xs[:, :, :], t[:, :, :], y[:, :, :], root, 0, newton, 1)

            @block.gpsimd
            def _(pool):
                pool.wait_ge(hi_done, 1)
                pool.tensor_tensor(w_lo[:, :, :], raw[:, :, :], w_hi[:, :, :].bitcast(F32),
                                   ALU.subtract).then_inc(lo_done, 1)

            @block.tensor
            def _(pe):
                pe.wait_ge(squared, 1)
                for n in range(2):
                    mm = pe.matmul(ps[:, n, :], c.ones[:, :], sq[:, 2 * n:2 * n + 2, :].rearrange("p a t -> p (a t)"),
                                   start=True, stop=True)
                mm.then_inc(mean, 1)
                pe.wait_ge(lo_done, 1)
                for n in range(2):
                    tok = slice(n * P, (n + 1) * P)
                    for k in range(DT):
                        pe.matmul(pv[:, n, :], m_hi[:, k, tok], w_hi[:, k, :], start=(k == 0), stop=False)
                        pe.matmul(pv[:, n, :], m_hi[:, k, tok], w_lo[:, k, :], start=False, stop=False)
                        mm = pe.matmul(pv[:, n, :], m_lo[:, k, tok], w_hi[:, k, :], start=False, stop=(k == DT - 1))
                mm.then_inc(mv_sum, 1)

            @block.vector
            def _(dve):
                dve.wait_ge(mean, 1)
                dve.tensor_scalar(xs[:, :, :].rearrange("p (n a) t -> p n (a t)", n=2), ps[:, :, :], 1.0 / P, RMS_EPS,
                                  ALU.mult, ALU.add).then_inc(newton, 1)
                rsqrt_dve(dve, xs[:, :, :], t[:, :, :], y[:, :, :], root, 0, newton, 1)
                dve.scalar_tensor_tensor(mk[:, :, :], mk[:, :, :], vec(c, "mkn"), y[:, :, :], ALU.mult,
                                         ALU.mult).then_inc(newton, 1)
                dve.wait_ge(mv_sum, 1)
                dve.tensor_copy(mv[:, :, :], pv[:, :, :]).then_inc(mv_out, 1)




def attention_prep(nc, c, tag, g, T, pa, kw, vw):
    nb, nt = pieces(T)
    normed_tiles = [0, 1, 2, 3, 4, 6, 7, 8, 9]
    n_n = len(normed_tiles)
    prompt = T if g == 0 else PROMPT_END
    with Phase(nc, tag) as f:
        sq = f.sb("sq", [P, 2, T])
        xs, t, y = (f.sb(n, [P, n_n, T]) for n in ("xs", "t", "y"))
        ps = f.ps("ps", [P, 2, 2, 512])
        squared, ss, ss_read = f.sem("squared"), f.sem("ss"), f.sem("ss_read")
        root, newton, done, out, v_done, cache = (
            f.sem(n) for n in ("root", "newton", "done", "out", "v_done", "cache"))
        block = f.block()

        @block.sync
        def _(sp):
            if g == 1:
                w0 = WINDOW + PROMPT_END
                sp.dma_start(kw[:, w0:w0 + WINDOW], c.a["cache_k"]).then_inc(cache, 16)
                sp.dma_start(vw[:, w0:w0 + WINDOW], c.a["cache_v"]).then_inc(cache, 16)
                sp.wait_ge(cache, 32)
                sp.wait_ge(done, n_n)
                sp.wait_ge(v_done, 1)
                for dst, src in (("o_kp", kw[:, PROMPT_END:PROMPT_END + WINDOW]),
                                 ("o_vp", vw[:, PROMPT_END:PROMPT_END + WINDOW]),
                                 ("o_ks", kw[:, w0 + CHUNK:w0 + KEYS]), ("o_vs", vw[:, w0 + CHUNK:w0 + KEYS])):
                    sp.dma_start(c.a[dst], src).then_inc(out, 16)
                sp.wait_ge(out, 64)

        @block.gpsimd
        def _(pool):
            pool.tensor_copy(vw[:, WINDOW:WINDOW + prompt], pa[:, 5, 0:prompt])
            if g == 0:
                pool.memset(kw[:, 0:WINDOW], 0.0)
                pool.memset(vw[:, 0:WINDOW], 0.0).then_inc(v_done, 1)
            else:
                pool.tensor_copy(vw[:, 2 * WINDOW + prompt:2 * WINDOW + T], pa[:, 5, prompt:T])
                pool.tensor_copy(kw[:, 0:WINDOW], c.kv_carry[:, 0])
                pool.tensor_copy(vw[:, 0:WINDOW], c.kv_carry[:, 1]).then_inc(v_done, 1)

        @block.scalar
        def _(act):
            for n, m in enumerate(normed_tiles):
                if n >= 2:
                    act.wait_ge(ss, n - 1)
                act.activation(sq[:, n % 2], pa[:, m], ACT.Square).then_inc(squared, 1)
            rsqrt_act(act, c, xs[:, :, :], t[:, :, :], y[:, :, :], root, 0, ss_read, n_n)

        @block.tensor
        def _(pe):
            for n, m in enumerate(normed_tiles):
                pe.wait_ge(squared, n + 1)
                if n >= 2:
                    pe.wait_ge(ss_read, n - 1)
                for b in range(nb):
                    mm = pe.matmul(ps[:, n % 2, b, 0:nt], (c.ones_head if m < 5 else c.ones)[:, :],
                                   sq[:, n % 2, b * nt:(b + 1) * nt], start=True, stop=True)
                mm.then_inc(ss, 1)

        @block.vector
        def _(dve):
            for n, m in enumerate(normed_tiles):
                dve.wait_ge(ss, n + 1)
                dve.tensor_scalar(two(xs[:, n], T), ps[:, n % 2, 0:nb, 0:nt], 1.0 / (64 if m < 5 else P), RMS_EPS,
                                  ALU.mult, ALU.add).then_inc(ss_read, 1)
            rsqrt_dve(dve, xs[:, :, :], t[:, :, :], y[:, :, :], root, 0, newton, 0)
            for n, m in enumerate(normed_tiles):
                gain = vec(c, "qn" if m < 4 else "kn" if m == 4 else "mqn")
                if m != 4:
                    dve.scalar_tensor_tensor(pa[:, m], pa[:, m], gain, y[:, n], ALU.mult, ALU.mult).then_inc(done, 1)
                    continue
                ins = dve.scalar_tensor_tensor(kw[:, WINDOW:WINDOW + prompt], pa[:, m, 0:prompt], gain,
                                               y[:, n, 0:prompt], ALU.mult, ALU.mult)
                if g == 1:
                    ins = dve.scalar_tensor_tensor(kw[:, 2 * WINDOW + prompt:2 * WINDOW + T], pa[:, m, prompt:T], gain,
                                                   y[:, n, prompt:T], ALU.mult, ALU.mult)
                ins.then_inc(done, 1)
            if g == 0:
                dve.wait_ge(done, n_n)
                dve.wait_ge(v_done, 1)
                dve.tensor_copy(c.kv_carry[:, 0], kw[:, T:T + WINDOW])
                dve.tensor_copy(c.kv_carry[:, 1], vw[:, T:T + WINDOW])


def attention_phase(nc, c, tag, g, T, pa, kw, vw, o):
    n_chunks = T // CHUNK
    with Phase(nc, tag) as f:
        alibi = f.sb("alibi", [P, 3, 4, KEYS])
        mk, mv = f.sb("mk", [P, 2, 4, MEM]), f.sb("mv", [P, 2, 2, 512])
        q, qm = f.sb("q", [P, 4, CHUNK]), f.sb("qm", [P, 4, CHUNK])
        kwin, vwin = f.sb("kwin", [P, KEYS]), f.sb("vwin", [P, KEYS])
        s, p = f.sb("s", [P, 4, KEYS]), f.sb("p", [P, 4, KEYS])
        pm = f.sb("pm", [P, 2, MEM])
        top, neg, srow, total, inv = (f.sb(n, [P, 4]) for n in ("top", "neg", "srow", "total", "inv"))
        esink = f.sb("esink", [P, 4])
        mtop, mneg, mtotal, minv = (f.sb(n, [P, 2]) for n in ("mtop", "mneg", "mtotal", "minv"))
        vt = f.sb("vt", [P, 2, P])
        pt, pt_tail, pmt = f.sb("pt", [P, 4, P]), f.sb("pt_tail", [CHUNK, 4, P]), f.sb("pmt", [P, 4, P])
        ps_s, ps_m = f.ps("ps_s", [P, 2, 512]), f.ps("ps_m", [P, 2, MEM])
        ps_v = f.ps("ps_v", [P, 4, P])
        ps_t, ps_tail, ps_mt = f.ps("ps_t", [P, 4, P]), f.ps("ps_tail", [P, 4, P]), f.ps("ps_mt", [P, 4, P])
        ps_o = f.ps("ps_o", [P, 8, CHUNK])
        names = ("consts staged swa_scores mem_scores v_turned v_read biased topped shifted sink_exp exps summed "
                 "inverse scaled turned pt_read tail_read mem_top mem_neg mem_exps mem_inv mem_scaled mem_turned "
                 "pmt_read pv mem_pv swa_out mem_out").split()
        S = {n: f.sem(n) for n in names}
        block = f.block()

        def plan(c_):
            if g == 1 and c_ == n_chunks - 1:
                return WINDOW + PROMPT_END, 2, 1
            return CHUNK * c_, (c_ if g == 0 and c_ < 2 else 2), 0

        def chunks(eng, body):
            peeled = 2 if g == 0 else 1
            last = n_chunks if g == 0 else n_chunks - 1
            for i in range(peeled):
                body(i, i == 0, *plan(i))
            with eng.Fori(peeled, last) as i:
                body(i, False, i * CHUNK, 2, 0)
            if g == 1:
                body(last, False, *plan(last))

        @block.sync
        def _(sp):
            sp.dma_start(alibi[:, :, :, :], c.a["alibi"]).then_inc(S["consts"], 16)
            sp.dma_start(mk[:, 0], c.a["o_mk"]).then_inc(S["consts"], 16)
            sp.dma_start(mv[:, 0], c.a["o_mv"]).then_inc(S["consts"], 16)
            sp.dma_start(mk[:, 1], c.a["cache_mk"]).then_inc(S["consts"], 16)
            sp.dma_start(mv[:, 1], c.a["cache_mv"]).then_inc(S["consts"], 16)
            sp.wait_ge(S["consts"], 80)

        @block.gpsimd
        def _(pool):
            def chunk(i, first, win, bias, mem):
                if not first:
                    pool.wait_ge(S["swa_scores"], i)
                    pool.wait_ge(S["mem_scores"], i)
                    pool.wait_ge(S["v_turned"], i)
                pool.tensor_copy(q[:, :, :], cols(pa, slice(0, 4), i * CHUNK, CHUNK))
                pool.tensor_copy(kwin[:, :], kw[:, win:win + KEYS] if isinstance(win, int) else kw[:, bass.ds(win, KEYS)])
                pool.tensor_copy(vwin[:, :], vw[:, win:win + KEYS] if isinstance(win, int) else vw[:, bass.ds(win, KEYS)])
                pool.tensor_copy(qm[:, :, :], cols(pa, slice(6, 10), i * CHUNK, CHUNK)).then_inc(S["staged"], 1)

            chunks(pool, chunk)

        @block.tensor
        def _(pe):
            pe.wait_ge(S["consts"], 80)

            def chunk(i, first, win, bias, mem):
                pe.wait_ge(S["staged"], i + 1)
                if not first:
                    pe.wait_ge(S["biased"], i)
                    pe.wait_ge(S["v_read"], i)
                pe.transpose(ps_v[:, 0, :], vwin[:, 0:P], c.ident[:, :])
                pe.matmul(ps_v[0:CHUNK, 1, :], vwin[:, P:KEYS], c.ident[:, :],
                          start=True, stop=True).then_inc(S["v_turned"], 1)
                for j in range(4):
                    for e in range(2):
                        h = slice(64 * e, 64 * e + 64)
                        mm = pe.matmul(ps_s[h, j // 2, (j % 2) * KEYS:(j % 2 + 1) * KEYS], q[h, j, :], kwin[h, :],
                                       start=True, stop=True)
                mm.then_inc(S["swa_scores"], 1)
                if not first:
                    pe.wait_ge(S["mem_exps"], i)
                for h in range(4):
                    mm = pe.matmul(ps_m[64 * (h % 2):64 * (h % 2) + 64, h // 2, :], qm[:, h, :], mk[:, mem, h, :],
                                   start=True, stop=True)
                mm.then_inc(S["mem_scores"], 1)
                pe.wait_ge(S["scaled"], i + 1)
                if not first:
                    pe.wait_ge(S["pt_read"], i)
                    pe.wait_ge(S["tail_read"], i)
                for j in range(4):
                    pe.transpose(ps_t[:, j, :], p[:, j, 0:P], c.ident[:, :])
                for j in range(4):
                    mm = pe.matmul(ps_tail[0:CHUNK, j, :], p[:, j, P:KEYS], c.ident[:, :], start=True, stop=True)
                mm.then_inc(S["turned"], 1)
                pe.wait_ge(S["mem_scaled"], i + 1)
                if not first:
                    pe.wait_ge(S["pmt_read"], i)
                for a in range(4):
                    mm = pe.transpose(ps_mt[:, a, :], pm[:, a // 2, (a % 2) * P:(a % 2 + 1) * P], c.ident[:, :])
                mm.then_inc(S["mem_turned"], 1)
                pe.wait_ge(S["v_read"], i + 1)
                pe.wait_ge(S["pt_read"], i + 1)
                pe.wait_ge(S["tail_read"], i + 1)
                if not first:
                    pe.wait_ge(S["swa_out"], i)
                    pe.wait_ge(S["mem_out"], i)
                for e in range(2):
                    h = slice(64 * e, 64 * e + 64)
                    pe.matmul(ps_o[h, 0:4, :], vt[:, 0, h], pt[:, :, h], start=True, stop=False)
                    mm = pe.matmul(ps_o[h, 0:4, :], vt[0:CHUNK, 1, h], pt_tail[:, :, h], start=False, stop=True)
                mm.then_inc(S["pv"], 1)
                pe.wait_ge(S["pmt_read"], i + 1)
                for h in range(4):
                    q_ = slice(64 * (h % 2), 64 * (h % 2) + 64)
                    for half in range(2):
                        mm = pe.matmul(ps_o[:, 4 + h, :], mv[:, mem, half, h * P:(h + 1) * P],
                                       pmt[:, 2 * (h // 2) + half, q_], start=(half == 0), stop=(half == 1))
                mm.then_inc(S["mem_pv"], 1)

            chunks(pe, chunk)

        @block.vector
        def _(dve):
            dve.wait_ge(S["consts"], 80)

            def chunk(i, first, win, bias, mem):
                dve.wait_ge(S["swa_scores"], i + 1)
                for a in range(2):
                    ins = dve.scalar_tensor_tensor(
                        s[:, 2 * a:2 * a + 2, :], ps_s[:, a, 0:2 * KEYS].rearrange("p (j k) -> p j k", j=2), 0.125,
                        alibi[:, bias, 2 * a:2 * a + 2, :], ALU.mult, ALU.add)
                ins.then_inc(S["biased"], 1)
                dve.wait_ge(S["biased"], i + 1)
                dve.tensor_reduce(top[:, :], s[:, :, :], AX.X, ALU.max).then_inc(S["topped"], 1)
                dve.wait_ge(S["mem_scores"], i + 1)
                dve.tensor_reduce(mtop[:, :], ps_m[:, :, :], AX.X, ALU.max).then_inc(S["mem_top"], 1)
                dve.wait_ge(S["topped"], 3 * i + 1)
                dve.tensor_tensor(top[:, :], top[:, :], vec(c, "sink", 0, 4), ALU.max).then_inc(S["topped"], 1)
                dve.wait_ge(S["mem_top"], i + 1)
                dve.tensor_scalar(mneg[:, :], mtop[:, :], -float(P) ** -0.5, None, ALU.mult).then_inc(S["mem_neg"], 1)
                dve.wait_ge(S["topped"], 3 * i + 2)
                dve.tensor_scalar(neg[:, :], top[:, :], -1.0, None, ALU.mult)
                dve.tensor_tensor(srow[:, :], vec(c, "sink", 0, 4), top[:, :], ALU.subtract).then_inc(S["topped"], 1)
                dve.wait_ge(S["v_turned"], i + 1)
                if not first:
                    dve.wait_ge(S["pv"], i)
                dve.tensor_copy(vt[:, 0, :], ps_v[:, 0, :])
                dve.tensor_copy(vt[0:CHUNK, 1, :], ps_v[0:CHUNK, 1, :]).then_inc(S["v_read"], 1)
                dve.wait_ge(S["exps"], i + 1)
                dve.tensor_tensor(total[:, :], total[:, :], esink[:, :], ALU.add).then_inc(S["summed"], 1)
                dve.wait_ge(S["summed"], i + 1)
                dve.reciprocal(inv[:, :], total[:, :]).then_inc(S["inverse"], 1)
                dve.wait_ge(S["inverse"], i + 1)
                dve.tensor_tensor(p[:, :, :], p[:, :, :], inv[:, :].unsqueeze(2).to_broadcast([P, 4, KEYS]),
                                  ALU.mult).then_inc(S["scaled"], 1)
                dve.wait_ge(S["mem_exps"], i + 1)
                dve.reciprocal(minv[:, :], mtotal[:, :]).then_inc(S["mem_inv"], 1)
                dve.wait_ge(S["mem_inv"], i + 1)
                dve.tensor_tensor(pm[:, :, :], pm[:, :, :], minv[:, :].unsqueeze(2).to_broadcast([P, 2, MEM]),
                                  ALU.mult).then_inc(S["mem_scaled"], 1)
                dve.wait_ge(S["turned"], i + 1)
                if not first:
                    dve.wait_ge(S["pv"], i)
                dve.tensor_copy(pt_tail[:, :, :], ps_tail[0:CHUNK, :, :]).then_inc(S["tail_read"], 1)
                dve.wait_ge(S["mem_pv"], i + 1)
                copy(dve, cols(o, slice(0, 4), i * CHUNK, CHUNK), ps_o[:, 0:4, :]).then_inc(S["swa_out"], 1)
                copy(dve, cols(o, slice(4, 8), i * CHUNK, CHUNK), ps_o[:, 4:8, :]).then_inc(S["mem_out"], 1)

            chunks(dve, chunk)

        @block.scalar
        def _(act):
            def chunk(i, first, win, bias, mem):
                act.wait_ge(S["topped"], 3 * i + 3)
                if not first:
                    act.wait_ge(S["turned"], i)
                for j in range(4):
                    act.activation(p[:, j, :], s[:, j, :], ACT.Exp, bias=neg[:, j:j + 1], accum_out=total[:, j:j + 1])
                act.activation(esink[:, :], srow[:, :], ACT.Exp).then_inc(S["exps"], 1)
                act.wait_ge(S["mem_neg"], i + 1)
                if not first:
                    act.wait_ge(S["mem_turned"], i)
                for a in range(2):
                    ins = act.activation(pm[:, a, :], ps_m[:, a, :], ACT.Exp, bias=mneg[:, a:a + 1],
                                         scale=float(P) ** -0.5, accum_out=mtotal[:, a:a + 1])
                ins.then_inc(S["mem_exps"], 1)
                act.wait_ge(S["turned"], i + 1)
                if not first:
                    act.wait_ge(S["pv"], i)
                act.activation(pt[:, :, :], ps_t[:, :, :], ACT.Copy).then_inc(S["pt_read"], 1)
                act.wait_ge(S["mem_turned"], i + 1)
                if not first:
                    act.wait_ge(S["mem_pv"], i)
                act.activation(pmt[:, :, :], ps_mt[:, :, :], ACT.Copy).then_inc(S["pmt_read"], 1)

            chunks(act, chunk)



RAW, MIX, EXTRA = 0, 14, 28
X_BON, X_CUM, X_KK, X_G = slice(0, 4), slice(4, 8), slice(8, 12), slice(12, 16)
X_WA, X_XG = 14, 15
LOW, LOW_T, EYE, OFF, UP, BD, BD_LOW, BD_LOW_T, BD_UP = range(9)
X_R, X_K, X_V, X_B = slice(16, 20), slice(20, 24), slice(24, 28), slice(28, 32)


def rwkv_prep(nc, c, tag, g, T, ar):
    nb, nt = pieces(T)
    with Phase(nc, tag) as f:
        mask = f.sb("mask", [P, T])
        half = f.sb("half", [P, 8])
        one_ka = f.sb("one_ka", [P, 4])
        t1, t2, t3, sq = (f.sb(n, [P, 4, T]) for n in ("t1", "t2", "t3", "sq"))
        ps = f.ps("ps", [P, 2, 2, 512])
        setup, d_done, mixed, lora_in = f.sem("setup"), f.sem("d_done"), f.sem("mixed"), f.sem("lora_in")
        prod, tan, dstep, root, newton, a_free = (
            f.sem(n) for n in ("prod", "tan", "dstep", "root", "newton", "a_free"))
        out, g_done, sq_done = f.sem("out"), f.sem("g_done"), f.sem("sq_done")
        read = f.sem("read")
        block = f.block()
        pp = lambda n: ps[:, n % 2, 0:nb, 0:nt]
        raw = ar[:, RAW:RAW + 14, :]
        mix = ar[:, MIX:MIX + 14, :]

        @block.sync
        def _(sp):
            if g == 1:
                sp.wait_ge(d_done, 4)
                sp.dma_start(c.a["o_shp"], c.shift_out[:, 0]).then_inc(out, 16)
                sp.dma_start(c.a["o_shs"], c.shift_out[:, 1]).then_inc(out, 16)
                sp.wait_ge(out, 32)

        @block.gpsimd
        def _(pool):
            pool.memset(mask[:, :], 1.0).then_inc(setup, 1)
            pool.wait_ge(setup, 1)
            pool.memset(mask[:, :].rearrange("p (c t) -> p c t", t=CHUNK)[:, :, 0:1], 0.0).then_inc(setup, 1)
            pool.tensor_scalar(half[:, :], vec(c, "w0", 0, 8), 0.5, None, ALU.mult).then_inc(setup, 1)
            pool.tensor_scalar(one_ka[:, :], vec(c, "ka", 0, 4), -1.0, 1.0, ALU.mult, ALU.add).then_inc(setup, 1)

        @block.vector
        def _(dve):
            dve.tensor_tensor(mix[:, :, 1:T], raw[:, :, 0:T - 1], raw[:, :, 1:T], ALU.subtract).then_inc(d_done, 1)
            if g == 0:
                dve.tensor_scalar(mix[:, :, 0:1], raw[:, :, 0:1], -1.0, None, ALU.mult).then_inc(d_done, 1)
                dve.tensor_copy(c.shift_carry[:, :], raw[:, :, T - 1]).then_inc(d_done, 1)
            else:
                dve.wait_ge(d_done, 1)
                dve.tensor_tensor(mix[:, :, 0], c.shift_carry[:, :], raw[:, :, 0], ALU.subtract).then_inc(d_done, 1)
                dve.tensor_tensor(mix[:, :, PROMPT_END], vec(c, "shift", 0, 14), raw[:, :, PROMPT_END],
                                  ALU.subtract).then_inc(d_done, 1)
                dve.tensor_copy(c.shift_out[:, 0], raw[:, :, PROMPT_END - 1])
                dve.tensor_copy(c.shift_out[:, 1], raw[:, :, T - 1]).then_inc(d_done, 1)
            dve.wait_ge(d_done, 3 if g == 0 else 4)
            for m in range(14):
                dve.scalar_tensor_tensor(mix[:, m], mix[:, m], vec(c, "mu", m), raw[:, m], ALU.mult,
                                         ALU.add).then_inc(mixed, 1)
            dve.wait_ge(mixed, 14)
            dve.wait_ge(tan, 2)
            dve.tensor_scalar(ar[:, X_XG], ar[:, X_XG], 0.5, 0.5, ALU.mult, ALU.add).then_inc(lora_in, 1)
            dve.wait_ge(tan, 2 + 4)
            dve.tensor_scalar(t1[:, :, :], t1[:, :, :], -0.5 * DECAY, -0.5 * DECAY, ALU.mult, ALU.add).then_inc(dstep, 1)
            dve.wait_ge(dstep, 1)
            dve.wait_ge(setup, 4)
            for m in range(4):
                dve.tensor_tensor_scan(ar[:, 4 + m], mask[:, :], t1[:, m], 0.0, ALU.mult, ALU.add)
            dve.wait_ge(tan, 2 + 8)
            dve.tensor_scalar(t2[:, :, :], t2[:, :, :], 0.5, 0.5, ALU.mult, ALU.add).then_inc(dstep, 1)
            for m in range(4):
                ins = dve.tensor_scalar(ar[:, 8 + m], ar[:, 20 + m], vec(c, "kk", m), None, ALU.mult)
            ins.then_inc(dstep, 1)
            dve.wait_ge(dstep, 3)
            for m in range(4):
                ins = dve.tensor_scalar(t3[:, m], t2[:, m], vec(c, "ka", m), one_ka[:, m:m + 1], ALU.mult, ALU.add)
            ins.then_inc(dstep, 1)
            dve.wait_ge(dstep, 4)
            dve.tensor_tensor(ar[:, X_K, :], ar[:, X_K, :], t3[:, :, :], ALU.mult).then_inc(dstep, 1)
            dve.wait_ge(dstep, 5)
            for m in range(4):
                ins = dve.scalar_tensor_tensor(t3[:, m], ar[:, 16 + m], vec(c, "rk", m), ar[:, 20 + m],
                                               ALU.mult, ALU.mult)
            ins.then_inc(dstep, 1)
            for m in range(4):
                dve.wait_ge(prod, 12 + m + 1)
                ins = dve.tensor_scalar(two(t1[:, m], T), pp(12 + m), 1e-24, None, ALU.max)
                ins.then_inc(read, 1)
            dve.wait_ge(read, 4)
            rsqrt_dve(dve, t1[:, :, :], sq[:, :, :], ar[:, X_B, :], root, 0, newton, 0)
            dve.tensor_tensor(ar[:, X_KK, :], ar[:, X_KK, :], ar[:, X_B, :], ALU.mult).then_inc(dstep, 1)
            dve.wait_ge(dstep, 7)
            dve.tensor_tensor(ar[:, X_B, :], ar[:, X_KK, :], t2[:, :, :], ALU.mult)
            for m in range(4):
                dve.wait_ge(prod, 16 + m + 1)
                dve.tensor_tensor(two(ar[:, m], T), pp(16 + m), two(ar[:, 24 + m], T), ALU.mult).then_inc(read, 1)

        @block.scalar
        def _(act):
            act.wait_ge(mixed, 1)
            act.activation(ar[0:64, X_WA], ar[0:64, X_WA], ACT.Tanh).then_inc(tan, 1)
            act.wait_ge(mixed, 2)
            act.activation(ar[:, X_XG], ar[:, X_XG], ACT.Tanh, scale=0.5).then_inc(tan, 1)
            act.wait_ge(setup, 4)
            for m in range(8):
                act.wait_ge(prod, m + 1)
                dst = t1 if m < 4 else t2
                act.activation(two(dst[:, m % 4], T), pp(m), ACT.Tanh, bias=half[:, m:m + 1], scale=0.5).then_inc(tan, 1)
            for m in range(4):
                act.wait_ge(prod, 8 + m + 1)
                if m == 3:
                    act.wait_ge(prod, 12)
                act.activation(two(ar[:, 12 + m], T), pp(8 + m), ACT.Copy).then_inc(g_done, 1)
            act.wait_ge(dstep, 3)
            act.activation(sq[:, :, :], ar[:, X_KK, :], ACT.Square).then_inc(sq_done, 1)
            rsqrt_act(act, c, t1[:, :, :], sq[:, :, :], ar[:, X_B, :], root, 0, read, 4, scaled=True)

        @block.tensor
        def _(pe):
            def product(n, lhs, rhs, lo, hi):
                for b in range(nb):
                    mm = pe.matmul(ps[:, n % 2, b, 0:nt], lhs, rhs[lo:hi, b * nt:(b + 1) * nt], start=True, stop=True)
                mm.then_inc(prod, 1)

            pe.wait_ge(tan, 1)
            for m in range(4):
                if m >= 2:
                    pe.wait_ge(tan, 2 + m - 1)
                product(m, c.lora[0:64, 0, m * P:(m + 1) * P], ar[:, X_WA], 0, 64)
            for m in range(4):
                pe.wait_ge(tan, 2 + 4 + m - 1)
                product(4 + m, c.lora[64:128, 0, m * P:(m + 1) * P], ar[:, X_WA], 64, 128)
            pe.wait_ge(lora_in, 1)
            for m in range(4):
                pe.wait_ge(tan, min(10, 2 + 8 + m - 1))
                if m >= 2:
                    pe.wait_ge(g_done, m - 1)
                product(8 + m, c.lora[:, 1, m * P:(m + 1) * P], ar[:, X_XG], 0, 128)
            pe.wait_ge(sq_done, 1)
            for m in range(4):
                if m < 2:
                    pe.wait_ge(g_done, 3 + m)
                else:
                    pe.wait_ge(read, m - 1)
                product(12 + m, c.ones_head[:, :], sq[:, m], 0, 128)
            pe.wait_ge(dstep, 6)
            for m in range(4):
                pe.wait_ge(read, 3 + m)
                product(16 + m, c.ones_head[:, :], t3[:, m], 0, 128)


def rwkv_scan(nc, c, tag, g, T, ar, o):
    n_chunks = T // CHUNK
    C = CHUNK
    with Phase(nc, tag) as f:
        two_of = lambda name, shape: [f.sb(f"{name}{u}", shape) for u in range(2)]
        ep, b_s, pc = two_of("ep", [P, 4, C + 1]), two_of("b_s", [P, 4, C]), two_of("pc", [P, 4, 1])
        ar_s, a_bd = two_of("ar_s", [P, 4, 2 * C]), two_of("a_bd", [P, 4, P])
        bk_bd = two_of("bk_bd", [P, 2, 4, P])
        v_bd, v_s = two_of("v_bd", [P, 4, P]), two_of("v_s", [P, 4, C])
        off_s, off_bd = two_of("off_s", [P, 4, C]), two_of("off_bd", [P, 4, P])
        w1_s, w1_bd = two_of("w1_s", [P, 2, 4, C]), two_of("w1_bd", [P, 2, 4, P])
        w2_s, w2_bd = two_of("w2_s", [P, 2, 4, C]), two_of("w2_bd", [P, 2, 4, P])
        y = two_of("y", [P, 2, 4, C])
        lk_bd, mbk = two_of("lk_bd", [P, 4, P]), two_of("mbk", [P, 2, 4, C])
        x, sa_s, sa_bd, s_bd = f.sb("x", [P, 4, C]), f.sb("sa_s", [P, 4, C]), f.sb("sa_bd", [P, 4, P]), f.sb("s_bd", [P, 4, P])
        ps_a = [f.ps(f"ps_a{u}", [P, 2, 4, C]) for u in range(2)]
        ps_b = [f.ps(f"ps_b{u}", [P, 2, 4, C]) for u in range(2)]
        ps_g = f.ps("ps_g", [P, 2, 4, P])
        ps_x, ps_s = f.ps("ps_x", [P, 2, 4, C]), f.ps("ps_s", [P, 2, 4, C])
        names = ("zeros decays shared operands blocks v_in low low_read gram at_read gram_read off hat tok tok_read "
                 "vtok vtok_read pow2 pow2_read pow4 pow4_read y2_read pow8 pow8_read y4_read y8 y8_read invt "
                 "invt_bd nblk nblk_read n_read f1 nsq nsq_read gsum gsum_read tinv tinv_read xs xs_read sa "
                 "sa_read sa_bd s_bd scaled ssum osum o_read state swapped stored").split()
        S = {n: f.sem(n) for n in names}
        block = f.block()
        H = [slice(0, 64), slice(64, 128)]
        M = c.masks
        bc = lambda m: m.unsqueeze(1).to_broadcast([P, 4, m.shape[1]])
        spread = lambda s: s.unsqueeze(2).to_broadcast([P, s.shape[1], 2, C])
        wide = lambda b: b.rearrange("p j (e t) -> p j e t", e=2)
        block_mask = lambda m, n=4: M[:, m].rearrange("p (e t) -> p e t", e=2).unsqueeze(1).to_broadcast(
            [P, n, 2, C])
        pc_of = lambda u, n: pc[u][:, :, 0:1].to_broadcast([P, 4, n])

        def pairs(eng, body):
            n_loop = n_chunks // 2 - 1
            pair = lambda i: ((2 * i, 0, False), (2 * i + 1, 1, False))
            end = ((n_chunks - 1, 0, False),) if n_chunks % 2 else pair(n_chunks // 2 - 1)
            body(((0, 0, True), (1, 1, True)), pair(1))
            with eng.Fori(1, n_loop) as i:
                body(pair(i), pair(i + 1))
            if n_chunks % 2:
                body(pair(n_loop), end)
            body(end, ())

        def to_blocks(act, dst, src):
            for e in range(2):
                ins = act.activation(dst[H[e], :, e * C:(e + 1) * C], src[H[e]], ACT.Copy)
            return ins

        def is_sample(n):
            return g == 1 and isinstance(n, int) and n == n_chunks - 1

        @block.scalar
        def _(act):
            def decays(us):
                for n, u, early in us:
                    if not early:
                        act.wait_ge(S["shared"], n - 1)
                        act.wait_ge(S["gram"], n - 1)
                    act.activation(ep[u][:, :, 1:C + 1], cols(ar, X_CUM, n * C, C), ACT.Exp)
                    act.activation(b_s[u][:, :, :], cols(ar, X_CUM, n * C, C), ACT.Exp,
                                   scale=-1.0).then_inc(S["decays"], 1)

            def body(us, nxt):
                for n, u, early in us:
                    act.wait_ge(S["vtok"], n + 1)
                    act.activation(v_s[u][:, :, :], ps_b[u][:, 1], ACT.Copy)
                    to_blocks(act, v_bd[u], ps_b[u][:, 1]).then_inc(S["vtok_read"], 1)
                for n, u, early in us:
                    act.wait_ge(S["pow2"], n + 1)
                    act.activation(w2_s[u][:, :, :, :], ps_a[u][:, :, :, :], ACT.Copy)
                    to_blocks(act, w2_bd[u].rearrange("p q j t -> p (q j) t"),
                              ps_a[u].rearrange("p q j t -> p (q j) t")).then_inc(S["pow2_read"], 1)
                for n, u, early in us:
                    act.wait_ge(S["tok"], n + 1)
                    to_blocks(act, bk_bd[u].rearrange("p q j t -> p (q j) t"),
                              ps_g[:, 0].rearrange("p j (q t) -> p (j q) t", q=2)).then_inc(S["tok_read"], 1)
                for n, u, early in us:
                    act.wait_ge(S["pow8"], n + 1)
                    to_blocks(act, w2_bd[u][:, 0], ps_a[u][:, 0]).then_inc(S["pow8_read"], 1)
                for n, u, early in us:
                    act.wait_ge(S["invt"], n + 1)
                    act.activation(w2_s[u][:, 0], ps_a[u][:, 0], ACT.Copy)
                    to_blocks(act, w2_bd[u][:, 0], ps_a[u][:, 0]).then_inc(S["invt_bd"], 1)
                for n, u, early in us:
                    act.wait_ge(S["nblk"], n + 1)
                    to_blocks(act, w1_bd[u][:, 0], ps_b[u][:, 0]).then_inc(S["nblk_read"], 1)
                for n, u, early in us:
                    act.wait_ge(S["nsq"], n + 1)
                    to_blocks(act, w1_bd[u][:, 1], ps_a[u][:, 0]).then_inc(S["nsq_read"], 1)
                decays(nxt)
                for n, u, early in us:
                    act.wait_ge(S["tinv"], n + 1)
                    to_blocks(act, w2_bd[u][:, 0], ps_a[u][:, 0]).then_inc(S["tinv_read"], 1)
                for n, u, early in us:
                    act.wait_ge(S["sa_read"], n + 1)
                    to_blocks(act, sa_bd, ps_x[:, 1]).then_inc(S["sa_bd"], 1)
                    act.wait_ge(S["osum"], n + 1)
                    act.activation(cols(o, slice(0, 4), n * C, C), ps_b[u][:, 1], ACT.Copy).then_inc(S["o_read"], 1)

            act.wait_ge(S["zeros"], 1)
            decays(((0, 0, True), (1, 1, True)))
            pairs(act, body)

        @block.gpsimd
        def _(pool):
            for u in range(2):
                pool.memset(ep[u][:, :, 0:1], 1.0)
                for b in (bk_bd[u], w2_bd[u]):
                    pool.memset(b[:, :, :, :], 0.0)
                pool.memset(v_bd[u][:, :, :], 0.0)
            pool.memset(sa_bd[:, :, :], 0.0).then_inc(S["zeros"], 1)

            def blocks(us):
                for n, u, early in us:
                    if not early:
                        pool.wait_ge(S["osum"], n - 1)
                    pool.tensor_tensor(wide(v_bd[u]), spread(cols(ar, X_V, n * C, C)), block_mask(BD),
                                       ALU.mult).then_inc(S["v_in"], 1)
                    pool.wait_ge(S["operands"], n + 1)
                    pool.tensor_tensor(wide(a_bd[u]), spread(ar_s[u][:, :, 0:C]), block_mask(BD), ALU.mult)
                    pool.tensor_tensor(wide(bk_bd[u][:, 0]), spread(b_s[u][:, :, :]), block_mask(BD),
                                       ALU.mult).then_inc(S["blocks"], 1)

            def body(us, nxt):
                for n, u, early in us:
                    pool.wait_ge(S["gram"], n + 1)
                    for q in range(2):
                        ins = pool.tensor_tensor(bk_bd[u][:, q], bk_bd[u][:, q], pc_of(u, P), ALU.mult)
                    ins.then_inc(S["hat"], 1)
                for n, u, early in us:
                    pool.wait_ge(S["low_read"], 2 * n + 2)
                    pool.tensor_tensor(wide(off_bd[u]), spread(off_s[u][:, :, :]), block_mask(BD),
                                       ALU.mult).then_inc(S["off"], 1)
                for n, u, early in us:
                    if is_sample(n):
                        pool.wait_ge(S["swapped"], 2)
                    elif not (early and n == 0):
                        pool.wait_ge(S["state"], n)
                    if not (early and n == 0):
                        pool.wait_ge(S["osum"], n)
                    pool.tensor_tensor(wide(s_bd), spread(c.state[:, :, :]), block_mask(BD),
                                       ALU.mult).then_inc(S["s_bd"], 1)
                blocks(nxt)

            pool.wait_ge(S["zeros"], 1)
            blocks(((0, 0, True), (1, 1, True)))
            pairs(pool, body)

        @block.vector
        def _(dve):
            def operands(us):
                for n, u, early in us:
                    dve.wait_ge(S["decays"], n + 1)
                    if not early:
                        dve.wait_ge(S["osum"], n - 1)
                        dve.wait_ge(S["state"], n - 1)
                    dve.scalar_tensor_tensor(ar_s[u][:, :, 0:C], cols(ar, X_KK, n * C, C), -1.0, ep[u][:, :, 0:C],
                                             ALU.mult, ALU.mult)
                    dve.tensor_tensor(ar_s[u][:, :, C:2 * C], cols(ar, X_R, n * C, C), ep[u][:, :, 1:C + 1], ALU.mult)
                    for e in range(2):
                        src = ar[H[e], X_K, n * C:(n + 1) * C] if isinstance(n, int) else (
                            ar[H[e], X_K, bass.ds(n * C, C)])
                        ins = dve.tensor_tensor(bk_bd[u][H[e], 1, :, e * C:(e + 1) * C], src, b_s[u][H[e], :, :],
                                                ALU.mult)
                    dve.tensor_copy(pc[u][:, :, :], ep[u][:, :, C:C + 1]).then_inc(S["shared"], 1)
                    dve.wait_ge(S["shared"], n + 1)
                    dve.tensor_tensor(b_s[u][:, :, :], cols(ar, X_B, n * C, C), b_s[u][:, :, :],
                                      ALU.mult).then_inc(S["operands"], 1)

            def body(us, nxt):
                for n, u, early in us:
                    dve.wait_ge(S["low"], n + 1)
                    low = ps_a[u][:, 0]
                    dve.tensor_tensor(w1_s[u][:, 0], low, bc(M[:, LOW, 0:C]), ALU.mult).then_inc(S["low_read"], 1)
                    dve.tensor_tensor(wide(w1_bd[u][:, 0]), spread(low), block_mask(BD_LOW), ALU.mult)
                    dve.tensor_tensor(off_s[u][:, :, :], low, bc(M[:, OFF, 0:C]), ALU.mult)
                    dve.wait_ge(S["low_read"], 2 * n + 1)
                    dve.tensor_tensor(y[u][:, 0], w1_s[u][:, 0], bc(M[:, EYE, 0:C]), ALU.add).then_inc(S["low_read"], 1)
                    dve.wait_ge(S["gram"], n + 1)
                    dve.tensor_tensor(w1_s[u][:, 1], ps_g[:, 0, :, 0:C], bc(M[:, LOW_T, 0:C]), ALU.mult)
                    dve.tensor_tensor(wide(w1_bd[u][:, 1]), spread(ps_g[:, 0, :, 0:C]), block_mask(BD_LOW_T),
                                      ALU.mult).then_inc(S["at_read"], 1)
                    dve.tensor_tensor(mbk[u][:, :, :, :].rearrange("p q j t -> p (q j) t"),
                                      ps_g[:, :, :, C:2 * C].rearrange("p q j t -> p (q j) t"),
                                      M[:, UP, C:2 * C].unsqueeze(1).to_broadcast([P, 8, C]), ALU.mult)
                    dve.tensor_tensor(wide(lk_bd[u]), spread(ps_g[:, 1, :, 0:C]), block_mask(BD_UP),
                                      ALU.mult).then_inc(S["gram_read"], 1)
                for n, u, early in us:
                    dve.wait_ge(S["pow4"], n + 1)
                    dve.tensor_tensor(wide(w1_bd[u].rearrange("p q j t -> p (q j) t")),
                                      spread(ps_a[u].rearrange("p q j t -> p (q j) t")), block_mask(BD, 8), ALU.mult)
                    dve.tensor_copy(w1_s[u][:, 1], ps_a[u][:, 1]).then_inc(S["pow4_read"], 1)
                    dve.tensor_tensor(y[u][:, 1], ps_b[u][:, 0], y[u][:, 0], ALU.add).then_inc(S["y2_read"], 1)
                for n, u, early in us:
                    dve.wait_ge(S["pow8"], n + 1)
                    dve.wait_ge(S["y2_read"], n + 1)
                    dve.tensor_tensor(y[u][:, 0], ps_b[u][:, 0], y[u][:, 1], ALU.add).then_inc(S["y4_read"], 1)
                for n, u, early in us:
                    dve.wait_ge(S["y8"], n + 1)
                    dve.wait_ge(S["y4_read"], n + 1)
                    for e in range(2):
                        ins = dve.tensor_tensor(w2_bd[u][H[e], 1, :, e * C:(e + 1) * C], ps_b[u][H[e], 0],
                                                y[u][H[e], 0], ALU.add)
                    ins.then_inc(S["y8_read"], 1)
                for n, u, early in us:
                    dve.wait_ge(S["nblk"], n + 1)
                    dve.tensor_copy(w1_s[u][:, 0], ps_a[u][:, 0]).then_inc(S["n_read"], 1)
                    dve.wait_ge(S["nblk_read"], n + 1)
                    dve.tensor_tensor(y[u][:, 1], ps_b[u][:, 0], bc(M[:, EYE, 0:C]), ALU.add).then_inc(S["f1"], 1)
                for n, u, early in us:
                    dve.wait_ge(S["gsum"], n + 1)
                    dve.wait_ge(S["f1"], n + 1)
                    dve.tensor_tensor(w2_s[u][:, 1], ps_b[u][:, 0], y[u][:, 1], ALU.add).then_inc(S["gsum_read"], 1)
                for n, u, early in us:
                    if is_sample(n):
                        dve.wait_ge(S["state"], n)
                        dve.tensor_copy(c.state_out[:, :, :], c.state[:, :, :]).then_inc(S["swapped"], 1)
                        dve.wait_ge(S["swapped"], 1)
                        dve.tensor_copy(c.state[:, :, :], c.state_in[:, :, :]).then_inc(S["swapped"], 1)
                        dve.wait_ge(S["swapped"], 2)
                    dve.wait_ge(S["xs"], n + 1)
                    dve.tensor_copy(x[:, :, :], ps_x[:, 0]).then_inc(S["xs_read"], 1)
                    dve.wait_ge(S["s_bd"], n + 1)
                    dve.tensor_tensor(c.state[:, :, :], c.state[:, :, :], pc_of(u, C), ALU.mult).then_inc(S["scaled"], 1)
                    dve.wait_ge(S["sa"], n + 1)
                    dve.tensor_copy(sa_s[:, :, :], ps_x[:, 1]).then_inc(S["sa_read"], 1)
                    dve.wait_ge(S["ssum"], n + 1)
                    dve.wait_ge(S["scaled"], n + 1)
                    dve.tensor_tensor(c.state[:, :, :], ps_s[:, 0], c.state[:, :, :], ALU.add).then_inc(S["state"], 1)
                operands(nxt)

            dve.wait_ge(S["zeros"], 1)
            operands(((0, 0, True), (1, 1, True)))
            pairs(dve, body)

        @block.tensor
        def _(pe):
            def heads(out, lhs, rhs, start=True, stop=True):
                for j in range(4):
                    mm = pe.matmul(out[:, j, :], lhs[:, j, :], rhs[:, j, :], start=start, stop=stop)
                return mm

            eye = bc(M[:, EYE, 0:C])

            def body(us, nxt):
                last = us[-1][0]
                for n, u, early in us:
                    pe.wait_ge(S["blocks"], n + 1)
                    if not early:
                        pe.wait_ge(S["tinv_read"], n - 1)
                    heads(ps_a[u][:, 0], a_bd[u], b_s[u]).then_inc(S["low"], 1)
                    pe.wait_ge(S["v_in"], n + 1)
                    if not early:
                        pe.wait_ge(S["gsum_read"], n - 1)
                        pe.wait_ge(S["o_read"], n - 1)
                    heads(ps_b[u][:, 1], v_bd[u], eye).then_inc(S["vtok"], 1)
                    if u:
                        pe.wait_ge(S["gram_read"], n)
                    elif not early:
                        pe.wait_ge(S["tok_read"], n)
                    heads(ps_g[:, 0], bk_bd[u][:, 0], ar_s[u])
                    heads(ps_g[:, 1], bk_bd[u][:, 1], ar_s[u]).then_inc(S["gram"], 1)
                for n, u, early in us:
                    pe.wait_ge(S["low_read"], 2 * n + 2)
                    pe.wait_ge(S["at_read"], n + 1)
                    heads(ps_a[u][:, 0], w1_bd[u][:, 1], w1_s[u][:, 0])
                    heads(ps_a[u][:, 1], w1_bd[u][:, 0], w1_s[u][:, 1]).then_inc(S["pow2"], 1)
                for n, u, early in us:
                    pe.wait_ge(S["hat"], n + 1)
                    pe.wait_ge(S["gram_read"], last + 1)
                    if u:
                        pe.wait_ge(S["tok_read"], n)
                    turned = ps_g[:, 0].rearrange("p j (q t) -> p (j q) t", q=2)
                    heads(turned[:, 0:4], bk_bd[u][:, 0], eye)
                    heads(turned[:, 4:8], bk_bd[u][:, 1], eye).then_inc(S["tok"], 1)
                for n, u, early in us:
                    pe.wait_ge(S["pow2_read"], n + 1)
                    pe.wait_ge(S["vtok_read"], n + 1)
                    heads(ps_a[u][:, 0], w2_bd[u][:, 1], w2_s[u][:, 0])
                    heads(ps_a[u][:, 1], w2_bd[u][:, 0], w2_s[u][:, 1])
                    heads(ps_b[u][:, 0], w2_bd[u][:, 1], y[u][:, 0]).then_inc(S["pow4"], 1)
                for n, u, early in us:
                    pe.wait_ge(S["pow4_read"], n + 1)
                    pe.wait_ge(S["y2_read"], n + 1)
                    heads(ps_a[u][:, 0], w1_bd[u][:, 0], w1_s[u][:, 1])
                    heads(ps_b[u][:, 0], w1_bd[u][:, 1], y[u][:, 1]).then_inc(S["pow8"], 1)
                for n, u, early in us:
                    pe.wait_ge(S["pow8_read"], n + 1)
                    pe.wait_ge(S["y4_read"], n + 1)
                    heads(ps_b[u][:, 0], w2_bd[u][:, 0], y[u][:, 0]).then_inc(S["y8"], 1)
                for n, u, early in us:
                    pe.wait_ge(S["y8_read"], n + 1)
                    heads(ps_a[u][:, 0], w2_bd[u][:, 1], eye).then_inc(S["invt"], 1)
                for n, u, early in us:
                    pe.wait_ge(S["off"], n + 1)
                    pe.wait_ge(S["invt_bd"], n + 1)
                    heads(ps_b[u][:, 0], off_bd[u], w2_s[u][:, 0])
                    heads(ps_a[u][:, 0], w2_bd[u][:, 0], off_s[u]).then_inc(S["nblk"], 1)
                for n, u, early in us:
                    pe.wait_ge(S["nblk_read"], n + 1)
                    pe.wait_ge(S["n_read"], n + 1)
                    heads(ps_a[u][:, 0], w1_bd[u][:, 0], w1_s[u][:, 0]).then_inc(S["nsq"], 1)
                for n, u, early in us:
                    pe.wait_ge(S["nsq_read"], n + 1)
                    pe.wait_ge(S["f1"], n + 1)
                    heads(ps_b[u][:, 0], w1_bd[u][:, 1], y[u][:, 1]).then_inc(S["gsum"], 1)
                for n, u, early in us:
                    pe.wait_ge(S["gsum_read"], n + 1)
                    heads(ps_a[u][:, 0], w2_bd[u][:, 1], w2_s[u][:, 1]).then_inc(S["tinv"], 1)
                for n, u, early in us:
                    pe.wait_ge(S["vtok_read"], n + 1)
                    if is_sample(n):
                        pe.wait_ge(S["swapped"], 2)
                    elif not (early and n == 0):
                        pe.wait_ge(S["state"], n)
                    if not (early and n == 0):
                        pe.wait_ge(S["sa_bd"], n)
                    for j in range(4):
                        pe.matmul(ps_x[:, 0, j, :], a_bd[u][:, j, :], c.state[:, j, :], start=True, stop=False)
                        mm = pe.matmul(ps_x[:, 0, j, :], lk_bd[u][:, j, :], v_s[u][:, j, :], start=False, stop=True)
                    mm.then_inc(S["xs"], 1)
                    pe.wait_ge(S["tinv_read"], n + 1)
                    pe.wait_ge(S["xs_read"], n + 1)
                    heads(ps_x[:, 1], w2_bd[u][:, 0], x).then_inc(S["sa"], 1)
                    pe.wait_ge(S["tok_read"], n + 1)
                    pe.wait_ge(S["sa_read"], n + 1)
                    for j in range(4):
                        pe.matmul(ps_s[:, 0, j, :], bk_bd[u][:, 0, j, :], sa_s[:, j, :], start=True, stop=False)
                        mm = pe.matmul(ps_s[:, 0, j, :], bk_bd[u][:, 1, j, :], v_s[u][:, j, :], start=False, stop=True)
                    mm.then_inc(S["ssum"], 1)
                    pe.wait_ge(S["s_bd"], n + 1)
                    pe.wait_ge(S["sa_bd"], n + 1)
                    for j in range(4):
                        out = ps_b[u][:, 1, j, :]
                        pe.matmul(out, s_bd[:, j, :], ar_s[u][:, j, C:2 * C], start=True, stop=False)
                        pe.matmul(out, v_bd[u][:, j, :], mbk[u][:, 1, j, :], start=False, stop=False)
                        mm = pe.matmul(out, sa_bd[:, j, :], mbk[u][:, 0, j, :], start=False, stop=True)
                    mm.then_inc(S["osum"], 1)

            pairs(pe, body)

        @block.sync
        def _(sp):
            if g == 1:
                sp.wait_ge(S["state"], n_chunks)
                sp.dma_start(c.a["o_rp"], c.state_out[:, :, :]).then_inc(S["stored"], 16)
                sp.dma_start(c.a["o_rs"], c.state[:, :, :]).then_inc(S["stored"], 16)
                sp.wait_ge(S["stored"], 32)


def rwkv_post(nc, c, tag, T, ar, o):
    nb, nt = pieces(T)
    with Phase(nc, tag) as f:
        sq, xs, t, y = (f.sb(n, [P, 4, T]) for n in ("sq", "xs", "t", "y"))
        ps = f.ps("ps", [P, 2, 2, 512])
        mean, centred, squared, var, root, newton, done = (
            f.sem(n) for n in ("mean", "centred", "squared", "var", "root", "newton", "done"))
        read = f.sem("read")
        block = f.block()

        @block.tensor
        def _(pe):
            for m in range(4):
                if m >= 2:
                    pe.wait_ge(centred, m - 1)
                for b in range(nb):
                    mm = pe.matmul(ps[:, m % 2, b, 0:nt], c.ones_head[:, :], o[:, m, b * nt:(b + 1) * nt],
                                   start=True, stop=True)
                mm.then_inc(mean, 1)
            for m in range(4):
                pe.wait_ge(squared, m + 1)
                if m >= 2:
                    pe.wait_ge(read, m - 1)
                else:
                    pe.wait_ge(centred, 3 + m)
                for b in range(nb):
                    mm = pe.matmul(ps[:, m % 2, b, 0:nt], c.ones_head[:, :], sq[:, m, b * nt:(b + 1) * nt],
                                   start=True, stop=True)
                mm.then_inc(var, 1)

        @block.scalar
        def _(act):
            for m in range(4):
                act.wait_ge(centred, m + 1)
                act.activation(sq[:, m], o[:, m], ACT.Square).then_inc(squared, 1)
            rsqrt_act(act, c, xs[:, :, :], t[:, :, :], y[:, :, :], root, 0, read, 4)

        @block.vector
        def _(dve):
            for m in range(4):
                dve.wait_ge(mean, m + 1)
                dve.scalar_tensor_tensor(two(o[:, m], T), ps[:, m % 2, 0:nb, 0:nt], -1.0 / 64, two(o[:, m], T),
                                         ALU.mult, ALU.add).then_inc(centred, 1)
            for m in range(4):
                dve.wait_ge(var, m + 1)
                dve.tensor_scalar(two(xs[:, m], T), ps[:, m % 2, 0:nb, 0:nt], 1.0 / 64, GN_EPS, ALU.mult,
                                  ALU.add).then_inc(read, 1)
            dve.wait_ge(read, 4)
            rsqrt_dve(dve, xs[:, :, :], t[:, :, :], y[:, :, :], root, 0, newton, 0)
            for m in range(4):
                dve.scalar_tensor_tensor(o[:, m], o[:, m], vec(c, "ln_g", m), y[:, m], ALU.mult,
                                         ALU.mult).then_inc(done, 1)
            for m in range(4):
                dve.wait_ge(done, m + 1)
                dve.scalar_tensor_tensor(o[:, m], o[:, m], vec(c, "ln_b", m), ar[:, m], ALU.add,
                                         ALU.add).then_inc(done, 1)
            dve.wait_ge(done, 8)
            dve.tensor_tensor(o[:, 0:4, :], o[:, 0:4, :], ar[:, X_G, :], ALU.mult)




def split_phase(nc, c, tag, src, hi, lo):
    tiles = len(src)
    with Phase(nc, tag) as f:
        hi_done, lo_done = f.sem("hi_done"), f.sem("lo_done")
        block = f.block()

        @block.scalar
        def _(act):
            for k in range(tiles):
                act.activation(hi[:, k], src[k], ACT.Copy).then_inc(hi_done, 1)

        @block.vector
        def _(dve):
            for k in range(0, tiles, 2):
                dve.wait_ge(hi_done, k + 1)
                dve.tensor_tensor(lo[:, k], src[k], hi[:, k].bitcast(F32), ALU.subtract)

        @block.gpsimd
        def _(pool):
            for k in range(1, tiles, 2):
                pool.wait_ge(hi_done, k + 1)
                pool.tensor_tensor(lo[:, k], src[k], hi[:, k].bitcast(F32), ALU.subtract)


def merge_phase(nc, c, tag, T, o_hi, o_lo, merged):
    def epilogue(f, sum_free, acc):
        th, pr = f.sb("th", [P, 2, T]), f.sb("pr", [P, T])
        tan, added = f.sem("tan"), f.sem("added")

        def act(eng, i, a):
            if a % 2:
                return
            n = 3 * i + a // 2
            eng.activation(two(th[:, 0], T), acc(a), ACT.Tanh, scale=0.5).then_inc(tan, 1)
            eng.wait_ge(tan, n + 1)
            if not (isinstance(n, int) and n == 0):
                eng.wait_ge(sum_free[1], n)
            eng.activation(th[:, 1], th[:, 0], ACT.Copy, scale=0.5, bias=0.5).then_inc(sum_free[0], 1)

        def dve(eng, i, a, first):
            if a % 2 == 0:
                return
            n = 3 * i + a // 2
            eng.wait_ge(sum_free[0], n + 1)
            dst = at(merged, i)
            out = dst if a == 1 else pr[:, :]
            if a == 3 and not first:
                eng.wait_ge(added, 2 * i)
            if a == 5:
                eng.wait_ge(added, 2 * i + 1)
            eng.tensor_tensor(two(out, T), acc(a), two(th[:, 1], T), ALU.mult).then_inc(sum_free[1], 1)
            if a > 1:
                eng.wait_ge(sum_free[1], n + 1)
                eng.tensor_tensor(dst, dst, pr[:, :], ALU.add).then_inc(added, 1)
        return {"act": act, "dve": dve}

    body = []
    for n in range(3):
        body.append(((n, c.a["w_gate"]), DT, c.x_hi, c.x_lo, True, True))
        body.append(((n, c.a["w_branch"]), 4, o_hi[:, 4 * n:4 * n + 4, :], o_lo[:, 4 * n:4 * n + 4, :], True, True))
    dense_phase(nc, c, tag, T, DT, body, epilogue, slots=3, act_lag=2)


def add_phase(nc, c, tag, T, steps, body, base, load=None, store=None):
    def epilogue(f, sum_free, acc):
        if load is not None:
            base_in = f.sem("base_in")

            def load_base(sp):
                sp.dma_start(base[:, :, :], load).then_inc(base_in, 16)

        def dve(eng, i, a, first):
            if load is not None and first and a == 0:
                eng.wait_ge(base_in, 16)
            m = 2 * i + a
            ins = eng.tensor_tensor(two(at(base, m), T), acc(a), two(at(base, m), T), ALU.add)
            ins.then_inc(sum_free[a], 1)
        return {"dve": dve, **({"load": load_base} if load is not None else {})}

    def store_step(sp, i):
        if isinstance(i, int):
            return sp.dma_start(store[:, 2 * i:2 * i + 2, :], base[:, 2 * i:2 * i + 2, :])
        return sp.dma_start(store[:, bass.ds(2 * i, 2), :], base[:, bass.ds(2 * i, 2), :])

    dense_phase(nc, c, tag, T, steps, body, epilogue, store=store_step if store is not None else None)


def up_phase(nc, c, tag, g, T, h_hi, h_lo):
    def epilogue(f, sum_free, acc):
        a_raw, cv, gl = f.sb("a_raw", [P, T + 2]), f.sb("cv", [P, T]), f.sb("gl", [P, T])
        h = f.sb("h", [P, T])
        a_in, conv, gelu, hi_done, lo_done = (f.sem(n) for n in ("a_in", "conv", "gelu", "h_hi_done", "h_lo_done"))
        h_done = sum_free[1]
        ws = f.sb("ws", [P, 4])
        if g == 1:
            fix = f.sb("fix", [P, 4])
        per = 4 if g == 0 else 7
        cw, cb, cs = VEC["conv_w"][0], VEC["conv_b"][0], VEC["conv_s"][0]

        def col(tensor, i, n=1):
            return tensor[:, i:i + n] if isinstance(i, int) else tensor[:, bass.ds(i, n)]

        def act(eng, i, a):
            if a == 0:
                eng.wait_ge(conv, per * i + per)
                if not (isinstance(i, int) and i == 0):
                    eng.wait_ge(h_done, i)
                eng.activation(gl[:, :], cv[:, :], ACT.Gelu_apprx_tanh).then_inc(gelu, 1)
            else:
                eng.wait_ge(h_done, i + 1)
                eng.activation(at(h_hi, i), h[:, :], ACT.Copy).then_inc(hi_done, 1)

        def dve(eng, i, a, first):
            if a == 0:
                copy(eng, a_raw[:, 0:2], col(c.conv_carry, 2 * i, 2)).then_inc(a_in, 1)
                eng.tensor_copy(two(a_raw[:, 2:T + 2], T), acc(0)).then_inc(sum_free[0], 1)
                eng.tensor_copy(ws[:, 0:3], col(c.vecs, cw + 3 * i, 3))
                eng.tensor_copy(ws[:, 3:4], col(c.vecs, cb + i)).then_inc(a_in, 1)
                eng.wait_ge(sum_free[0], i + 1)
                eng.wait_ge(a_in, 2 * i + 2)
                if not first:
                    eng.wait_ge(gelu, i)
                eng.tensor_scalar(cv[:, :], a_raw[:, 2:T + 2], ws[:, 2:3], ws[:, 3:4], ALU.mult,
                                  ALU.add).then_inc(conv, 1)
                eng.wait_ge(conv, per * i + 1)
                eng.scalar_tensor_tensor(cv[:, :], a_raw[:, 1:T + 1], ws[:, 1:2], cv[:, :], ALU.mult,
                                         ALU.add).then_inc(conv, 1)
                eng.wait_ge(conv, per * i + 2)
                eng.scalar_tensor_tensor(cv[:, :], a_raw[:, 0:T], ws[:, 0:1], cv[:, :], ALU.mult,
                                         ALU.add).then_inc(conv, 1)
                eng.wait_ge(conv, per * i + 3)
                if g == 0:
                    copy(eng, col(c.conv_carry, 2 * i, 2), a_raw[:, T:T + 2]).then_inc(conv, 1)
                    return
                e0 = PROMPT_END
                copy(eng, fix[:, 0:2], col(c.vecs, cs + 2 * i, 2))
                eng.tensor_copy(fix[:, 2:4], a_raw[:, 2 + e0:4 + e0])
                copy(eng, col(c.conv_carry, 2 * i, 2), a_raw[:, e0:e0 + 2])
                eng.tensor_copy(col(c.conv_last, 2 * i, 2), a_raw[:, T:T + 2]).then_inc(conv, 1)
                eng.wait_ge(conv, per * i + 4)
                eng.tensor_scalar(cv[:, e0:e0 + 2], fix[:, 2:4], ws[:, 2:3], ws[:, 3:4], ALU.mult,
                                  ALU.add).then_inc(conv, 1)
                eng.wait_ge(conv, per * i + 5)
                eng.scalar_tensor_tensor(cv[:, e0:e0 + 2], fix[:, 1:3], ws[:, 1:2], cv[:, e0:e0 + 2], ALU.mult,
                                         ALU.add).then_inc(conv, 1)
                eng.wait_ge(conv, per * i + 6)
                eng.scalar_tensor_tensor(cv[:, e0:e0 + 2], fix[:, 0:2], ws[:, 0:1], cv[:, e0:e0 + 2], ALU.mult,
                                         ALU.add).then_inc(conv, 1)
            else:
                eng.wait_ge(gelu, i + 1)
                if not first:
                    eng.wait_ge(lo_done, i)
                eng.tensor_tensor(two(h[:, :], T), acc(1), two(gl[:, :], T), ALU.mult).then_inc(h_done, 1)
                eng.wait_ge(hi_done, i + 1)
                eng.tensor_tensor(at(h_lo, i), h[:, :], at(h_hi, i).bitcast(F32), ALU.subtract).then_inc(lo_done, 1)
        return {"act": act, "dve": dve}

    body = [((s, c.a["w_up"]), DT, c.x_hi, c.x_lo, True, True) for s in range(2)]
    dense_phase(nc, c, tag, T, FT, body, epilogue, act_lag=2)




class Consts:
    pass


def build(nc, a):
    c = Consts()
    c.a = a
    with Phase(nc, "k") as k:
        c.vecs = k.sb("vecs", [P, N_VEC])
        c.ident, c.ones, c.ones_head = k.sb("ident", [P, P]), k.sb("ones", [P, P]), k.sb("ones_head", [P, P])
        c.lora = k.sb("lora", [P, 2, 512])
        c.masks = k.sb("masks", [P, 9, P])
        c.state, c.state_in, c.state_out = (k.sb(n, [P, 4, CHUNK]) for n in ("state", "state_in", "state_out"))
        c.kv_carry = k.sb("kv_carry", [P, 2, WINDOW])
        c.shift_carry, c.shift_out = k.sb("shift_carry", [P, 14]), k.sb("shift_out", [P, 2, 14])
        c.conv_carry, c.conv_last = k.sb("conv_carry", [P, 2 * FT]), k.sb("conv_last", [P, 2 * FT])

        with Phase(nc, "start") as f:
            in_sem, zero = f.sem("in"), f.sem("zero")
            block = f.block()

            @block.sync
            def _(sp):
                for n, (dst, src) in enumerate((
                        (c.vecs[:, :], a["vecs"]), (c.ident[:, :], a["ident"]), (c.ones[:, :], a["ones"]),
                        (c.ones_head[:, :], a["ones_head"]), (c.lora[:, :, :], a["lora"]),
                        (c.masks[:, :, :], a["masks"]), (c.state_in[:, :, :], a["state"]))):
                    sp.dma_start(dst, src).then_inc(in_sem, 16)
                sp.wait_ge(in_sem, 16 * 7)

            @block.vector
            def _(dve):
                dve.memset(c.state[:, :, :], 0.0)
                dve.memset(c.conv_carry[:, :], 0.0)

        memory_phase(nc, c)
        for g, (start, T) in enumerate(GROUPS):
            group(nc, c, g, start, T)

        with Phase(nc, "end") as f:
            out = f.sem("out")
            block = f.block()

            @block.sync
            def _(sp):
                sp.dma_start(a["o_cp"], c.conv_carry[:, :]).then_inc(out, 16)
                sp.dma_start(a["o_cs"], c.conv_last[:, :]).then_inc(out, 16)
                sp.wait_ge(out, 32)


def load(nc, tag, dst, src):
    with Phase(nc, tag) as f:
        in_sem = f.sem("in")
        block = f.block()

        @block.sync
        def _(sp):
            sp.dma_start(dst, src).then_inc(in_sem, 16)
            sp.wait_ge(in_sem, 16)


def group(nc, c, g, start, T):
    a, t = c.a, f"g{g}"
    x_src = a["xT"][:, :, start:start + T]
    with Phase(nc, t) as k:
        c.x_hi, c.x_lo = k.sb("x_hi", [P, DT, T], F32R), k.sb("x_lo", [P, DT, T], F32R)
        with Phase(nc, t + "o") as ko:
            o_a = ko.sb("o_a", [P, 4, T])
            with Phase(nc, t + "x") as kx:
                x = kx.sb("x", [P, DT, T])
                load(nc, t + "ld", x[:, :, :], x_src)
                norm_phase(nc, c, t + "n1", T, x, "norm1_g", c.x_hi, c.x_lo)
            with Phase(nc, t + "r") as kr:
                ar = kr.sb("ar", [P, 32, T])
                project_phase(nc, c, t + "pr", T, R_TILES, a["w_rwkv"], 0, ar, 0)
                rwkv_prep(nc, c, t + "rp", g, T, ar)
                rwkv_scan(nc, c, t + "rs", g, T, ar, o_a)
                rwkv_post(nc, c, t + "rq", T, ar, o_a)
            o_bm = ko.sb("o_bm", [P, 8, T])
            with Phase(nc, t + "a") as ka:
                pa = ka.sb("pa", [P, A_TILES, T])
                width = WINDOW + T if g == 0 else 2 * WINDOW + T
                kw, vw = ka.sb("kw", [P, width]), ka.sb("vw", [P, width])
                project_phase(nc, c, t + "pa", T, A_TILES, a["w_attn"], 0, pa, 0)
                attention_prep(nc, c, t + "ap", g, T, pa, kw, vw)
                attention_phase(nc, c, t + "at", g, T, pa, kw, vw, o_bm)
            with Phase(nc, t + "m") as km:
                merged = km.sb("merged", [P, DT, T])
                with Phase(nc, t + "s") as ks:
                    o_hi, o_lo = ks.sb("o_hi", [P, 12, T], F32R), ks.sb("o_lo", [P, 12, T], F32R)
                    parts = [o_a[:, k] for k in range(4)] + [o_bm[:, k] for k in range(8)]
                    split_phase(nc, c, t + "so", parts, o_hi, o_lo)
                    merge_phase(nc, c, t + "mg", T, o_hi, o_lo, merged)
                split_phase(nc, c, t + "sm", [merged[:, k] for k in range(DT)], c.x_hi, c.x_lo)
        with Phase(nc, t + "y") as ky:
            x1 = ky.sb("x1", [P, DT, T])
            body = [((s, a["w_out"]), DT, c.x_hi, c.x_lo, True, True) for s in range(2)]
            add_phase(nc, c, t + "wo", T, DT // 2, body, x1, load=x_src)
            norm_phase(nc, c, t + "n2", T, x1, "norm2_g", c.x_hi, c.x_lo)
            h_hi, h_lo = ky.sb("h_hi", [P, FT, T], F32R), ky.sb("h_lo", [P, FT, T], F32R)
            up_phase(nc, c, t + "up", g, T, h_hi, h_lo)
            half = FT // 2
            body = []
            for s in range(4):
                k0 = (s % 2) * half
                body.append(((s, a["w_down"]), half, h_hi[:, k0:k0 + half, :], h_lo[:, k0:k0 + half, :],
                             s % 2 == 0, s % 2 == 1))

            add_phase(nc, c, t + "wd", T, DT // 2, body, x1, store=a["o_y"][:, :, start:start + T])




def tiles(w):
    k, m = w.shape
    return np.ascontiguousarray(w.reshape(k // P, P, m // P, P).transpose(2, 1, 0, 3).reshape(m // P, P, k))


def columns(v):
    return v.reshape(-1, P).T


def constants():
    i = np.arange(P)
    ident = np.eye(P, dtype=np.float32)
    head = (i[:, None] // 64 == i[None, :] // 64).astype(np.float32)
    r, q = i % 64, np.arange(P)
    masks = np.zeros((P, 9, P), np.float32)
    same = r[:, None] // 16 == q[None, :] // 16
    masks[:, LOW] = same & (r[:, None] > q[None, :])
    masks[:, LOW_T] = same & (r[:, None] < q[None, :])
    masks[:, EYE] = r[:, None] == q[None, :]
    masks[:, OFF] = (r[:, None] // 16 > q[None, :] // 16)
    masks[:, UP, 0:64] = r[:, None] < q[None, 0:64]
    masks[:, UP, 64:128] = r[:, None] <= q[None, 0:64]
    q64 = q % 64
    masks[:, BD] = head
    masks[:, BD_LOW] = head * (r[:, None] // 16 == q64[None, :] // 16) * (r[:, None] > q64[None, :])
    masks[:, BD_LOW_T] = head * (r[:, None] // 16 == q64[None, :] // 16) * (r[:, None] < q64[None, :])
    masks[:, BD_UP] = head * (r[:, None] < q64[None, :])
    slopes = np.exp2(-8.0 * np.arange(1, 9, dtype=np.float32) / 8).astype(np.float32)
    dist = np.abs(WINDOW + np.arange(64)[:, None] - np.arange(KEYS)[None, :]).astype(np.float32)
    alibi = np.zeros((P, 3, 4, KEYS), np.float32)
    for v in range(3):
        for j in range(4):
            for e in range(2):
                t = -slopes[j + 4 * e] * dist
                t = np.where(np.arange(KEYS)[None, :] < WINDOW - CHUNK * v, np.float32(-1e30), t)
                alibi[64 * e:64 * e + 64, v, j] = t
    return {"ident": ident, "ones": np.ones((P, P), np.float32), "ones_head": head, "masks": masks, "alibi": alibi}


def lay_out(x):
    f32 = np.float32
    w_in = np.asarray(x["w_in"][0])
    rw = w_in[:, 0:1792]
    order = [slice(1536, 1664), slice(1664, 1792), slice(0, 512), slice(512, 1024), slice(1024, 1536)]
    reorder = lambda v: np.concatenate([v[..., s] for s in order], - 1)
    heads = [h for j in range(4) for h in (j, j + 4)]
    q = w_in[:, 1792:2304].reshape(D, 8, 64)[:, heads].reshape(D, 512)
    attn = np.concatenate([q, w_in[:, 2304:3072]], 1)
    gates = w_in[:, 3072:].reshape(D, 3, DT, P).transpose(0, 2, 1, 3).reshape(D, 3 * D)
    branch = np.asarray(x["w_branch"][0]).copy()
    branch[1] = branch[1].reshape(8, 64, D)[heads].reshape(512, D)
    branch = np.stack([tiles(b) for b in branch], 1).reshape(3 * DT, P, 512)
    up = np.asarray(x["w_up"][0]).reshape(D, 2, FT, P).transpose(0, 2, 1, 3).reshape(D, 2 * FF)
    down = tiles(np.asarray(x["w_down"][0])).reshape(DT, P, 2, FF // 2).transpose(0, 2, 1, 3).reshape(2 * DT, P, FF // 2)
    mem_kv = np.asarray(x["w_mem_kv"][0])
    both = lambda v: np.tile(v, 2)[:, None]
    sink = np.asarray(x["swa_sink"][0])
    sinks = np.concatenate([np.tile(sink[4 * e:4 * e + 4][None], (64, 1)) for e in range(2)], 0)
    conv_w = np.asarray(x["conv_w"][0]).reshape(3, FT, P).transpose(2, 1, 0).reshape(P, 3 * FT)
    conv_s = np.asarray(x["state_conv"][0, 0]).reshape(2, FT, P).transpose(2, 1, 0).reshape(P, 2 * FT)
    one = lambda n: columns(np.asarray(x[n][0]).reshape(-1))
    vecs = np.concatenate([
        one("norm1_g"), one("norm2_g"), one("mem_norm_g"), columns(reorder(np.asarray(x["rwkv_mu"][0]))),
        one("rwkv_w0"), one("rwkv_a0"), one("rwkv_kk"), one("rwkv_ka"), one("rwkv_rk"), one("rwkv_ln_g"),
        one("rwkv_ln_b"), both(np.asarray(x["swa_qn_g"][0])), both(np.asarray(x["swa_kn_g"][0])),
        one("mem_qn_g"), one("mem_kn_g"), sinks, conv_w, one("conv_b"),
        columns(reorder(np.asarray(x["state_shift"][0, 0, 0]))), conv_s,
        np.full((P, 1), 0.5 * np.log(LN_SCALE), f32)], 1)
    assert vecs.shape == (P, N_VEC)
    fm = lambda v: v.reshape(-1, DT, P).transpose(2, 1, 0)
    tokens = np.concatenate([np.asarray(x["x_prompt"][0]), np.asarray(x["x_sample"][0])], 0)
    lora = np.stack([np.concatenate([np.asarray(x["rwkv_w2"][0]), np.asarray(x["rwkv_a2"][0])], 0),
                     np.asarray(x["rwkv_g2"][0])], 1)
    out = {
        "xT": fm(tokens), "memT": fm(np.asarray(x["mem_prompt"][0])), "vecs": vecs, "lora": lora,
        "w_attn": tiles(attn), "w_rwkv": tiles(reorder(rw)), "w_gate": tiles(gates), "w_branch": branch,
        "w_out": tiles(np.asarray(x["w_out"][0])), "w_up": tiles(up), "w_down": down,
        "w_mk": tiles(mem_kv[:, 0:512]), "w_mv": mem_kv[:, 512:].reshape(DT, P, 512).transpose(1, 0, 2),
        "cache_k": np.asarray(x["cache_swa_k"][0, 0]).reshape(WINDOW, P).T,
        "cache_v": np.asarray(x["cache_swa_v"][0, 0]).reshape(WINDOW, P).T,
        "cache_mk": np.asarray(x["cache_mem_k"][0, 0]).transpose(2, 1, 0),
        "cache_mv": np.asarray(x["cache_mem_v"][0, 0]).reshape(2, P, 512).transpose(1, 0, 2),
        "state": np.asarray(x["state_rwkv"][0, 0]).reshape(4, 2, 64, 64).transpose(1, 3, 0, 2).reshape(P, 4, 64),
    }
    out.update(constants())
    return {n: np.ascontiguousarray(v) for n, v in out.items()}


OUTS = {
    "o_y": (P, DT, SEQ + DEC), "o_mk": (P, 4, MEM), "o_mv": (P, 2, 512), "o_kp": (P, WINDOW), "o_vp": (P, WINDOW),
    "o_ks": (P, WINDOW), "o_vs": (P, WINDOW), "o_rp": (P, 4, 64), "o_rs": (P, 4, 64), "o_shp": (P, 14),
    "o_shs": (P, 14), "o_cp": (P, 2 * FT), "o_cs": (P, 2 * FT),
}


def kernel(**inputs):
    import concourse.bacc as _bacc
    from concourse.bass_utils import run_bass_kernel_spmd as _run

    nc = _bacc.Bacc("TRN2", target_bir_lowering=False, num_devices=1)
    arrays = lay_out(inputs)
    a = {n: nc.dram_tensor(n, v.shape, mybir.dt.from_np(v.dtype), kind="ExternalInput").ap() for n, v in arrays.items()}
    for n, s in OUTS.items():
        a[n] = nc.dram_tensor(n, s, F32, kind="ExternalOutput").ap()
    build(nc, a)
    r = _run(nc, [arrays], core_ids=[0]).results[0]

    y = r["o_y"].transpose(2, 1, 0).reshape(SEQ + DEC, D)
    kv = lambda v: np.ascontiguousarray(v.T).reshape(1, 1, WINDOW, 2, 64)
    state = lambda v: v.reshape(2, 64, 4, 64).transpose(2, 0, 3, 1).reshape(1, 1, 8, 64, 64)

    def shift(v):
        flat = v.T.reshape(1792)
        return np.concatenate([flat[256:], flat[0:256]]).reshape(1, 1, 1, 1792)

    conv = lambda v: v.reshape(P, FT, 2).transpose(2, 1, 0).reshape(1, 1, 2, FF)
    return (y[None, 0:SEQ], y[None, SEQ:],
            kv(r["o_kp"]), kv(r["o_vp"]),
            r["o_mk"].transpose(2, 1, 0).reshape(1, 1, MEM, 4, P),
            r["o_mv"].transpose(1, 0, 2).reshape(1, 1, MEM, 4, P),
            state(r["o_rp"]), shift(r["o_shp"]), conv(r["o_cp"]),
            kv(r["o_ks"]), kv(r["o_vs"]), state(r["o_rs"]), shift(r["o_shs"]), conv(r["o_cs"]))
```

```python
from contextlib import ExitStack

import numpy as np

import concourse.bass as bass
from concourse import mybir

F32 = mybir.dt.float32
F32R = mybir.dt.float32r
ACT = mybir.ActivationFunctionType
ALU = mybir.AluOpType
AX = mybir.AxisListType

P = 128
D = 1024
DT = D // P
SEQ, DEC = 1024, 64
CHUNK = 64
WINDOW = 128
KEYS = WINDOW + CHUNK
FF = 2816
FT = FF // P
MEM = 256
R_TILES = 14
A_TILES = 10
GROUPS = ((0, 576), (576, 512))
PROMPT_END = SEQ - GROUPS[1][0]
RMS_EPS = 1e-6
GN_EPS = 64e-5
DECAY = float(np.exp(-0.5))
LN_SCALE = 2.0 ** 20
RING = 4

VEC = {}
_at = 0
for _name, _n in (("norm1_g", 8), ("norm2_g", 8), ("mem_g", 8), ("mu", 14), ("w0", 4), ("a0", 4), ("kk", 4),
                  ("ka", 4), ("rk", 4), ("ln_g", 4), ("ln_b", 4), ("qn", 1), ("kn", 1), ("mqn", 1), ("mkn", 1),
                  ("sink", 4), ("conv_w", 3 * FT), ("conv_b", FT), ("shift", 14), ("conv_s", 2 * FT),
                  ("log_half_scale", 1)):
    VEC[_name] = (_at, _at + _n)
    _at += _n
N_VEC = _at


def loop(eng, start, end, body):
    body(start, True)
    if end - start > 1:
        with eng.Fori(start + 1, end) as i:
            body(i, False)


def at(tensor, i):
    if isinstance(i, int):
        return tensor[:, i]
    return tensor[:, bass.ds(i, 1)].rearrange("p a t -> p (a t)")


def cols(tensor, tiles, start, n):
    if isinstance(start, int):
        return tensor[:, tiles, start:start + n]
    return tensor[:, tiles, bass.ds(start, n)]


def copy(eng, dst, src):
    return eng.tensor_scalar(dst, src, 1.0, None, ALU.mult)


class Phase:

    def __init__(self, nc, tag):
        self.nc, self.tag, self.stack, self.sems = nc, tag, ExitStack(), []

    def __enter__(self):
        self.stack.__enter__()
        return self

    def __exit__(self, *exc):
        out = self.stack.__exit__(*exc)
        for sem in self.sems:
            self.nc.gpsimd.sem_clear(sem)
        return out

    def sb(self, name, shape, dtype=F32):
        return self.stack.enter_context(self.nc.sbuf_tensor(f"{self.tag}_{name}", shape, dtype))

    def ps(self, name, shape):
        return self.stack.enter_context(self.nc.psum_tensor(f"{self.tag}_{name}", shape, F32))

    def sem(self, name):
        self.sems.append(self.stack.enter_context(self.nc.semaphore(f"{self.tag}_{name}")))
        return self.sems[-1]

    def block(self):
        return self.stack.enter_context(self.nc.Block())


def pieces(T):
    n = -(-T // 512)
    return n, T // n


def two(ap, T):
    return ap.rearrange("p (n t) -> p n t", n=pieces(T)[0])


def vec(c, name, i=0, n=1):
    a = VEC[name][0] + i
    return c.vecs[:, a:a + n]


def first_two(w):
    return [w[0], w[1]]


def load_ahead(sp, c, weights, loaded):
    for s, w in enumerate(weights):
        sp.dma_start(c.raw[s][:, 0:w.shape[-1]], w).then_inc(loaded, 16)
    sp.wait_ge(loaded, 32)




def norm_phase(nc, c, tag, T, x, gain, hi, lo, w_next, src=None):
    nb, nt = pieces(T)
    with Phase(nc, tag) as f:
        sq, total = f.sb("sq", [P, DT, T]), f.sb("total", [P, T])
        xs, y, t = f.sb("xs", [P, T]), f.sb("y", [P, T]), f.sb("t", [P, T])
        xn = f.sb("xn", [P, RING, T])
        ps = f.ps("ps", [P, nb, 512])
        squared, added, mean = f.sem("squared"), f.sem("added"), f.sem("mean")
        root, newton = f.sem("root"), f.sem("newton")
        normed, hi_done = f.sem("normed"), f.sem("hi_done")
        lo_done = [f.sem("lo_even"), f.sem("lo_odd")]
        loaded, ahead = [f.sem(f"loaded{k}") for k in range(0, DT, 2)], f.sem("ahead")
        block = f.block()

        @block.sync
        def _(sp):
            if src is not None:
                for k in range(0, DT, 2):
                    sp.dma_start(x[:, k:k + 2, :], src[:, k:k + 2, :]).then_inc(loaded[k // 2], 16)
            load_ahead(sp, c, w_next, ahead)

        @block.scalar
        def _(act):
            for k in range(DT):
                if src is not None and k % 2 == 0:
                    act.wait_ge(loaded[k // 2], 16)
                act.activation(sq[:, k], x[:, k], ACT.Square).then_inc(squared, 1)
            act.wait_ge(newton, 1)
            act.activation(t[:, :], xs[:, :], ACT.Ln).then_inc(root, 1)
            act.wait_ge(root, 1)
            act.activation(y[:, :], t[:, :], ACT.Exp, scale=-0.5).then_inc(root, 1)
            for k in range(DT):
                act.wait_ge(normed, k + 1)
                act.activation(hi[:, k], xn[:, k % RING], ACT.Copy).then_inc(hi_done, 1)

        @block.tensor
        def _(pe):
            pe.wait_ge(added, DT - 1)
            for n in range(nb):
                mm = pe.matmul(ps[:, n, 0:nt], c.ones[:, :], total[:, n * nt:(n + 1) * nt], start=True, stop=True)
            mm.then_inc(mean, 1)

        @block.vector
        def _(dve):
            dve.wait_ge(squared, 2)
            dve.tensor_tensor(total[:, :], sq[:, 0], sq[:, 1], ALU.add).then_inc(added, 1)
            for k in range(2, DT - 1):
                dve.wait_ge(squared, k + 1)
                dve.wait_ge(added, k - 1)
                dve.tensor_tensor(total[:, :], total[:, :], sq[:, k], ALU.add).then_inc(added, 1)
            dve.wait_ge(added, DT - 2)
            dve.wait_ge(squared, DT)
            dve.tensor_tensor(total[:, :], total[:, :], sq[:, DT - 1], ALU.add).then_inc(added, 1)
            dve.wait_ge(mean, 1)
            dve.tensor_scalar(two(xs[:, :], T), ps[:, :, 0:nt], 1.0 / D, RMS_EPS, ALU.mult, ALU.add).then_inc(newton, 1)
            dve.wait_ge(root, 2)
            dve.wait_ge(newton, 1)
            dve.tensor_tensor(t[:, :], xs[:, :], y[:, :], ALU.mult).then_inc(newton, 1)
            dve.wait_ge(newton, 2)
            dve.scalar_tensor_tensor(t[:, :], t[:, :], -0.5, y[:, :], ALU.mult, ALU.mult).then_inc(newton, 1)
            dve.wait_ge(newton, 3)
            dve.scalar_tensor_tensor(y[:, :], t[:, :], 1.5, y[:, :], ALU.add, ALU.mult).then_inc(newton, 1)
            dve.wait_ge(newton, 4)
            for k in range(DT + 2):
                if k < DT:
                    if k >= RING:
                        dve.wait_ge(lo_done[k % 2], (k - RING) // 2 + 1)
                    dve.scalar_tensor_tensor(xn[:, k % RING], x[:, k], vec(c, gain, k), y[:, :],
                                             ALU.mult, ALU.mult).then_inc(normed, 1)
                j = k - 2
                if j > 0 and j % 2:
                    dve.wait_ge(hi_done, j + 1)
                    dve.tensor_tensor(lo[:, j], xn[:, j % RING], hi[:, j].bitcast(F32),
                                      ALU.subtract).then_inc(lo_done[1], 1)

        @block.gpsimd
        def _(pool):
            for k in range(0, DT, 2):
                pool.wait_ge(hi_done, k + 1)
                pool.tensor_tensor(lo[:, k], xn[:, k % RING], hi[:, k].bitcast(F32),
                                   ALU.subtract).then_inc(lo_done[0], 1)




def dense_phase(nc, c, tag, T, steps, body, epilogue, slots=2, act_lag=1, store=None, w_next=None):
    nb, nt = pieces(T)
    n_w = len(body)
    n_sum = sum(b[5] for b in body)
    assert n_w % slots == 0 and n_sum % 2 == 0 and act_lag <= n_w
    with Phase(nc, tag) as f:
        slot_k = [max(b[1] for b in body[s::slots]) for s in range(slots)]
        raw = c.raw + [f.sb(f"raw{s}", [P, slot_k[s] * P]) for s in range(2, slots)]
        done_before = [int(s < 2) for s in range(slots)]
        w_hi = [f.sb(f"w_hi{s}", [P, k * P], F32R) for s, k in enumerate(slot_k)]
        w_lo = [f.sb(f"w_lo{s}", [P, k * P], F32R) for s, k in enumerate(slot_k)]
        sums = f.ps("sums", [P, 2, 2, 512])
        loaded = [f.sem(f"loaded{s}") for s in range(slots)]
        stored, ahead = f.sem("stored") if store else None, f.sem("ahead") if w_next else None
        hi_done, lo_done, w_used = f.sem("hi_done"), f.sem("lo_done"), f.sem("w_used")
        sum_free = [f.sem(f"sum_free{s}") for s in range(2)]
        work = epilogue(f, sum_free, lambda a: sums[:, a % 2, 0:nb, 0:nt])
        sum_of, last_tile, a = [], [], 0
        for n, b in enumerate(body):
            sum_of.append(a)
            if b[5]:
                last_tile.append(n)
            a += b[5]
        block = f.block()

        def wait_sum(eng, i, a):
            eng.wait_ge(w_used, n_w * i + last_tile[a] + 1)

        @block.sync
        def _(sp):
            stride = [sum(1 for o in body if o[0][1] is b[0][1]) for b in body]

            def results(i):
                for h in range(2):
                    sp.wait_ge(sum_free[h], (n_sum // 2) * (i + 1))
                store(sp, i).then_inc(stored, 16)

            def step(i, first):
                for b, ((index, w), kt, *_) in enumerate(body):
                    if not (first and b < slots):
                        sp.wait_ge(lo_done, n_w * i + b - slots + 1)
                    src = w[index] if first else w[bass.ds(index + i * stride[b], 1)].rearrange("a p m -> p (a m)")
                    if not (first and b < slots and done_before[b]):
                        sp.dma_start(raw[b % slots][:, 0:kt * P], src).then_inc(loaded[b % slots], 16)
                    if first and b == slots - 1 and "load" in work:
                        work["load"](sp)
                if store and not first:
                    results(i - 1)

            loop(sp, 0, steps, step)
            if w_next:
                sp.wait_ge(lo_done, n_w * steps)
                load_ahead(sp, c, w_next, ahead)
            if store:
                results(steps - 1)
                sp.wait_ge(stored, 16 * steps)

        @block.scalar
        def _(act):
            ended = []
            for b in range(n_w):
                t = (b - act_lag) % n_w
                ended.append((sum_of[t], b < act_lag) if body[t][5] else None)

            def rest(i, b):
                a, last_step = ended[b]
                j = i - 1 if last_step else i
                wait_sum(act, j, a)
                work["act"](act, j, a)

            def step(i, first):
                for b, (_, kt, *_) in enumerate(body):
                    if not (first and b < slots and done_before[b]):
                        act.wait_ge(loaded[b % slots],
                                    16 * ((n_w // slots) * i + b // slots + 1 - done_before[b % slots]))
                    if not (first and b < slots):
                        act.wait_ge(w_used, n_w * i + b - slots + 1)
                    act.activation(w_hi[b % slots][:, 0:kt * P], raw[b % slots][:, 0:kt * P],
                                   ACT.Copy).then_inc(hi_done, 1)
                    if "act" in work and ended[b] and not (first and ended[b][1]):
                        rest(i, b)

            loop(act, 0, steps, step)
            if "act" in work:
                for b in range(n_w):
                    if ended[b] and ended[b][1]:
                        rest(steps, b)

        @block.gpsimd
        def _(pool):
            def step(i, first):
                for b, (_, kt, *_) in enumerate(body):
                    pool.wait_ge(hi_done, n_w * i + b + 1)
                    pool.tensor_tensor(w_lo[b % slots][:, 0:kt * P], raw[b % slots][:, 0:kt * P],
                                       w_hi[b % slots][:, 0:kt * P].bitcast(F32), ALU.subtract).then_inc(lo_done, 1)

            loop(pool, 0, steps, step)

        @block.tensor
        def _(pe):
            def step(i, first):
                for b, (_, kt, x_hi, x_lo, begins, ends) in enumerate(body):
                    a = sum_of[b]
                    pe.wait_ge(lo_done, n_w * i + b + 1)
                    if begins and not (first and a < 2):
                        pe.wait_ge(sum_free[a % 2], (n_sum // 2) * i + a // 2)
                    for n in range(nb):
                        out = sums[:, a % 2, n, 0:nt]
                        for k in range(kt):
                            wh = w_hi[b % slots][:, k * P:(k + 1) * P]
                            wl = w_lo[b % slots][:, k * P:(k + 1) * P]
                            xh, xl = x_hi[:, k, n * nt:(n + 1) * nt], x_lo[:, k, n * nt:(n + 1) * nt]
                            pe.matmul(out, wh, xh, start=(begins and k == 0), stop=False)
                            pe.matmul(out, wh, xl, start=False, stop=False)
                            mm = pe.matmul(out, wl, xh, start=False, stop=(ends and k == kt - 1))
                    mm.then_inc(w_used, 1)

            loop(pe, 0, steps, step)

        @block.vector
        def _(dve):
            def step(i, first):
                for a in range(n_sum):
                    wait_sum(dve, i, a)
                    work["dve"](dve, i, a, first)

            if "dve_first" in work:
                work["dve_first"](dve)
            loop(dve, 0, steps, step)


def project_phase(nc, c, tag, T, tiles, w, dst, split=None):
    def epilogue(f, sum_free, acc):
        def dve(eng, i, a, first):
            copy(eng, two(at(dst, 2 * i + a), T), acc(a)).then_inc(sum_free[a], 1)

        if split is None:
            return {"dve": dve}
        split_done = f.sem("split_done")

        def split_first(eng):
            src, hi, lo = split
            for k in range(4):
                eng.tensor_copy(hi[:, k], src[:, k]).then_inc(split_done, 1)
            for k in range(4):
                eng.wait_ge(split_done, k + 1)
                eng.tensor_tensor(lo[:, k], src[:, k], hi[:, k].bitcast(F32), ALU.subtract)
        return {"dve": dve, "dve_first": split_first}

    body = [((s, w), DT, c.x_hi, c.x_lo, True, True) for s in range(2)]
    dense_phase(nc, c, tag, T, tiles // 2, body, epilogue)


def rsqrt_act(act, c, xs, t, y, root, r0, xs_ready, n0, scaled=False):
    act.wait_ge(xs_ready, n0)
    act.activation(t, xs, ACT.Ln, scale=LN_SCALE if scaled else 1.0).then_inc(root, 1)
    act.wait_ge(root, r0 + 1)
    act.activation(y, t, ACT.Exp, scale=-0.5,
                   **({"bias": vec(c, "log_half_scale")} if scaled else {})).then_inc(root, 1)


def rsqrt_dve(dve, xs, t, y, root, r0, newton, n0):
    dve.wait_ge(root, r0 + 2)
    dve.tensor_tensor(t, xs, y, ALU.mult).then_inc(newton, 1)
    dve.wait_ge(newton, n0 + 1)
    dve.scalar_tensor_tensor(t, t, -0.5, y, ALU.mult, ALU.mult).then_inc(newton, 1)
    dve.wait_ge(newton, n0 + 2)
    dve.scalar_tensor_tensor(y, t, 1.5, y, ALU.add, ALU.mult).then_inc(newton, 1)
    dve.wait_ge(newton, n0 + 3)




def memory_phase(nc, c):
    with Phase(nc, "mem") as g:
        mem = g.sb("mem", [P, DT, MEM])
        m_hi, m_lo = g.sb("m_hi", [P, DT, MEM], F32R), g.sb("m_lo", [P, DT, MEM], F32R)
        mk = g.sb("mk", [P, 4, MEM])
        norm_phase(nc, c, "mem1", MEM, mem, "mem_g", m_hi, m_lo, first_two(c.a["w_mk"]), c.a["memT"])

        def epilogue(f, sum_free, acc):
            def dve(eng, i, a, first):
                copy(eng, two(at(mk, 2 * i + a), MEM), acc(a)).then_inc(sum_free[a], 1)
            return {"dve": dve}

        body = [((s, c.a["w_mk"]), DT, m_hi, m_lo, True, True) for s in range(2)]
        dense_phase(nc, c, "mem2", MEM, 2, body, epilogue)

        with Phase(nc, "mem3") as f:
            sq, xs, t, y = (f.sb(n, [P, 4, MEM]) for n in ("sq", "xs", "t", "y"))
            raw = f.sb("raw", [P, DT, 512])
            w_hi, w_lo = f.sb("w_hi", [P, DT, 512], F32R), f.sb("w_lo", [P, DT, 512], F32R)
            mv = f.sb("mv", [P, 2, 512])
            ps, pv = f.ps("ps", [P, 2, 512]), f.ps("pv", [P, 2, 512])
            squared, mean, root, newton = f.sem("squared"), f.sem("mean"), f.sem("root"), f.sem("newton")
            hi_done, lo_done, mv_sum, mv_out, out = (f.sem(n) for n in ("hi_done", "lo_done", "mv_sum", "mv_out", "out"))
            loaded = [f.sem(f"loaded{k}") for k in range(0, DT, 2)]
            block = f.block()

            @block.sync
            def _(sp):
                for k in range(0, DT, 2):
                    sp.dma_start(raw[:, k:k + 2, :], c.a["w_mv"][:, k:k + 2, :]).then_inc(loaded[k // 2], 16)
                sp.wait_ge(newton, 5)
                sp.dma_start(c.a["o_mk"], mk[:, :, :]).then_inc(out, 16)
                sp.wait_ge(mv_out, 1)
                sp.dma_start(c.a["o_mv"], mv[:, :, :]).then_inc(out, 16)
                sp.wait_ge(out, 32)

            @block.scalar
            def _(act):
                act.activation(sq[:, :, :], mk[:, :, :], ACT.Square).then_inc(squared, 1)
                for k in range(0, DT, 2):
                    act.wait_ge(loaded[k // 2], 16)
                    act.activation(w_hi[:, k:k + 2, :], raw[:, k:k + 2, :], ACT.Copy).then_inc(hi_done, 1)
                rsqrt_act(act, c, xs[:, :, :], t[:, :, :], y[:, :, :], root, 0, newton, 1)

            @block.gpsimd
            def _(pool):
                for k in range(0, DT, 2):
                    pool.wait_ge(hi_done, k // 2 + 1)
                    pool.tensor_tensor(w_lo[:, k:k + 2, :], raw[:, k:k + 2, :], w_hi[:, k:k + 2, :].bitcast(F32),
                                       ALU.subtract).then_inc(lo_done, 1)

            @block.tensor
            def _(pe):
                pe.wait_ge(squared, 1)
                for n in range(2):
                    mm = pe.matmul(ps[:, n, :], c.ones[:, :], sq[:, 2 * n:2 * n + 2, :].rearrange("p a t -> p (a t)"),
                                   start=True, stop=True)
                mm.then_inc(mean, 1)
                for k in range(DT):
                    pe.wait_ge(lo_done, k // 2 + 1)
                    for n in range(2):
                        tok = slice(n * P, (n + 1) * P)
                        pe.matmul(pv[:, n, :], m_hi[:, k, tok], w_hi[:, k, :], start=(k == 0), stop=False)
                        pe.matmul(pv[:, n, :], m_hi[:, k, tok], w_lo[:, k, :], start=False, stop=False)
                        mm = pe.matmul(pv[:, n, :], m_lo[:, k, tok], w_hi[:, k, :], start=False, stop=(k == DT - 1))
                mm.then_inc(mv_sum, 1)

            @block.vector
            def _(dve):
                dve.wait_ge(mean, 1)
                dve.tensor_scalar(xs[:, :, :].rearrange("p (n a) t -> p n (a t)", n=2), ps[:, :, :], 1.0 / P, RMS_EPS,
                                  ALU.mult, ALU.add).then_inc(newton, 1)
                rsqrt_dve(dve, xs[:, :, :], t[:, :, :], y[:, :, :], root, 0, newton, 1)
                dve.scalar_tensor_tensor(mk[:, :, :], mk[:, :, :], vec(c, "mkn"), y[:, :, :], ALU.mult,
                                         ALU.mult).then_inc(newton, 1)
                dve.wait_ge(mv_sum, 1)
                dve.tensor_copy(mv[:, :, :], pv[:, :, :]).then_inc(mv_out, 1)




def attention_prep(nc, c, tag, g, T, pa, kw, vw):
    nb, nt = pieces(T)
    normed_tiles = [0, 1, 2, 3, 4, 6, 7, 8, 9]
    n_n = len(normed_tiles)
    prompt = T if g == 0 else PROMPT_END
    with Phase(nc, tag) as f:
        sq = f.sb("sq", [P, 2, T])
        to_rows, from_rows = f.sb("to_rows", [P, n_n, P]), f.sb("from_rows", [P, n_n, P])
        xs, t, y = (f.sb(n, [P, T]) for n in ("xs", "t", "y"))
        ps, ps_y = f.ps("ps", [P, 2, 512]), f.ps("ps_y", [P, 2, 2, 512])
        tables, squared, ss, spread = f.sem("tables"), f.sem("squared"), f.sem("ss"), f.sem("spread")
        root, newton, done, out, v_done, cache = (
            f.sem(n) for n in ("root", "newton", "done", "out", "v_done", "cache"))
        block = f.block()

        @block.sync
        def _(sp):
            sp.dma_start(to_rows[:, :, :], c.a["to_rows"]).then_inc(tables, 16)
            sp.dma_start(from_rows[:, :, :], c.a["from_rows"]).then_inc(tables, 16)
            if g == 1:
                w0 = WINDOW + PROMPT_END
                sp.dma_start(kw[:, w0:w0 + WINDOW], c.a["cache_k"]).then_inc(cache, 16)
                sp.dma_start(vw[:, w0:w0 + WINDOW], c.a["cache_v"]).then_inc(cache, 16)
                sp.wait_ge(cache, 32)
                sp.wait_ge(done, n_n)
                sp.wait_ge(v_done, 1)
                for dst, src in (("o_kp", kw[:, PROMPT_END:PROMPT_END + WINDOW]),
                                 ("o_vp", vw[:, PROMPT_END:PROMPT_END + WINDOW]),
                                 ("o_ks", kw[:, w0 + CHUNK:w0 + KEYS]), ("o_vs", vw[:, w0 + CHUNK:w0 + KEYS])):
                    sp.dma_start(c.a[dst], src).then_inc(out, 16)
                sp.wait_ge(out, 64)

        @block.gpsimd
        def _(pool):
            pool.tensor_copy(vw[:, WINDOW:WINDOW + prompt], pa[:, 5, 0:prompt])
            if g == 0:
                pool.memset(kw[:, 0:WINDOW], 0.0)
                pool.memset(vw[:, 0:WINDOW], 0.0).then_inc(v_done, 1)
            else:
                pool.tensor_copy(vw[:, 2 * WINDOW + prompt:2 * WINDOW + T], pa[:, 5, prompt:T])
                pool.tensor_copy(kw[:, 0:WINDOW], c.kv_carry[:, 0])
                pool.tensor_copy(vw[:, 0:WINDOW], c.kv_carry[:, 1]).then_inc(v_done, 1)

        @block.scalar
        def _(act):
            for n, m in enumerate(normed_tiles):
                if n >= 2:
                    act.wait_ge(ss, n - 1)
                act.activation(sq[:, n % 2], pa[:, m], ACT.Square).then_inc(squared, 1)
            rsqrt_act(act, c, xs[:, :], t[:, :], y[:, :], root, 0, newton, 1)

        @block.tensor
        def _(pe):
            pe.wait_ge(tables, 32)
            for n in range(n_n):
                pe.wait_ge(squared, n + 1)
                for b in range(nb):
                    mm = pe.matmul(ps[:, b, 0:nt], to_rows[:, n, :], sq[:, n % 2, b * nt:(b + 1) * nt],
                                   start=(n == 0), stop=(n == n_n - 1))
                mm.then_inc(ss, 1)
            pe.wait_ge(newton, 4)
            for n in range(n_n):
                if n >= 2:
                    pe.wait_ge(done, n - 1)
                for b in range(nb):
                    mm = pe.matmul(ps_y[:, n % 2, b, 0:nt], from_rows[:, n, :], y[:, b * nt:(b + 1) * nt],
                                   start=True, stop=True)
                mm.then_inc(spread, 1)

        @block.vector
        def _(dve):
            dve.wait_ge(ss, n_n)
            dve.tensor_scalar(two(xs[:, :], T), ps[:, 0:nb, 0:nt], RMS_EPS, None, ALU.add).then_inc(newton, 1)
            rsqrt_dve(dve, xs[:, :], t[:, :], y[:, :], root, 0, newton, 1)
            for n, m in enumerate(normed_tiles):
                dve.wait_ge(spread, n + 1)
                gain = vec(c, "qn" if m < 4 else "kn" if m == 4 else "mqn")
                if m != 4:
                    dve.scalar_tensor_tensor(two(pa[:, m], T), two(pa[:, m], T), gain, ps_y[:, n % 2, 0:nb, 0:nt],
                                             ALU.mult, ALU.mult).then_inc(done, 1)
                    continue
                if g == 0:
                    ins = dve.scalar_tensor_tensor(two(kw[:, WINDOW:WINDOW + T], T), two(pa[:, m], T), gain,
                                                   ps_y[:, n % 2, 0:nb, 0:nt], ALU.mult, ALU.mult)
                else:
                    dve.scalar_tensor_tensor(kw[:, WINDOW:WINDOW + prompt], pa[:, m, 0:prompt], gain,
                                             ps_y[:, n % 2, 0, 0:prompt], ALU.mult, ALU.mult)
                    ins = dve.scalar_tensor_tensor(kw[:, 2 * WINDOW + prompt:2 * WINDOW + T], pa[:, m, prompt:T],
                                                   gain, ps_y[:, n % 2, 0, prompt:T], ALU.mult, ALU.mult)
                ins.then_inc(done, 1)
            if g == 0:
                dve.wait_ge(done, n_n)
                dve.wait_ge(v_done, 1)
                dve.tensor_copy(c.kv_carry[:, 0], kw[:, T:T + WINDOW])
                dve.tensor_copy(c.kv_carry[:, 1], vw[:, T:T + WINDOW])


def wait_past(eng, sem, value):
    if not (isinstance(value, int) and value <= 0):
        eng.wait_ge(sem, value)


def attention_phase(nc, c, tag, g, T, pa, kw, vw, o_hi, o_lo, room):
    n_chunks = T // CHUNK
    C = CHUNK
    w0 = WINDOW + PROMPT_END
    with Phase(nc, tag) as f:
        alibi = f.sb("alibi", [P, 3, 4, KEYS])
        memories = [("o_mk", "o_mv"), ("cache_mk", "cache_mv")][0:1 + g]
        mk, mv = f.sb("mk", [P, len(memories), 4, MEM]), f.sb("mv", [P, len(memories), 2, 512])
        two_of = lambda name, shape: [f.sb(f"{name}{u}", shape) for u in range(2)]
        q_bd, s, p = two_of("q_bd", [P, 4, P]), two_of("s", [P, 4, KEYS]), two_of("p", [P, 4, KEYS])
        top, neg, srow, total, esink, inv = (
            two_of(n, [P, 4]) for n in ("top", "neg", "srow", "total", "esink", "inv"))
        diag, pt, pt_tail = two_of("diag", [P, 4, P]), two_of("pt", [P, 4, P]), two_of("pt_tail", [P, 4, P])
        qm, pm, mdiag = f.sb("qm", [P, 4, P]), f.sb("pm", [P, 4, MEM]), f.sb("mdiag", [P, 4, P])
        mtop, mneg, mtotal, minv = (f.sb(n, [P, 4]) for n in ("mtop", "mneg", "mtotal", "minv"))
        v_in = f.sb("v_in", [P, P])
        flat = room[:, :, :].rearrange("p k t -> p (k t)")
        pmt, whole = (flat[:, n * 8 * P:(n + 1) * 8 * P].rearrange("p (h q) -> p h q", h=8) for n in range(2))
        v_before, v_now = f.sb("v_before", [P, P]), f.sb("v_now", [P, P])
        v_cache, v_sample = (f.sb("v_cache", [P, P]), f.sb("v_sample", [P, P])) if g == 1 else (None, None)
        ps_s, ps_m = f.ps("ps_s", [P, 2, 512]), f.ps("ps_m", [P, 4, MEM])
        ps_t, ps_tail = f.ps("ps_t", [P, 4, P]), f.ps("ps_tail", [P, 4, P])
        ps_o, ps_v = f.ps("ps_o", [P, 4, P]), f.ps("ps_v", [P, 4, P])
        names = ("consts ahead q_staged m_staged v_staged scores biased topped sunk shifted exps summed inverse scaled "
                 "turned pt_read pv v_turned v_moved v_read swa_out o_lo mem_scores mem_top mem_shifted mem_exps "
                 "mem_inverse mem_scaled mem_turned pmt_read mem_pv mem_out").split()
        S = {n: f.sem(n) for n in names}
        block = f.block()
        H = [slice(0, 64), slice(64, 128)]

        def is_sample(n):
            return g == 1 and isinstance(n, int) and n == n_chunks - 1

        def pair(i):
            return i, ((2 * i, 0), (2 * i + 1, 1))

        end = (n_chunks // 2, ((n_chunks - 1, 0),)) if n_chunks % 2 else pair(n_chunks // 2 - 1)

        def pairs(eng, first, body):
            first(pair(0))
            body(pair(0), pair(1))
            with eng.Fori(1, end[0] - 1) as i:
                body(pair(i), pair(i + 1))
            body(pair(end[0] - 1), end)
            body(end, None)

        def window(tensor, n):
            start = w0 if is_sample(n) else n * C
            return tensor[:, start:start + KEYS] if isinstance(start, int) else tensor[:, bass.ds(start, KEYS)]

        @block.sync
        def _(sp):
            sp.dma_start(alibi[:, :, :, :], c.a["alibi"]).then_inc(S["consts"], 16)
            for n, (keys, values) in enumerate(memories):
                sp.dma_start(mk[:, n], c.a[keys]).then_inc(S["consts"], 16)
                sp.dma_start(mv[:, n], c.a[values]).then_inc(S["consts"], 16)
            sp.wait_ge(S["consts"], 16 + 32 * len(memories))
            load_ahead(sp, c, [c.a["w_gate"][0], c.a["w_branch"][0]], S["ahead"])

        @block.gpsimd
        def _(pool):
            def stage(m, chunks):
                nq = C * len(chunks)
                for n, u in chunks:
                    wait_past(pool, S["scores"], n - 1)
                    pool.tensor_tensor(q_bd[u][:, :, :].rearrange("p j (e t) -> p j e t", e=2),
                                       cols(pa, slice(0, 4), n * C, C).unsqueeze(2).to_broadcast([P, 4, 2, C]),
                                       c.masks[:, BD].rearrange("p (e t) -> p e t", e=2).unsqueeze(1).to_broadcast(
                                           [P, 4, 2, C]), ALU.mult).then_inc(S["q_staged"], 1)
                n0 = chunks[0][0]
                wait_past(pool, S["v_turned"], m)
                start = WINDOW + n0 * C
                nv = C if is_sample(chunks[-1][0]) else nq
                pool.tensor_copy(v_in[:, 0:nv], vw[:, start:start + nv] if isinstance(start, int) else (
                    vw[:, bass.ds(start, nv)])).then_inc(S["v_staged"], 1)
                wait_past(pool, S["mem_scores"], m)
                pool.tensor_copy(qm[:, :, 0:nq], cols(pa, slice(6, 10), n0 * C, nq)).then_inc(S["m_staged"], 1)

            def rounded_off(m, chunks):
                n0, nq = chunks[0][0], C * len(chunks)
                pool.wait_ge(S["mem_out"], m + 1)
                pool.tensor_tensor(cols(o_lo, slice(4, 12), n0 * C, nq), whole[:, :, 0:nq],
                                   cols(o_hi, slice(4, 12), n0 * C, nq).bitcast(F32), ALU.subtract).then_inc(S["o_lo"], 1)

            def body(now, ahead):
                stage(*ahead)
                rounded_off(*now)

            stage(*pair(0))
            stage(*pair(1))
            body(pair(0), pair(2) if end[0] > 2 else end)
            if end[0] > 3:
                with pool.Fori(1, end[0] - 2) as i:
                    body(pair(i), pair(i + 2))
            body(pair(end[0] - 2), end)
            rounded_off(*pair(end[0] - 1))
            rounded_off(*end)

        @block.tensor
        def _(pe):
            def scores(n, u):
                pe.wait_ge(S["q_staged"], n + 1)
                wait_past(pe, S["biased"], n)
                keys = window(kw, n)
                for j in range(4):
                    mm = pe.matmul(ps_s[:, j // 2, (j % 2) * KEYS:(j % 2 + 1) * KEYS], q_bd[u][:, j, :], keys,
                                   start=True, stop=True)
                mm.then_inc(S["scores"], 1)

            def mem_scores(m, chunks):
                pe.wait_ge(S["m_staged"], m + 1)
                wait_past(pe, S["pmt_read"], m)
                nq = C * len(chunks)
                for h in range(4):
                    if is_sample(chunks[-1][0]):
                        for u in range(2):
                            mm = pe.matmul(ps_m[H[u], h, :], qm[:, h, H[u]], mk[:, u, h, :], start=True, stop=True)
                    else:
                        mm = pe.matmul(ps_m[0:nq, h, :], qm[:, h, 0:nq], mk[:, 0, h, :], start=True, stop=True)
                mm.then_inc(S["mem_scores"], 1)

            def turn_values(m, chunks):
                pe.wait_ge(S["v_staged"], m + 1)
                wait_past(pe, S["v_read"], m)
                wait_past(pe, S["mem_out"], m - 1)
                nv = C if is_sample(chunks[-1][0]) else C * len(chunks)
                mm = pe.matmul(ps_v[0:nv, 0, :], v_in[:, 0:nv], c.ident[:, :], start=True, stop=True)
                if isinstance(m, int) and m == 0:
                    mm = pe.matmul(ps_v[:, 1, :], vw[:, 0:WINDOW], c.ident[:, :], start=True, stop=True)
                if is_sample(chunks[-1][0]):
                    pe.matmul(ps_v[:, 1, :], vw[:, w0 + C:w0 + KEYS], c.ident[:, :], start=True, stop=True)
                    mm = pe.matmul(ps_v[H[1], 2, :], vw[:, w0:w0 + C], c.ident[:, :], start=True, stop=True)
                mm.then_inc(S["v_turned"], 1)

            def first(now):
                pe.wait_ge(S["consts"], 16 + 32 * len(memories))
                m, chunks = now
                for n, u in chunks:
                    scores(n, u)
                turn_values(m, chunks)
                mem_scores(m, chunks)

            def body(now, then):
                m, chunks = now
                nq = C * len(chunks)
                for n, u in chunks:
                    if then and u < len(then[1]):
                        scores(*then[1][u])
                    pe.wait_ge(S["scaled"], n + 1)
                    wait_past(pe, S["pt_read"], n)
                    main, tail = (slice(0, P), slice(P, KEYS)) if u == 0 else (slice(C, KEYS), slice(0, C))
                    for j in range(4):
                        pe.matmul(ps_t[:, j, :], p[u][:, j, main], diag[u][:, j, :], start=True, stop=True)
                    for j in range(4):
                        mm = pe.matmul(ps_tail[H[u], j, :], p[u][:, j, tail], diag[u][:, j, :], start=True, stop=True)
                    mm.then_inc(S["turned"], 1)
                    if then and u == 0:
                        turn_values(*then)
                    pe.wait_ge(S["v_read"], m + 1)
                    pe.wait_ge(S["pt_read"], n + 1)
                    if u == 0:
                        wait_past(pe, S["swa_out"], m)
                    before, own = (v_cache, v_sample) if is_sample(n) else (v_before, v_now)
                    v_main, v_tail = (before, own) if u == 0 else (own, before)
                    for e in range(2):
                        out = ps_o[H[e], :, u * C:(u + 1) * C]
                        pe.matmul(out, v_main[:, H[e]], pt[u][:, :, H[e]], start=True, stop=False)
                        mm = pe.matmul(out, v_tail[H[u], H[e]], pt_tail[u][H[u], :, H[e]], start=False, stop=True)
                    mm.then_inc(S["pv"], 1)
                pe.wait_ge(S["mem_scaled"], m + 1)
                turned = ps_m[:, :, :].rearrange("p h (a k) -> p (h a) k", a=2)
                for h in range(4):
                    for half in range(2):
                        mm = pe.matmul(turned[:, 2 * h + half, 0:nq], pm[0:nq, h, half * P:(half + 1) * P],
                                       mdiag[0:nq, h, 0:nq], start=True, stop=True)
                mm.then_inc(S["mem_turned"], 1)
                if then:
                    mem_scores(*then)
                pe.wait_ge(S["pmt_read"], m + 1)
                pe.wait_ge(S["v_read"], m + (2 if then else 1))
                wait_past(pe, S["mem_out"], m)
                for h in range(4):
                    for u, q_ in enumerate(H if is_sample(chunks[-1][0]) else [slice(0, nq)]):
                        for half in range(2):
                            mm = pe.matmul(ps_v[:, h, q_], mv[:, u, half, h * P:(h + 1) * P],
                                           pmt[:, 2 * h + half, q_], start=(half == 0), stop=(half == 1))
                mm.then_inc(S["mem_pv"], 1)

            pairs(pe, first, body)

        @block.vector
        def _(dve):
            def bias_and_top(n, u):
                bias = n if g == 0 and isinstance(n, int) and n < 2 else 2
                dve.wait_ge(S["scores"], n + 1)
                wait_past(dve, S["exps"], n - 1)
                for a in range(2):
                    ins = dve.scalar_tensor_tensor(
                        s[u][:, 2 * a:2 * a + 2, :], ps_s[:, a, 0:2 * KEYS].rearrange("p (j k) -> p j k", j=2), 0.125,
                        alibi[:, bias, 2 * a:2 * a + 2, :], ALU.mult, ALU.add)
                ins.then_inc(S["biased"], 1)
                dve.wait_ge(S["biased"], n + 1)
                dve.tensor_reduce(top[u][:, :], s[u][:, :, :], AX.X, ALU.max).then_inc(S["topped"], 1)
                dve.wait_ge(S["topped"], n + 1)
                dve.tensor_tensor(top[u][:, :], top[u][:, :], vec(c, "sink", 0, 4), ALU.max).then_inc(S["sunk"], 1)
                dve.wait_ge(S["sunk"], n + 1)
                dve.tensor_scalar(neg[u][:, :], top[u][:, :], -1.0, None, ALU.mult)
                dve.tensor_tensor(srow[u][:, :], vec(c, "sink", 0, 4), top[u][:, :], ALU.subtract).then_inc(S["shifted"], 1)

            def mem_top(m, chunks):
                nq = C * len(chunks)
                dve.wait_ge(S["mem_scores"], m + 1)
                dve.tensor_reduce(mtop[0:nq, :], ps_m[0:nq, :, :], AX.X, ALU.max).then_inc(S["mem_top"], 1)
                dve.wait_ge(S["mem_top"], m + 1)
                wait_past(dve, S["mem_exps"], m)
                dve.tensor_scalar(mneg[0:nq, :], mtop[0:nq, :], -float(P) ** -0.5, None,
                                  ALU.mult).then_inc(S["mem_shifted"], 1)

            def move_values(m, chunks):
                dve.wait_ge(S["v_turned"], m + 1)
                if isinstance(m, int) and m == 0:
                    dve.tensor_copy(v_before[:, :], ps_v[:, 1, :])
                else:
                    dve.wait_ge(S["pv"], 2 * m)
                    dve.tensor_copy(v_before[:, :], v_now[:, :]).then_inc(S["v_moved"], 1)
                    dve.wait_ge(S["v_moved"], m)
                if is_sample(chunks[-1][0]):
                    dve.tensor_copy(v_sample[:, :], ps_v[:, 1, :])
                    dve.tensor_copy(v_cache[H[1], :], ps_v[H[1], 2, :])
                nv = C if is_sample(chunks[-1][0]) else C * len(chunks)
                dve.tensor_copy(v_now[0:nv, :], ps_v[0:nv, 0, :]).then_inc(S["v_read"], 1)

            def first(now):
                dve.wait_ge(S["consts"], 16 + 32 * len(memories))
                m, chunks = now
                for n, u in chunks:
                    bias_and_top(n, u)
                move_values(m, chunks)
                mem_top(m, chunks)

            def body(now, then):
                m, chunks = now
                nq = C * len(chunks)
                for n, u in chunks:
                    dve.wait_ge(S["exps"], n + 1)
                    dve.tensor_tensor(total[u][:, :], total[u][:, :], esink[u][:, :], ALU.add).then_inc(S["summed"], 1)
                    dve.wait_ge(S["summed"], n + 1)
                    dve.reciprocal(inv[u][:, :], total[u][:, :]).then_inc(S["inverse"], 1)
                    dve.wait_ge(S["inverse"], n + 1)
                    dve.tensor_tensor(diag[u][:, :, :], c.ident[:, :].unsqueeze(1).to_broadcast([P, 4, P]),
                                      inv[u][:, :].unsqueeze(2).to_broadcast([P, 4, P]), ALU.mult).then_inc(S["scaled"], 1)
                    if u == 0:
                        dve.wait_ge(S["mem_exps"], m + 1)
                        dve.reciprocal(minv[0:nq, :], mtotal[0:nq, :]).then_inc(S["mem_inverse"], 1)
                        dve.wait_ge(S["mem_inverse"], m + 1)
                        wait_past(dve, S["mem_turned"], m)
                        dve.tensor_tensor(mdiag[0:nq, :, :], c.ident[0:nq, :].unsqueeze(1).to_broadcast([nq, 4, P]),
                                          minv[0:nq, :].unsqueeze(2).to_broadcast([nq, 4, P]),
                                          ALU.mult).then_inc(S["mem_scaled"], 1)
                    if then and u < len(then[1]):
                        bias_and_top(*then[1][u])
                if then:
                    move_values(*then)
                    mem_top(*then)

            pairs(dve, first, body)

        @block.scalar
        def _(act):
            def exps(n, u):
                act.wait_ge(S["shifted"], n + 1)
                wait_past(act, S["turned"], n - 1)
                for j in range(4):
                    act.activation(p[u][:, j, :], s[u][:, j, :], ACT.Exp, bias=neg[u][:, j:j + 1],
                                   accum_out=total[u][:, j:j + 1])
                act.activation(esink[u][:, :], srow[u][:, :], ACT.Exp).then_inc(S["exps"], 1)

            def mem_exps(m, chunks):
                nq = C * len(chunks)
                act.wait_ge(S["mem_shifted"], m + 1)
                wait_past(act, S["mem_turned"], m)
                for h in range(4):
                    ins = act.activation(pm[0:nq, h, :], ps_m[0:nq, h, :], ACT.Exp, bias=mneg[0:nq, h:h + 1],
                                         scale=float(P) ** -0.5, accum_out=mtotal[0:nq, h:h + 1])
                ins.then_inc(S["mem_exps"], 1)

            def first(now):
                m, chunks = now
                for n, u in chunks:
                    exps(n, u)
                mem_exps(m, chunks)

            def body(now, then):
                m, chunks = now
                nq = C * len(chunks)
                for n, u in chunks:
                    act.wait_ge(S["turned"], n + 1)
                    act.activation(pt[u][:, :, :], ps_t[:, :, :], ACT.Copy)
                    act.activation(pt_tail[u][H[u], :, :], ps_tail[H[u], :, :], ACT.Copy).then_inc(S["pt_read"], 1)
                    if then and u < len(then[1]):
                        exps(*then[1][u])
                act.wait_ge(S["mem_turned"], m + 1)
                wait_past(act, S["mem_pv"], m)
                turned = ps_m[:, :, :].rearrange("p h (a k) -> p (h a) k", a=2)
                act.activation(pmt[:, :, 0:nq], turned[:, :, 0:nq], ACT.Copy).then_inc(S["pmt_read"], 1)
                act.wait_ge(S["pv"], chunks[-1][0] + 1)
                wait_past(act, S["o_lo"], m)
                act.activation(cols(o_hi, slice(4, 8), chunks[0][0] * C, nq), ps_o[:, :, 0:nq], ACT.Copy)
                act.activation(whole[:, 0:4, 0:nq], ps_o[:, :, 0:nq], ACT.Copy).then_inc(S["swa_out"], 1)
                if then:
                    mem_exps(*then)
                act.wait_ge(S["mem_pv"], m + 1)
                act.activation(cols(o_hi, slice(8, 12), chunks[0][0] * C, nq), ps_v[:, :, 0:nq], ACT.Copy)
                act.activation(whole[:, 4:8, 0:nq], ps_v[:, :, 0:nq], ACT.Copy).then_inc(S["mem_out"], 1)

            pairs(act, first, body)



X_CUM, X_KK, X_G = slice(4, 8), slice(8, 12), slice(12, 16)
X_WA, X_XG = 14, 15
X_R, X_K, X_V, X_B = slice(16, 20), slice(20, 24), slice(24, 28), slice(28, 32)
BD, BD_LOW, BD_LOW_T, BD_OFF_T, BD_UP, UP_INCL = range(6)
N_MASKS = 6


def rwkv_prep(nc, c, tag, g, T, ar):
    nb, nt = pieces(T)
    with Phase(nc, tag) as f:
        mask = f.sb("mask", [P, T])
        half = f.sb("half", [P, 8])
        one_ka = f.sb("one_ka", [P, 4])
        t1, t2, t3, sq = (f.sb(n, [P, 4, T]) for n in ("t1", "t2", "t3", "sq"))
        to_rows, from_rows = f.sb("to_rows", [P, 4, P]), f.sb("from_rows", [P, 4, P])
        xs, t, y = (f.sb(n, [P, T]) for n in ("xs", "t", "y"))
        ps, ps_rows = f.ps("ps", [P, 2, 2, 512]), f.ps("ps_rows", [P, 2, 512])
        tables, rows, xs_in, kk_done = f.sem("tables"), f.sem("rows"), f.sem("xs_in"), f.sem("kk_done")
        setup, saved, mixed, lora_in = f.sem("setup"), f.sem("saved"), f.sem("mixed"), f.sem("lora_in")
        parts = (slice(0, 2), slice(2, 8), slice(8, 14))
        d_done = [f.sem(f"d_done{n}") for n in range(3)]
        prod, tan, dstep, root, newton = (f.sem(n) for n in ("prod", "tan", "dstep", "root", "newton"))
        out, g_done, sq_done = f.sem("out"), f.sem("g_done"), f.sem("sq_done")
        read = f.sem("read")
        block = f.block()
        pp = lambda n: ps[:, n % 2, 0:nb, 0:nt]
        raw, mix = ar[:, 0:R_TILES, :], ar[:, R_TILES:2 * R_TILES, :]

        def before_less_token(eng, n):
            ts, sem = parts[n], d_done[n]
            eng.tensor_tensor(mix[:, ts, 1:T], raw[:, ts, 0:T - 1], raw[:, ts, 1:T], ALU.subtract).then_inc(sem, 1)
            if g == 0:
                eng.tensor_scalar(mix[:, ts, 0:1], raw[:, ts, 0:1], -1.0, None, ALU.mult).then_inc(sem, 1)
            else:
                eng.wait_ge(sem, 1)
                eng.tensor_tensor(mix[:, ts, 0], c.shift_carry[:, ts], raw[:, ts, 0], ALU.subtract).then_inc(sem, 1)
                eng.tensor_tensor(mix[:, ts, PROMPT_END], vec(c, "shift", ts.start, ts.stop - ts.start),
                                  raw[:, ts, PROMPT_END], ALU.subtract).then_inc(sem, 1)

        @block.sync
        def _(sp):
            sp.dma_start(to_rows[:, :, :], c.a["to_rows"][:, 0:4, :]).then_inc(tables, 16)
            sp.dma_start(from_rows[:, :, :], c.a["from_rows"][:, 0:4, :]).then_inc(tables, 16)
            if g == 1:
                sp.wait_ge(saved, 1)
                sp.dma_start(c.a["o_shp"], c.shift_out[:, 0]).then_inc(out, 16)
                sp.dma_start(c.a["o_shs"], c.shift_out[:, 1]).then_inc(out, 16)
                sp.wait_ge(out, 32)

        @block.gpsimd
        def _(pool):
            before_less_token(pool, 2)
            pool.memset(mask[:, :], 1.0).then_inc(setup, 1)
            pool.wait_ge(setup, 1)
            pool.memset(mask[:, :].rearrange("p (c t) -> p c t", t=CHUNK)[:, :, 0:1], 0.0).then_inc(setup, 1)
            pool.tensor_scalar(half[:, :], vec(c, "w0", 0, 8), 0.5, None, ALU.mult).then_inc(setup, 1)
            pool.tensor_scalar(one_ka[:, :], vec(c, "ka", 0, 4), -1.0, 1.0, ALU.mult, ALU.add).then_inc(setup, 1)

        @block.vector
        def _(dve):
            if g == 0:
                dve.tensor_copy(c.shift_carry[:, :], raw[:, :, T - 1]).then_inc(saved, 1)
            else:
                dve.tensor_copy(c.shift_out[:, 0], raw[:, :, PROMPT_END - 1])
                dve.tensor_copy(c.shift_out[:, 1], raw[:, :, T - 1]).then_inc(saved, 1)
            for n, part in enumerate(parts):
                if n < 2:
                    before_less_token(dve, n)
                dve.wait_ge(d_done[n], 2 + g)
                for m in range(part.start, part.stop):
                    dve.scalar_tensor_tensor(mix[:, m], mix[:, m], vec(c, "mu", m), raw[:, m], ALU.mult,
                                             ALU.add).then_inc(mixed, 1)
            dve.wait_ge(mixed, 14)
            dve.wait_ge(saved, 1)
            for m in range(4):
                ins = dve.tensor_scalar(ar[:, 8 + m], ar[:, 20 + m], vec(c, "kk", m), None, ALU.mult)
            ins.then_inc(kk_done, 1)
            dve.wait_ge(tan, 2)
            dve.tensor_scalar(ar[:, X_XG], ar[:, X_XG], 0.5, 0.5, ALU.mult, ALU.add).then_inc(lora_in, 1)
            dve.wait_ge(tan, 2 + 4)
            dve.tensor_scalar(t1[:, :, :], t1[:, :, :], -0.5 * DECAY, -0.5 * DECAY, ALU.mult, ALU.add).then_inc(dstep, 1)
            dve.wait_ge(dstep, 1)
            dve.wait_ge(setup, 4)
            for m in range(4):
                dve.tensor_tensor_scan(ar[:, 4 + m], mask[:, :], t1[:, m], 0.0, ALU.mult, ALU.add)
            dve.wait_ge(tan, 2 + 8)
            dve.tensor_scalar(t2[:, :, :], t2[:, :, :], 0.5, 0.5, ALU.mult, ALU.add).then_inc(dstep, 1)
            dve.wait_ge(dstep, 2)
            for m in range(4):
                ins = dve.tensor_scalar(t3[:, m], t2[:, m], vec(c, "ka", m), one_ka[:, m:m + 1], ALU.mult, ALU.add)
            ins.then_inc(dstep, 1)
            dve.wait_ge(dstep, 3)
            dve.tensor_tensor(ar[:, X_K, :], ar[:, X_K, :], t3[:, :, :], ALU.mult).then_inc(dstep, 1)
            dve.wait_ge(dstep, 4)
            for m in range(4):
                ins = dve.scalar_tensor_tensor(t3[:, m], ar[:, 16 + m], vec(c, "rk", m), ar[:, 20 + m],
                                               ALU.mult, ALU.mult)
            ins.then_inc(dstep, 1)
            dve.wait_ge(rows, 1)
            dve.tensor_scalar(two(xs[:, :], T), ps_rows[:, 0:nb, 0:nt], 64.0, 1e-24, ALU.mult,
                              ALU.max).then_inc(xs_in, 1)
            for m in range(4):
                dve.wait_ge(prod, 12 + m + 1)
                dve.tensor_tensor(two(ar[:, m], T), pp(12 + m), two(ar[:, 24 + m], T), ALU.mult).then_inc(read, 1)
            rsqrt_dve(dve, xs[:, :], t[:, :], y[:, :], root, 0, newton, 0)
            for m in range(4):
                dve.wait_ge(prod, 16 + m + 1)
                dve.tensor_tensor(two(ar[:, 8 + m], T), pp(16 + m), two(ar[:, 8 + m], T), ALU.mult).then_inc(read, 1)
            dve.wait_ge(read, 8)
            dve.tensor_tensor(ar[:, X_B, :], ar[:, X_KK, :], t2[:, :, :], ALU.mult)

        @block.scalar
        def _(act):
            act.wait_ge(mixed, 1)
            act.activation(ar[0:64, X_WA], ar[0:64, X_WA], ACT.Tanh).then_inc(tan, 1)
            act.wait_ge(mixed, 2)
            act.activation(ar[:, X_XG], ar[:, X_XG], ACT.Tanh, scale=0.5).then_inc(tan, 1)
            act.wait_ge(setup, 4)
            for m in range(8):
                act.wait_ge(prod, m + 1)
                dst = t1 if m < 4 else t2
                act.activation(two(dst[:, m % 4], T), pp(m), ACT.Tanh, bias=half[:, m:m + 1], scale=0.5).then_inc(tan, 1)
            act.wait_ge(kk_done, 1)
            act.activation(sq[:, :, :], ar[:, X_KK, :], ACT.Square).then_inc(sq_done, 1)
            for m in range(4):
                act.wait_ge(prod, 8 + m + 1)
                if m == 3:
                    act.wait_ge(prod, 12)
                act.activation(two(ar[:, 12 + m], T), pp(8 + m), ACT.Copy).then_inc(g_done, 1)
            rsqrt_act(act, c, xs[:, :], t[:, :], y[:, :], root, 0, xs_in, 1, scaled=True)

        @block.tensor
        def _(pe):
            def product(n, lhs, rhs, lo, hi):
                for b in range(nb):
                    mm = pe.matmul(ps[:, n % 2, b, 0:nt], lhs, rhs[lo:hi, b * nt:(b + 1) * nt], start=True, stop=True)
                mm.then_inc(prod, 1)

            pe.wait_ge(tan, 1)
            for m in range(4):
                if m >= 2:
                    pe.wait_ge(tan, 2 + m - 1)
                product(m, c.lora[0:64, 0, m * P:(m + 1) * P], ar[:, X_WA], 0, 64)
            for m in range(4):
                pe.wait_ge(tan, 2 + 4 + m - 1)
                product(4 + m, c.lora[64:128, 0, m * P:(m + 1) * P], ar[:, X_WA], 64, 128)
            pe.wait_ge(lora_in, 1)
            for m in range(4):
                pe.wait_ge(tan, min(10, 2 + 8 + m - 1))
                if m >= 2:
                    pe.wait_ge(g_done, m - 1)
                product(8 + m, c.lora[:, 1, m * P:(m + 1) * P], ar[:, X_XG], 0, 128)
            pe.wait_ge(tables, 32)
            pe.wait_ge(sq_done, 1)
            for m in range(4):
                for b in range(nb):
                    mm = pe.matmul(ps_rows[:, b, 0:nt], to_rows[:, m, :], sq[:, m, b * nt:(b + 1) * nt],
                                   start=(m == 0), stop=(m == 3))
            mm.then_inc(rows, 1)
            pe.wait_ge(dstep, 5)
            for m in range(4):
                if m < 2:
                    pe.wait_ge(g_done, 3 + m)
                else:
                    pe.wait_ge(read, m - 1)
                product(12 + m, c.ones_head[:, :], t3[:, m], 0, 128)
            pe.wait_ge(newton, 3)
            for m in range(4):
                pe.wait_ge(read, 3 + m)
                product(16 + m, from_rows[:, m, :], y, 0, 128)


def rwkv_scan(nc, c, tag, g, T, ar, o):
    n_chunks = T // CHUNK
    C = CHUNK
    with Phase(nc, tag) as f:
        two_of = lambda name, shape: [f.sb(f"{name}{u}", shape) for u in range(2)]
        ep, en_bd, pc = two_of("ep", [P, 4, C + 1]), two_of("en_bd", [P, 4, P]), two_of("pc", [P, 4, 1])
        ar_s, a_bd = two_of("ar_s", [P, 4, 2 * C]), two_of("a_bd", [P, 4, P])
        b_bd, k_bd = two_of("b_bd", [P, 4, P]), two_of("k_bd", [P, 4, P])
        v_bd = two_of("v_bd", [P, 4, P])
        m1, m2 = two_of("m1", [P, 4, P]), two_of("m2", [P, 4, P])
        m3, m4 = two_of("m3", [P, 4, P]), two_of("m4", [P, 4, P])
        y = two_of("y", [P, 4, P])
        off_t, lk_bd, mb, mk = two_of("off_t", [P, 4, P]), two_of("lk_bd", [P, 4, P]), two_of("mb", [P, 4, C]), (
            two_of("mk", [P, 4, C]))
        x, sa, s0p = f.sb("x", [P, 4, P]), f.sb("sa", [P, 4, P]), f.sb("s0p", [P, 4, P])
        ps = [[f.ps(f"ps{u}{b}", [P, 4, P]) for b in range(3)] for u in range(2)]
        ps_q = [f.ps(f"ps_q{b}", [P, 4, P]) for b in range(2)]
        names = ("zeros decays operands blocks v_in vtok vtok_read gram at_read mk_read low low_read y1 hat tok "
                 "tok_read pow2 pow2_read pow4 pow4_read y2_read pow8 pow8_read y4_read y8 y8_read dinv dinv_read "
                 "mprod m_read t1 t1_read t2 t2_read t3 t3_read s0p xs xs_read sa sa_read ssum state osum o_read "
                 "stored").split()
        S = {n: f.sem(n) for n in names}
        block = f.block()
        H = [slice(0, 64), slice(64, 128)]
        bc = lambda m: m.unsqueeze(1).to_broadcast([P, 4, m.shape[1]])
        mask = lambda m: bc(c.masks[:, m])
        spread = lambda s: s.unsqueeze(2).to_broadcast([P, 4, 2, C])
        wide = lambda b: b.rearrange("p j (e t) -> p j e t", e=2)
        spread_mask = lambda m: c.masks[:, m].rearrange("p (e t) -> p e t", e=2).unsqueeze(1).to_broadcast(
            [P, 4, 2, C])
        pc_of = lambda u: pc[u][:, :, 0:1].to_broadcast([P, 4, P])
        first_pair = ((0, 0, True), (1, 1, True))

        def is_sample(n):
            return g == 1 and isinstance(n, int) and n == n_chunks - 1

        def state_in(n, u):
            return c.sample_state if is_sample(n) else c.state[(u + g) % 2]

        def state_out(u):
            return c.state[(u + g + 1) % 2]

        def pairs(eng, body):
            n_loop = n_chunks // 2 - 1
            pair = lambda i: ((2 * i, 0, False), (2 * i + 1, 1, False))
            end = ((n_chunks - 1, 0, False),) if n_chunks % 2 else pair(n_chunks // 2 - 1)
            body(first_pair, pair(1))
            with eng.Fori(1, n_loop) as i:
                body(pair(i), pair(i + 1))
            if n_chunks % 2:
                body(pair(n_loop), end)
            body(end, ())

        @block.scalar
        def _(act):
            def decays(us):
                for n, u, early in us:
                    if not early:
                        act.wait_ge(S["operands"], n - 1)
                    act.activation(ep[u][:, :, 1:C + 1], cols(ar, X_CUM, n * C, C), ACT.Exp)
                    for e in range(2):
                        src = ar[H[e], X_CUM, n * C:(n + 1) * C] if isinstance(n, int) else (
                            ar[H[e], X_CUM, bass.ds(n * C, C)])
                        ins = act.activation(en_bd[u][H[e], :, e * C:(e + 1) * C], src, ACT.Exp, scale=-1.0)
                    ins.then_inc(S["decays"], 1)

            def body(us, nxt):
                for n, u, early in us:
                    act.wait_ge(S["vtok"], n + 1)
                    act.activation(v_bd[u][:, :, :], ps_q[u][:, :, :], ACT.Copy).then_inc(S["vtok_read"], 1)
                for n, u, early in us:
                    act.wait_ge(S["pow2"], n + 1)
                    act.activation(m3[u][:, :, :], ps[u][0][:, :, :], ACT.Copy)
                    act.activation(m4[u][:, :, :], ps[u][1][:, :, :], ACT.Copy).then_inc(S["pow2_read"], 1)
                for n, u, early in us:
                    act.wait_ge(S["tok"], n + 1)
                    act.activation(b_bd[u][:, :, :], ps_q[0][:, :, :], ACT.Copy)
                    act.activation(k_bd[u][:, :, :], ps_q[1][:, :, :], ACT.Copy).then_inc(S["tok_read"], 1)
                for n, u, early in us:
                    act.wait_ge(S["pow4"], n + 1)
                    act.activation(m1[u][:, :, :], ps[u][0][:, :, :], ACT.Copy)
                    act.activation(m2[u][:, :, :], ps[u][1][:, :, :], ACT.Copy).then_inc(S["pow4_read"], 1)
                for n, u, early in us:
                    act.wait_ge(S["pow8"], n + 1)
                    act.activation(m3[u][:, :, :], ps[u][0][:, :, :], ACT.Copy).then_inc(S["pow8_read"], 1)
                for n, u, early in us:
                    act.wait_ge(S["dinv"], n + 1)
                    act.activation(m4[u][:, :, :], ps[u][0][:, :, :], ACT.Copy).then_inc(S["dinv_read"], 1)
                for n, u, early in us:
                    act.wait_ge(S["mprod"], n + 1)
                    act.activation(m1[u][:, :, :], ps[u][1][:, :, :], ACT.Copy).then_inc(S["m_read"], 1)
                decays(nxt)
                for n, u, early in us:
                    act.wait_ge(S["xs"], n + 1)
                    act.activation(x[:, :, :], ps_q[0][:, :, :], ACT.Copy).then_inc(S["xs_read"], 1)
                    act.wait_ge(S["sa"], n + 1)
                    act.activation(sa[:, :, :], ps_q[1][:, :, :], ACT.Copy).then_inc(S["sa_read"], 1)
                    act.wait_ge(S["osum"], n + 1)
                    act.activation(cols(o, slice(0, 4), n * C, C), ps[u][2][:, :, 0:C], ACT.Copy).then_inc(S["o_read"], 1)

            act.wait_ge(S["zeros"], 1)
            decays(first_pair)
            pairs(act, body)

        @block.gpsimd
        def _(pool):
            for u in range(2):
                pool.memset(ep[u][:, :, 0:1], 1.0)
                ins = pool.memset(en_bd[u][:, :, :], 0.0)
            ins.then_inc(S["zeros"], 1)

            def blocks(us):
                for n, u, early in us:
                    if not early:
                        pool.wait_ge(S["osum"], n - 1)
                    pool.tensor_tensor(wide(v_bd[u]), spread(cols(ar, X_V, n * C, C)), spread_mask(BD),
                                       ALU.mult).then_inc(S["v_in"], 1)
                    pool.wait_ge(S["operands"], n + 1)
                    pool.tensor_tensor(wide(a_bd[u]), spread(ar_s[u][:, :, 0:C]), spread_mask(BD),
                                       ALU.mult).then_inc(S["blocks"], 1)

            def body(us, nxt):
                for n, u, early in us:
                    pool.wait_ge(S["at_read"], n + 1)
                    pool.tensor_tensor(y[u][:, :, :], m2[u][:, :, :], bc(c.ident[:, :]), ALU.add).then_inc(S["y1"], 1)
                for n, u, early in us:
                    pool.wait_ge(S["low"], n + 1)
                    pool.tensor_tensor(b_bd[u][:, :, :], b_bd[u][:, :, :], pc_of(u), ALU.mult)
                    pool.tensor_tensor(k_bd[u][:, :, :], k_bd[u][:, :, :], pc_of(u), ALU.mult).then_inc(S["hat"], 1)
                for n, u, early in us:
                    if not (early and n == 0):
                        pool.wait_ge(S["state"], n)
                    pool.tensor_tensor(s0p[:, :, :], state_in(n, u)[:, :, :], pc_of(u), ALU.mult).then_inc(S["s0p"], 1)
                    blocks(nxt[u:u + 1])

            blocks(first_pair)
            pairs(pool, body)

        @block.vector
        def _(dve):
            def operands(us):
                for n, u, early in us:
                    dve.wait_ge(S["decays"], n + 1)
                    if not early:
                        dve.wait_ge(S["osum"], n - 1)
                        dve.wait_ge(S["s0p"], n - 1)
                    dve.scalar_tensor_tensor(ar_s[u][:, :, 0:C], cols(ar, X_KK, n * C, C), -1.0, ep[u][:, :, 0:C],
                                             ALU.mult, ALU.mult)
                    dve.tensor_tensor(ar_s[u][:, :, C:2 * C], cols(ar, X_R, n * C, C), ep[u][:, :, 1:C + 1], ALU.mult)
                    dve.tensor_tensor(wide(b_bd[u]), spread(cols(ar, X_B, n * C, C)), wide(en_bd[u]), ALU.mult)
                    dve.tensor_copy(pc[u][:, :, :], ep[u][:, :, C:C + 1])
                    dve.tensor_tensor(wide(k_bd[u]), spread(cols(ar, X_K, n * C, C)), wide(en_bd[u]),
                                      ALU.mult).then_inc(S["operands"], 1)

            def body(us, nxt):
                for n, u, early in us:
                    dve.wait_ge(S["gram"], n + 1)
                    lt = spread(ps[u][1][:, :, 0:C])
                    dve.tensor_tensor(wide(m2[u]), lt, spread_mask(BD_LOW_T), ALU.mult).then_inc(S["at_read"], 1)
                    dve.tensor_tensor(wide(off_t[u]), lt, spread_mask(BD_OFF_T), ALU.mult)
                    dve.tensor_tensor(mb[u][:, :, :], ps[u][1][:, :, C:2 * C], bc(c.masks[:, UP_INCL, 0:C]), ALU.mult)
                    dve.tensor_tensor(wide(lk_bd[u]), spread(ps[u][2][:, :, 0:C]), spread_mask(BD_UP), ALU.mult)
                    dve.tensor_tensor(mk[u][:, :, :], ps[u][2][:, :, C:2 * C], bc(c.masks[:, UP_INCL, 0:C]),
                                      ALU.mult).then_inc(S["mk_read"], 1)
                    dve.wait_ge(S["low"], n + 1)
                    dve.tensor_tensor(m1[u][:, :, :], ps[u][0][:, :, :], mask(BD_LOW), ALU.mult).then_inc(S["low_read"], 1)
                for n, u, early in us:
                    dve.wait_ge(S["pow4"], n + 1)
                    dve.tensor_tensor(y[u][:, :, :], ps[u][2][:, :, :], y[u][:, :, :], ALU.add).then_inc(S["y2_read"], 1)
                for n, u, early in us:
                    dve.wait_ge(S["pow8"], n + 1)
                    dve.wait_ge(S["y2_read"], n + 1)
                    dve.tensor_tensor(y[u][:, :, :], ps[u][1][:, :, :], y[u][:, :, :], ALU.add).then_inc(S["y4_read"], 1)
                for n, u, early in us:
                    dve.wait_ge(S["y8"], n + 1)
                    dve.wait_ge(S["y4_read"], n + 1)
                    dve.tensor_tensor(y[u][:, :, :], ps[u][2][:, :, :], y[u][:, :, :], ALU.add).then_inc(S["y8_read"], 1)
                for n, u, early in us:
                    dve.wait_ge(S["t1"], n + 1)
                    dve.wait_ge(S["y8_read"], n + 1)
                    dve.tensor_tensor(m2[u][:, :, :], ps[u][2][:, :, :], y[u][:, :, :], ALU.add).then_inc(S["t1_read"], 1)
                for n, u, early in us:
                    dve.wait_ge(S["t2"], n + 1)
                    dve.tensor_tensor(m3[u][:, :, :], ps[u][0][:, :, :], y[u][:, :, :], ALU.add).then_inc(S["t2_read"], 1)
                for n, u, early in us:
                    dve.wait_ge(S["t3"], n + 1)
                    dve.tensor_tensor(m2[u][:, :, :], ps[u][1][:, :, :], y[u][:, :, :], ALU.add).then_inc(S["t3_read"], 1)
                for n, u, early in us:
                    dve.wait_ge(S["ssum"], n + 1)
                    dve.wait_ge(S["s0p"], n + 1)
                    dve.tensor_tensor(state_out(u)[:, :, :], ps_q[0][:, :, :], s0p[:, :, :],
                                      ALU.add).then_inc(S["state"], 1)
                    operands(nxt[u:u + 1])

            dve.wait_ge(S["zeros"], 1)
            operands(first_pair)
            pairs(dve, body)

        @block.tensor
        def _(pe):
            def heads(out, *operands):
                for j in range(4):
                    for k, (lhs, rhs) in enumerate(operands):
                        mm = pe.matmul(out[:, j, :], lhs[:, j, :], rhs[:, j, :], start=(k == 0),
                                       stop=(k == len(operands) - 1))
                return mm

            ident = bc(c.ident[:, :])

            def body(us, nxt):
                last = us[-1][0]
                for n, u, early in us:
                    pe.wait_ge(S["v_in"], n + 1)
                    if not early:
                        pe.wait_ge(S["state"], n if u == 0 else n - 1)
                        pe.wait_ge(S["o_read"], n if u == 0 else n - 1)
                    heads(ps_q[u], (v_bd[u], ident)).then_inc(S["vtok"], 1)
                    pe.wait_ge(S["operands"], n + 1)
                    heads(ps[u][1], (b_bd[u], ar_s[u]))
                    heads(ps[u][2], (k_bd[u], ar_s[u])).then_inc(S["gram"], 1)
                    pe.wait_ge(S["blocks"], n + 1)
                    heads(ps[u][0], (a_bd[u], b_bd[u])).then_inc(S["low"], 1)
                for n, u, early in us:
                    pe.wait_ge(S["at_read"], n + 1)
                    pe.wait_ge(S["low_read"], n + 1)
                    heads(ps[u][0], (m2[u], m1[u]))
                    heads(ps[u][1], (m1[u], m2[u])).then_inc(S["pow2"], 1)
                for n, u, early in us:
                    pe.wait_ge(S["hat"], n + 1)
                    pe.wait_ge(S["vtok_read"], last + 1)
                    if u:
                        pe.wait_ge(S["tok_read"], n)
                    heads(ps_q[0], (b_bd[u], ident))
                    heads(ps_q[1], (k_bd[u], ident)).then_inc(S["tok"], 1)
                for n, u, early in us:
                    pe.wait_ge(S["y1"], n + 1)
                    pe.wait_ge(S["pow2_read"], n + 1)
                    heads(ps[u][0], (m4[u], m3[u]))
                    heads(ps[u][1], (m3[u], m4[u]))
                    heads(ps[u][2], (m3[u], y[u])).then_inc(S["pow4"], 1)
                for n, u, early in us:
                    pe.wait_ge(S["pow4_read"], n + 1)
                    pe.wait_ge(S["y2_read"], n + 1)
                    heads(ps[u][0], (m2[u], m1[u]))
                    heads(ps[u][1], (m1[u], y[u])).then_inc(S["pow8"], 1)
                for n, u, early in us:
                    pe.wait_ge(S["pow8_read"], n + 1)
                    pe.wait_ge(S["y4_read"], n + 1)
                    heads(ps[u][2], (m3[u], y[u])).then_inc(S["y8"], 1)
                for n, u, early in us:
                    pe.wait_ge(S["y8_read"], n + 1)
                    heads(ps[u][0], (y[u], ident)).then_inc(S["dinv"], 1)
                for n, u, early in us:
                    pe.wait_ge(S["dinv_read"], n + 1)
                    heads(ps[u][1], (off_t[u], m4[u])).then_inc(S["mprod"], 1)
                for n, u, early in us:
                    pe.wait_ge(S["m_read"], n + 1)
                    heads(ps[u][2], (m1[u], y[u])).then_inc(S["t1"], 1)
                for n, u, early in us:
                    pe.wait_ge(S["t1_read"], n + 1)
                    heads(ps[u][0], (m1[u], m2[u])).then_inc(S["t2"], 1)
                for n, u, early in us:
                    pe.wait_ge(S["t2_read"], n + 1)
                    heads(ps[u][1], (m1[u], m3[u])).then_inc(S["t3"], 1)
                for n, u, early in us:
                    old = state_in(n, u)
                    pe.wait_ge(S["tok_read"], last + 1)
                    if not (early and n == 0):
                        pe.wait_ge(S["state"], n)
                    heads(ps_q[0], (a_bd[u], old), (lk_bd[u], v_bd[u])).then_inc(S["xs"], 1)
                    pe.wait_ge(S["t3_read"], n + 1)
                    pe.wait_ge(S["xs_read"], n + 1)
                    heads(ps_q[1], (m2[u], x)).then_inc(S["sa"], 1)
                    pe.wait_ge(S["sa_read"], n + 1)
                    heads(ps_q[0], (b_bd[u], sa), (k_bd[u], v_bd[u])).then_inc(S["ssum"], 1)
                    heads(ps[u][2][:, :, 0:C], (old, ar_s[u][:, :, C:2 * C]), (v_bd[u], mk[u]),
                          (sa, mb[u])).then_inc(S["osum"], 1)

            pairs(pe, body)

        @block.sync
        def _(sp):
            if g == 1:
                sp.wait_ge(S["state"], n_chunks)
                sp.dma_start(c.a["o_rp"], c.state[(n_chunks - 1 + g) % 2][:, :, :]).then_inc(S["stored"], 16)
                sp.dma_start(c.a["o_rs"], c.state[(n_chunks + g) % 2][:, :, :]).then_inc(S["stored"], 16)
                sp.wait_ge(S["stored"], 32)


def rwkv_post(nc, c, tag, T, ar, o):
    nb, nt = pieces(T)
    with Phase(nc, tag) as f:
        to_rows, from_rows = f.sb("to_rows", [P, 4, P]), f.sb("from_rows", [P, 4, P])
        sq = f.sb("sq", [P, 4, T])
        xs, t, y = (f.sb(n, [P, T]) for n in ("xs", "t", "y"))
        ps, ps_rows = f.ps("ps", [P, 2, 2, 512]), f.ps("ps_rows", [P, 2, 512])
        ahead = f.sem("ahead")
        tables, mean, centred, squared, var, root, newton, spread, done = (
            f.sem(n) for n in ("tables", "mean", "centred", "squared", "var", "root", "newton", "spread", "done"))
        block = f.block()

        @block.sync
        def _(sp):
            sp.dma_start(to_rows[:, :, :], c.a["to_rows"][:, 0:4, :]).then_inc(tables, 16)
            sp.dma_start(from_rows[:, :, :], c.a["from_rows"][:, 0:4, :]).then_inc(tables, 16)
            load_ahead(sp, c, first_two(c.a["w_attn"]), ahead)

        @block.tensor
        def _(pe):
            for m in range(4):
                if m >= 2:
                    pe.wait_ge(centred, m - 1)
                for b in range(nb):
                    mm = pe.matmul(ps[:, m % 2, b, 0:nt], c.ones_head[:, :], o[:, m, b * nt:(b + 1) * nt],
                                   start=True, stop=True)
                mm.then_inc(mean, 1)
            pe.wait_ge(tables, 32)
            for m in range(4):
                pe.wait_ge(squared, m + 1)
                for b in range(nb):
                    mm = pe.matmul(ps_rows[:, b, 0:nt], to_rows[:, m, :], sq[:, m, b * nt:(b + 1) * nt],
                                   start=(m == 0), stop=(m == 3))
            mm.then_inc(var, 1)
            pe.wait_ge(newton, 4)
            for m in range(4):
                if m < 2:
                    pe.wait_ge(centred, 3 + m)
                else:
                    pe.wait_ge(done, m - 1)
                for b in range(nb):
                    mm = pe.matmul(ps[:, m % 2, b, 0:nt], from_rows[:, m, :], y[:, b * nt:(b + 1) * nt],
                                   start=True, stop=True)
                mm.then_inc(spread, 1)

        @block.scalar
        def _(act):
            for m in range(4):
                act.wait_ge(centred, m + 1)
                act.activation(sq[:, m], o[:, m], ACT.Square).then_inc(squared, 1)
            rsqrt_act(act, c, xs[:, :], t[:, :], y[:, :], root, 0, newton, 1)

        @block.gpsimd
        def _(pool):
            for m in range(2):
                pool.wait_ge(done, 5 + m)
                pool.tensor_tensor(o[:, m], o[:, m], ar[:, 12 + m], ALU.mult)

        @block.vector
        def _(dve):
            for m in range(4):
                dve.wait_ge(mean, m + 1)
                dve.scalar_tensor_tensor(two(o[:, m], T), ps[:, m % 2, 0:nb, 0:nt], -1.0 / 64, two(o[:, m], T),
                                         ALU.mult, ALU.add).then_inc(centred, 1)
            dve.wait_ge(var, 1)
            dve.tensor_scalar(two(xs[:, :], T), ps_rows[:, 0:nb, 0:nt], GN_EPS, None, ALU.add).then_inc(newton, 1)
            rsqrt_dve(dve, xs[:, :], t[:, :], y[:, :], root, 0, newton, 1)
            for m in range(4):
                dve.wait_ge(spread, m + 1)
                dve.scalar_tensor_tensor(two(o[:, m], T), two(o[:, m], T), vec(c, "ln_g", m),
                                         ps[:, m % 2, 0:nb, 0:nt], ALU.mult, ALU.mult).then_inc(done, 1)
            for m in range(4):
                dve.wait_ge(done, m + 1)
                dve.scalar_tensor_tensor(o[:, m], o[:, m], vec(c, "ln_b", m), ar[:, m], ALU.add,
                                         ALU.add).then_inc(done, 1)
            dve.wait_ge(done, 8)
            dve.tensor_tensor(o[:, 2:4, :], o[:, 2:4, :], ar[:, 14:16, :], ALU.mult)




def split_phase(nc, c, tag, src, hi, lo, w_next):
    tiles = len(src)
    with Phase(nc, tag) as f:
        hi_done, ahead = f.sem("hi_done"), f.sem("ahead")
        block = f.block()

        @block.sync
        def _(sp):
            load_ahead(sp, c, w_next, ahead)

        @block.scalar
        def _(act):
            for k in range(tiles):
                act.activation(hi[:, k], src[k], ACT.Copy).then_inc(hi_done, 1)

        @block.vector
        def _(dve):
            for k in range(0, tiles, 2):
                dve.wait_ge(hi_done, k + 1)
                dve.tensor_tensor(lo[:, k], src[k], hi[:, k].bitcast(F32), ALU.subtract)

        @block.gpsimd
        def _(pool):
            for k in range(1, tiles, 2):
                pool.wait_ge(hi_done, k + 1)
                pool.tensor_tensor(lo[:, k], src[k], hi[:, k].bitcast(F32), ALU.subtract)


def merge_phase(nc, c, tag, T, o_hi, o_lo, merged):
    def epilogue(f, sum_free, acc):
        th, pr = f.sb("th", [P, 2, T]), f.sb("pr", [P, T])
        tan, added = f.sem("tan"), f.sem("added")

        def act(eng, i, a):
            if a % 2:
                return
            n = 3 * i + a // 2
            eng.activation(two(th[:, 0], T), acc(a), ACT.Tanh, scale=0.5).then_inc(tan, 1)
            eng.wait_ge(tan, n + 1)
            if not (isinstance(n, int) and n == 0):
                eng.wait_ge(sum_free[1], n)
            eng.activation(th[:, 1], th[:, 0], ACT.Copy, scale=0.5, bias=0.5).then_inc(sum_free[0], 1)

        def dve(eng, i, a, first):
            if a % 2 == 0:
                return
            n = 3 * i + a // 2
            eng.wait_ge(sum_free[0], n + 1)
            dst = at(merged, i)
            out = dst if a == 1 else pr[:, :]
            if a == 3 and not first:
                eng.wait_ge(added, 2 * i)
            if a == 5:
                eng.wait_ge(added, 2 * i + 1)
            eng.tensor_tensor(two(out, T), acc(a), two(th[:, 1], T), ALU.mult).then_inc(sum_free[1], 1)
            if a > 1:
                eng.wait_ge(sum_free[1], n + 1)
                eng.tensor_tensor(dst, dst, pr[:, :], ALU.add).then_inc(added, 1)
        return {"act": act, "dve": dve}

    body = []
    for n in range(3):
        body.append(((n, c.a["w_gate"]), DT, c.x_hi, c.x_lo, True, True))
        body.append(((n, c.a["w_branch"]), 4, o_hi[:, 4 * n:4 * n + 4, :], o_lo[:, 4 * n:4 * n + 4, :], True, True))
    dense_phase(nc, c, tag, T, DT, body, epilogue, slots=3, act_lag=2)


def add_phase(nc, c, tag, T, steps, body, base, load=None, store=None):
    def epilogue(f, sum_free, acc):
        if load is not None:
            base_in = f.sem("base_in")

            def load_base(sp):
                sp.dma_start(base[:, :, :], load).then_inc(base_in, 16)

        def dve(eng, i, a, first):
            if load is not None and first and a == 0:
                eng.wait_ge(base_in, 16)
            m = 2 * i + a
            ins = eng.tensor_tensor(two(at(base, m), T), acc(a), two(at(base, m), T), ALU.add)
            ins.then_inc(sum_free[a], 1)
        return {"dve": dve, **({"load": load_base} if load is not None else {})}

    def store_step(sp, i):
        if isinstance(i, int):
            return sp.dma_start(store[:, 2 * i:2 * i + 2, :], base[:, 2 * i:2 * i + 2, :])
        return sp.dma_start(store[:, bass.ds(2 * i, 2), :], base[:, bass.ds(2 * i, 2), :])

    dense_phase(nc, c, tag, T, steps, body, epilogue, store=store_step if store is not None else None)


def up_phase(nc, c, tag, g, T, h_hi, h_lo):
    def epilogue(f, sum_free, acc):
        a_raw, cv, gl = f.sb("a_raw", [P, T + 2]), f.sb("cv", [P, T]), f.sb("gl", [P, T])
        h = f.sb("h", [P, T])
        a_in, conv, gelu, hi_done, lo_done = (f.sem(n) for n in ("a_in", "conv", "gelu", "h_hi_done", "h_lo_done"))
        h_done = sum_free[1]
        ws = f.sb("ws", [P, 4])
        if g == 1:
            fix = f.sb("fix", [P, 4])
        per = 4 if g == 0 else 7
        cw, cb, cs = VEC["conv_w"][0], VEC["conv_b"][0], VEC["conv_s"][0]

        def col(tensor, i, n=1):
            return tensor[:, i:i + n] if isinstance(i, int) else tensor[:, bass.ds(i, n)]

        def act(eng, i, a):
            if a == 0:
                eng.wait_ge(conv, per * i + per)
                if not (isinstance(i, int) and i == 0):
                    eng.wait_ge(h_done, i)
                eng.activation(gl[:, :], cv[:, :], ACT.Gelu_apprx_tanh).then_inc(gelu, 1)
            else:
                eng.wait_ge(h_done, i + 1)
                eng.activation(at(h_hi, i), h[:, :], ACT.Copy).then_inc(hi_done, 1)

        def dve(eng, i, a, first):
            if a == 0:
                copy(eng, a_raw[:, 0:2], col(c.conv_carry, 2 * i, 2)).then_inc(a_in, 1)
                eng.tensor_copy(two(a_raw[:, 2:T + 2], T), acc(0)).then_inc(sum_free[0], 1)
                eng.tensor_copy(ws[:, 0:3], col(c.vecs, cw + 3 * i, 3))
                eng.tensor_copy(ws[:, 3:4], col(c.vecs, cb + i)).then_inc(a_in, 1)
                eng.wait_ge(sum_free[0], i + 1)
                eng.wait_ge(a_in, 2 * i + 2)
                if not first:
                    eng.wait_ge(gelu, i)
                eng.tensor_scalar(cv[:, :], a_raw[:, 2:T + 2], ws[:, 2:3], ws[:, 3:4], ALU.mult,
                                  ALU.add).then_inc(conv, 1)
                eng.wait_ge(conv, per * i + 1)
                eng.scalar_tensor_tensor(cv[:, :], a_raw[:, 1:T + 1], ws[:, 1:2], cv[:, :], ALU.mult,
                                         ALU.add).then_inc(conv, 1)
                eng.wait_ge(conv, per * i + 2)
                eng.scalar_tensor_tensor(cv[:, :], a_raw[:, 0:T], ws[:, 0:1], cv[:, :], ALU.mult,
                                         ALU.add).then_inc(conv, 1)
                eng.wait_ge(conv, per * i + 3)
                if g == 0:
                    copy(eng, col(c.conv_carry, 2 * i, 2), a_raw[:, T:T + 2]).then_inc(conv, 1)
                    return
                e0 = PROMPT_END
                copy(eng, fix[:, 0:2], col(c.vecs, cs + 2 * i, 2))
                eng.tensor_copy(fix[:, 2:4], a_raw[:, 2 + e0:4 + e0])
                copy(eng, col(c.conv_carry, 2 * i, 2), a_raw[:, e0:e0 + 2])
                eng.tensor_copy(col(c.conv_last, 2 * i, 2), a_raw[:, T:T + 2]).then_inc(conv, 1)
                eng.wait_ge(conv, per * i + 4)
                eng.tensor_scalar(cv[:, e0:e0 + 2], fix[:, 2:4], ws[:, 2:3], ws[:, 3:4], ALU.mult,
                                  ALU.add).then_inc(conv, 1)
                eng.wait_ge(conv, per * i + 5)
                eng.scalar_tensor_tensor(cv[:, e0:e0 + 2], fix[:, 1:3], ws[:, 1:2], cv[:, e0:e0 + 2], ALU.mult,
                                         ALU.add).then_inc(conv, 1)
                eng.wait_ge(conv, per * i + 6)
                eng.scalar_tensor_tensor(cv[:, e0:e0 + 2], fix[:, 0:2], ws[:, 0:1], cv[:, e0:e0 + 2], ALU.mult,
                                         ALU.add).then_inc(conv, 1)
            else:
                eng.wait_ge(gelu, i + 1)
                if not first:
                    eng.wait_ge(lo_done, i)
                eng.tensor_tensor(two(h[:, :], T), acc(1), two(gl[:, :], T), ALU.mult).then_inc(h_done, 1)
                eng.wait_ge(hi_done, i + 1)
                eng.tensor_tensor(at(h_lo, i), h[:, :], at(h_hi, i).bitcast(F32), ALU.subtract).then_inc(lo_done, 1)
        return {"act": act, "dve": dve}

    body = [((s, c.a["w_up"]), DT, c.x_hi, c.x_lo, True, True) for s in range(2)]
    dense_phase(nc, c, tag, T, FT, body, epilogue, act_lag=2, w_next=first_two(c.a["w_down"]))




class Consts:
    pass


def build(nc, a):
    c = Consts()
    c.a = a
    with Phase(nc, "k") as k:
        c.vecs = k.sb("vecs", [P, N_VEC])
        c.ident, c.ones, c.ones_head = k.sb("ident", [P, P]), k.sb("ones", [P, P]), k.sb("ones_head", [P, P])
        c.lora = k.sb("lora", [P, 2, 512])
        c.masks = k.sb("masks", [P, N_MASKS, P])
        c.raw = [k.sb(f"raw{s}", [P, D]) for s in range(2)]
        c.state = [k.sb(f"state{s}", [P, 4, P]) for s in range(2)]
        c.sample_state = k.sb("sample_state", [P, 4, P])
        c.kv_carry = k.sb("kv_carry", [P, 2, WINDOW])
        c.shift_carry, c.shift_out = k.sb("shift_carry", [P, 14]), k.sb("shift_out", [P, 2, 14])
        c.conv_carry, c.conv_last = k.sb("conv_carry", [P, 2 * FT]), k.sb("conv_last", [P, 2 * FT])

        with Phase(nc, "start") as f:
            in_sem = f.sem("in")
            block = f.block()

            @block.sync
            def _(sp):
                for n, (dst, src) in enumerate((
                        (c.vecs[:, :], a["vecs"]), (c.ident[:, :], a["ident"]), (c.ones[:, :], a["ones"]),
                        (c.ones_head[:, :], a["ones_head"]), (c.lora[:, :, :], a["lora"]),
                        (c.masks[:, :, :], a["masks"]), (c.sample_state[:, :, :], a["state"]))):
                    sp.dma_start(dst, src).then_inc(in_sem, 16)
                sp.wait_ge(in_sem, 16 * 7)

            @block.vector
            def _(dve):
                dve.memset(c.state[0][:, :, :], 0.0)
                dve.memset(c.conv_carry[:, :], 0.0)

        memory_phase(nc, c)
        for g, (start, T) in enumerate(GROUPS):
            group(nc, c, g, start, T)

        with Phase(nc, "end") as f:
            out = f.sem("out")
            block = f.block()

            @block.sync
            def _(sp):
                sp.dma_start(a["o_cp"], c.conv_carry[:, :]).then_inc(out, 16)
                sp.dma_start(a["o_cs"], c.conv_last[:, :]).then_inc(out, 16)
                sp.wait_ge(out, 32)


def group(nc, c, g, start, T):
    a, t = c.a, f"g{g}"
    x_src = a["xT"][:, :, start:start + T]
    with Phase(nc, t) as k:
        c.x_hi, c.x_lo = k.sb("x_hi", [P, DT, T], F32R), k.sb("x_lo", [P, DT, T], F32R)
        with Phase(nc, t + "o") as ko:
            o_a = ko.sb("o_a", [P, 4, T])
            with Phase(nc, t + "x") as kx:
                x = kx.sb("x", [P, DT, T])
                norm_phase(nc, c, t + "n1", T, x, "norm1_g", c.x_hi, c.x_lo, first_two(a["w_rwkv"]), x_src)
            with Phase(nc, t + "r") as kr:
                ar = kr.sb("ar", [P, 32, T])
                project_phase(nc, c, t + "pr", T, R_TILES, a["w_rwkv"], ar)
                rwkv_prep(nc, c, t + "rp", g, T, ar)
                rwkv_scan(nc, c, t + "rs", g, T, ar, o_a)
                rwkv_post(nc, c, t + "rq", T, ar, o_a)
            o_hi, o_lo = ko.sb("o_hi", [P, 12, T], F32R), ko.sb("o_lo", [P, 12, T], F32R)
            with Phase(nc, t + "a") as ka:
                pa = ka.sb("pa", [P, A_TILES, T])
                width = WINDOW + T if g == 0 else 2 * WINDOW + T
                kw, vw = ka.sb("kw", [P, width]), ka.sb("vw", [P, width])
                project_phase(nc, c, t + "pa", T, A_TILES, a["w_attn"], pa, split=(o_a, o_hi, o_lo))
                attention_prep(nc, c, t + "ap", g, T, pa, kw, vw)
                attention_phase(nc, c, t + "at", g, T, pa, kw, vw, o_hi, o_lo, o_a)
            with Phase(nc, t + "m") as km:
                merged = km.sb("merged", [P, DT, T])
                merge_phase(nc, c, t + "mg", T, o_hi, o_lo, merged)
                split_phase(nc, c, t + "sm", [merged[:, k] for k in range(DT)], c.x_hi, c.x_lo,
                            first_two(a["w_out"]))
        with Phase(nc, t + "y") as ky:
            x1 = ky.sb("x1", [P, DT, T])
            body = [((s, a["w_out"]), DT, c.x_hi, c.x_lo, True, True) for s in range(2)]
            add_phase(nc, c, t + "wo", T, DT // 2, body, x1, load=x_src)
            norm_phase(nc, c, t + "n2", T, x1, "norm2_g", c.x_hi, c.x_lo, first_two(a["w_up"]))
            h_hi, h_lo = ky.sb("h_hi", [P, FT, T], F32R), ky.sb("h_lo", [P, FT, T], F32R)
            up_phase(nc, c, t + "up", g, T, h_hi, h_lo)
            body = []
            for m in range(2):
                for n, (index, w) in enumerate(((2 * m, a["w_down"]), (2 * m + 1, a["w_down"]), (m, a["w_down_end"]))):
                    ks = slice(n * DT, min((n + 1) * DT, FT))
                    body.append(((index, w), ks.stop - ks.start, h_hi[:, ks, :], h_lo[:, ks, :], n == 0, n == 2))
            add_phase(nc, c, t + "wd", T, DT // 2, body, x1, store=a["o_y"][:, :, start:start + T])




def tiles(w):
    k, m = w.shape
    return np.ascontiguousarray(w.reshape(k // P, P, m // P, P).transpose(2, 1, 0, 3).reshape(m // P, P, k))


def columns(v):
    return v.reshape(-1, P).T


def constants():
    i = np.arange(P)
    ident = np.eye(P, dtype=np.float32)
    head = (i[:, None] // 64 == i[None, :] // 64).astype(np.float32)
    r, q = i % 64, np.arange(P)
    t = q % 64
    masks = np.zeros((P, N_MASKS, P), np.float32)
    masks[:, BD] = head
    masks[:, BD_LOW] = head * (r[:, None] // 16 == t[None] // 16) * (r[:, None] > t[None])
    masks[:, BD_LOW_T] = head * (r[:, None] // 16 == t[None] // 16) * (r[:, None] < t[None])
    masks[:, BD_OFF_T] = head * (r[:, None] // 16 < t[None] // 16)
    masks[:, BD_UP] = head * (r[:, None] < t[None])
    masks[:, UP_INCL] = r[:, None] <= t[None]
    row = np.stack([2 * n + i // 64 if n < 5 else np.full(P, 5 + n) for n in range(9)], 1)
    from_rows = (i[:, None, None] == row.T[None]).astype(np.float32)
    to_rows = np.ascontiguousarray(from_rows.transpose(2, 1, 0))
    to_rows[:, 0:5] /= 64
    to_rows[:, 5:] /= P
    slopes = np.exp2(-8.0 * np.arange(1, 9, dtype=np.float32) / 8).astype(np.float32)
    dist = np.abs(WINDOW + np.arange(64)[:, None] - np.arange(KEYS)[None, :]).astype(np.float32)
    alibi = np.zeros((P, 3, 4, KEYS), np.float32)
    for v in range(3):
        for j in range(4):
            for e in range(2):
                t = -slopes[j + 4 * e] * dist
                t = np.where(np.arange(KEYS)[None, :] < WINDOW - CHUNK * v, np.float32(-1e30), t)
                alibi[64 * e:64 * e + 64, v, j] = t
    return {"ident": ident, "ones": np.ones((P, P), np.float32), "ones_head": head, "masks": masks, "alibi": alibi,
            "to_rows": to_rows, "from_rows": np.ascontiguousarray(from_rows)}


def lay_out(x):
    f32 = np.float32
    w_in = np.asarray(x["w_in"][0])
    rw = w_in[:, 0:1792]
    order = [slice(1536, 1664), slice(1664, 1792), slice(0, 512), slice(512, 1024), slice(1024, 1536)]
    reorder = lambda v: np.concatenate([v[..., s] for s in order], - 1)
    heads = [h for j in range(4) for h in (j, j + 4)]
    q = w_in[:, 1792:2304].reshape(D, 8, 64)[:, heads].reshape(D, 512)
    attn = np.concatenate([q, w_in[:, 2304:3072]], 1)
    gates = w_in[:, 3072:].reshape(D, 3, DT, P).transpose(0, 2, 1, 3).reshape(D, 3 * D)
    branch = np.asarray(x["w_branch"][0]).copy()
    branch[1] = branch[1].reshape(8, 64, D)[heads].reshape(512, D)
    branch = np.stack([tiles(b) for b in branch], 1).reshape(3 * DT, P, 512)
    up = np.asarray(x["w_up"][0]).reshape(D, 2, FT, P).transpose(0, 2, 1, 3).reshape(D, 2 * FF)
    down = tiles(np.asarray(x["w_down"][0]))
    down_start = down[:, :, 0:2 * D].reshape(DT, P, 2, D).transpose(0, 2, 1, 3).reshape(2 * DT, P, D)
    mem_kv = np.asarray(x["w_mem_kv"][0])
    both = lambda v: np.tile(v, 2)[:, None]
    sink = np.asarray(x["swa_sink"][0])
    sinks = np.concatenate([np.tile(sink[4 * e:4 * e + 4][None], (64, 1)) for e in range(2)], 0)
    conv_w = np.asarray(x["conv_w"][0]).reshape(3, FT, P).transpose(2, 1, 0).reshape(P, 3 * FT)
    conv_s = np.asarray(x["state_conv"][0, 0]).reshape(2, FT, P).transpose(2, 1, 0).reshape(P, 2 * FT)
    one = lambda n: columns(np.asarray(x[n][0]).reshape(-1))
    vecs = np.concatenate([
        one("norm1_g"), one("norm2_g"), one("mem_norm_g"), columns(reorder(np.asarray(x["rwkv_mu"][0]))),
        one("rwkv_w0"), one("rwkv_a0"), one("rwkv_kk"), one("rwkv_ka"), one("rwkv_rk"), one("rwkv_ln_g"),
        one("rwkv_ln_b"), both(np.asarray(x["swa_qn_g"][0])), both(np.asarray(x["swa_kn_g"][0])),
        one("mem_qn_g"), one("mem_kn_g"), sinks, conv_w, one("conv_b"),
        columns(reorder(np.asarray(x["state_shift"][0, 0, 0]))), conv_s,
        np.full((P, 1), 0.5 * np.log(LN_SCALE), f32)], 1)
    assert vecs.shape == (P, N_VEC)
    fm = lambda v: v.reshape(-1, DT, P).transpose(2, 1, 0)
    tokens = np.concatenate([np.asarray(x["x_prompt"][0]), np.asarray(x["x_sample"][0])], 0)
    lora = np.stack([np.concatenate([np.asarray(x["rwkv_w2"][0]), np.asarray(x["rwkv_a2"][0])], 0),
                     np.asarray(x["rwkv_g2"][0])], 1)
    heads_kv = np.asarray(x["state_rwkv"][0, 0]).reshape(4, 2, 64, 64).transpose(1, 3, 0, 2)
    state = np.zeros((P, 4, P), f32)
    for e in range(2):
        state[64 * e:64 * e + 64, :, 64 * e:64 * e + 64] = heads_kv[e]
    out = {
        "xT": fm(tokens), "memT": fm(np.asarray(x["mem_prompt"][0])), "vecs": vecs, "lora": lora,
        "w_attn": tiles(attn), "w_rwkv": tiles(reorder(rw)), "w_gate": tiles(gates), "w_branch": branch,
        "w_out": tiles(np.asarray(x["w_out"][0])), "w_up": tiles(up), "w_down": down_start,
        "w_down_end": down[:, :, 2 * D:], "w_mk": tiles(mem_kv[:, 0:512]),
        "w_mv": mem_kv[:, 512:].reshape(DT, P, 512).transpose(1, 0, 2),
        "cache_k": np.asarray(x["cache_swa_k"][0, 0]).reshape(WINDOW, P).T,
        "cache_v": np.asarray(x["cache_swa_v"][0, 0]).reshape(WINDOW, P).T,
        "cache_mk": np.asarray(x["cache_mem_k"][0, 0]).transpose(2, 1, 0),
        "cache_mv": np.asarray(x["cache_mem_v"][0, 0]).reshape(2, P, 512).transpose(1, 0, 2),
        "state": state,
    }
    out.update(constants())
    return {n: np.ascontiguousarray(v) for n, v in out.items()}


OUTS = {
    "o_y": (P, DT, SEQ + DEC), "o_mk": (P, 4, MEM), "o_mv": (P, 2, 512), "o_kp": (P, WINDOW), "o_vp": (P, WINDOW),
    "o_ks": (P, WINDOW), "o_vs": (P, WINDOW), "o_rp": (P, 4, P), "o_rs": (P, 4, P), "o_shp": (P, 14),
    "o_shs": (P, 14), "o_cp": (P, 2 * FT), "o_cs": (P, 2 * FT),
}


def kernel(**inputs):
    import concourse.bacc as _bacc
    from concourse.bass_utils import run_bass_kernel_spmd as _run

    nc = _bacc.Bacc("TRN2", target_bir_lowering=False, num_devices=1)
    arrays = lay_out(inputs)
    a = {n: nc.dram_tensor(n, v.shape, mybir.dt.from_np(v.dtype), kind="ExternalInput").ap() for n, v in arrays.items()}
    for n, s in OUTS.items():
        a[n] = nc.dram_tensor(n, s, F32, kind="ExternalOutput").ap()
    build(nc, a)
    r = _run(nc, [arrays], core_ids=[0]).results[0]

    y = r["o_y"].transpose(2, 1, 0).reshape(SEQ + DEC, D)
    kv = lambda v: np.ascontiguousarray(v.T).reshape(1, 1, WINDOW, 2, 64)

    def state(v):
        blocks = np.stack([v[64 * e:64 * e + 64, :, 64 * e:64 * e + 64] for e in range(2)])
        return blocks.transpose(2, 0, 3, 1).reshape(1, 1, 8, 64, 64)

    def shift(v):
        flat = v.T.reshape(1792)
        return np.concatenate([flat[256:], flat[0:256]]).reshape(1, 1, 1, 1792)

    conv = lambda v: v.reshape(P, FT, 2).transpose(2, 1, 0).reshape(1, 1, 2, FF)
    return (y[None, 0:SEQ], y[None, SEQ:],
            kv(r["o_kp"]), kv(r["o_vp"]),
            r["o_mk"].transpose(2, 1, 0).reshape(1, 1, MEM, 4, P),
            r["o_mv"].transpose(1, 0, 2).reshape(1, 1, MEM, 4, P),
            state(r["o_rp"]), shift(r["o_shp"]), conv(r["o_cp"]),
            kv(r["o_ks"]), kv(r["o_vs"]), state(r["o_rs"]), shift(r["o_shs"]), conv(r["o_cs"]))
```
